# Optimizing a Trainium2 kernel written in Bass

```python
import math
import jax, jax.numpy as jnp
from jax import lax
import numpy as np

D_MODEL = 2048
BATCH = 1
SEQ = 512
DEPTH = 1

D_MIX = D_MODEL
MLA_HEADS = 8
QK_NOPE_DIM = 128
QK_ROPE_DIM = 64
V_HEAD_DIM = 128
Q_LORA_RANK = 512
KV_LORA_RANK = 256
D_MLA = MLA_HEADS * V_HEAD_DIM
D_SSM = D_MIX - D_MLA
SSM_GROUP_CH = 16
SSM_GROUPS = D_SSM // SSM_GROUP_CH
SSM_STATE = 64
ROPE_THETA = 10000.0
NORM_EPS = 1e-6
Q_BLOCK = 128
STEP_MIN = 1e-3
STEP_MAX = 1e-1
D_IN = Q_LORA_RANK + KV_LORA_RANK + QK_ROPE_DIM + D_MLA + D_SSM + D_SSM

kernel_name = 'hymba_mla_s5_sandwich'

def _rms_norm(x, g):
    xf = x.astype(jnp.float32)
    inv = lax.rsqrt(jnp.mean(xf * xf, axis=-1, keepdims=True) + NORM_EPS)
    return (xf * inv * g.astype(jnp.float32)).astype(x.dtype)

def _rope_tables(positions):
    inv_freq = ROPE_THETA ** (-jnp.arange(0, QK_ROPE_DIM, 2, dtype=jnp.float32) / QK_ROPE_DIM)
    ang = positions.astype(jnp.float32)[..., None] * inv_freq
    ang = jnp.concatenate([ang, ang], axis=-1)
    return jnp.cos(ang), jnp.sin(ang)

def _apply_rope(x, cos, sin):
    xf = x.astype(jnp.float32)
    x1, x2 = jnp.split(xf, 2, axis=-1)
    rot = jnp.concatenate([-x2, x1], axis=-1)
    return (xf * cos + rot * sin).astype(x.dtype)

def _mla(c_q, c_kv, k_rope, positions, g_q, w_uq, g_kv, w_ukv):
    b, l, _ = c_q.shape
    q = jnp.einsum('blr,rf->blf', _rms_norm(c_q, g_q), w_uq)
    q = q.reshape(b, l, MLA_HEADS, QK_NOPE_DIM + QK_ROPE_DIM)
    q_nope, q_rope = q[..., :QK_NOPE_DIM], q[..., QK_NOPE_DIM:]
    kv = jnp.einsum('blr,rf->blf', _rms_norm(c_kv, g_kv), w_ukv)
    kv = kv.reshape(b, l, MLA_HEADS, QK_NOPE_DIM + V_HEAD_DIM)
    k_nope, v = kv[..., :QK_NOPE_DIM], kv[..., QK_NOPE_DIM:]
    cos, sin = _rope_tables(positions)
    q_rope = _apply_rope(q_rope, cos[:, :, None, :], sin[:, :, None, :])
    k_rope = _apply_rope(k_rope, cos, sin)

    n_blk = l // Q_BLOCK
    qn_blk = q_nope.reshape(b, n_blk, Q_BLOCK, MLA_HEADS, QK_NOPE_DIM).transpose(1, 0, 2, 3, 4)
    qr_blk = q_rope.reshape(b, n_blk, Q_BLOCK, MLA_HEADS, QK_ROPE_DIM).transpose(1, 0, 2, 3, 4)
    key_idx = jnp.arange(l)
    scale = 1.0 / math.sqrt(QK_NOPE_DIM + QK_ROPE_DIM)
    neg = jnp.finfo(jnp.float32).min

    def block(args):
        qn, qr, i = args
        s = (jnp.einsum('bqhd,bkhd->bhqk', qn, k_nope)
             + jnp.einsum('bqhr,bkr->bhqk', qr, k_rope))
        s = s.astype(jnp.float32) * scale
        q_idx = i * Q_BLOCK + jnp.arange(Q_BLOCK)
        causal = key_idx[None, :] <= q_idx[:, None]
        s = jnp.where(causal[None, None], s, neg)
        p = jax.nn.softmax(s, axis=-1).astype(v.dtype)
        return jnp.einsum('bhqk,bkhd->bqhd', p, v)

    o = lax.map(block, (qn_blk, qr_blk, jnp.arange(n_blk)))
    return o.transpose(1, 0, 2, 3, 4).reshape(b, l, D_MLA)

def _ssm_combine(e1, e2):
    a1, b1 = e1
    a2, b2 = e2
    return a1 * a2, a2 * b1 + b2

def _s5(u, a_re, a_im, b_re, b_im, c_re, c_im, d_skip, log_step, w_glu):
    b, l, _ = u.shape
    uf = u.astype(jnp.float32).reshape(b, l, SSM_GROUPS, SSM_GROUP_CH)
    a = lax.complex(a_re.astype(jnp.float32), a_im.astype(jnp.float32))
    step = jnp.exp(log_step.astype(jnp.float32))[:, None]
    a_bar = jnp.exp(step * a)
    b_mat = lax.complex(b_re.astype(jnp.float32), b_im.astype(jnp.float32))
    b_bar = ((a_bar - 1.0) / a)[..., None] * b_mat
    bu = jnp.einsum('gph,blgh->blgp', b_bar, uf.astype(jnp.complex64))
    a_seq = jnp.broadcast_to(a_bar, bu.shape)
    _, states = lax.associative_scan(_ssm_combine, (a_seq, bu), axis=1)
    c_mat = lax.complex(c_re.astype(jnp.float32), c_im.astype(jnp.float32))
    y = (jnp.einsum('ghp,blgp->blgh', c_mat, states).real
         + d_skip.astype(jnp.float32).reshape(SSM_GROUPS, SSM_GROUP_CH) * uf)
    y = jax.nn.gelu(y.reshape(b, l, D_SSM)).astype(u.dtype)
    val, gate = jnp.split(jnp.einsum('blc,cf->blf', y, w_glu), 2, axis=-1)
    return val * jax.nn.sigmoid(gate)

def _layer(x, positions, g_pre, g_post, w_in, g_q, w_uq, g_kv, w_ukv,
           a_re, a_im, b_re, b_im, c_re, c_im, d_skip, log_step, w_glu, w_out):
    h = _rms_norm(x, g_pre)
    proj = jnp.einsum('bld,df->blf', h, w_in)
    s1 = Q_LORA_RANK
    s2 = s1 + KV_LORA_RANK
    s3 = s2 + QK_ROPE_DIM
    s4 = s3 + D_MLA
    s5 = s4 + D_SSM
    c_q, c_kv, k_rope, gate_mla, u_ssm, gate_ssm = jnp.split(proj, [s1, s2, s3, s4, s5], axis=-1)
    mla_out = _mla(c_q, c_kv, k_rope, positions, g_q, w_uq, g_kv, w_ukv)
    ssm_out = _s5(u_ssm, a_re, a_im, b_re, b_im, c_re, c_im, d_skip, log_step, w_glu)
    mixed = jnp.concatenate([mla_out * jax.nn.silu(gate_mla),
                             ssm_out * jax.nn.silu(gate_ssm)], axis=-1)
    out = jnp.einsum('blf,fd->bld', mixed, w_out)
    return x + _rms_norm(out, g_post)

def setup_inputs(seed: int = 0) -> dict:
    key = jax.random.key(seed)
    k = jax.random.split(key, 20)
    f32 = jnp.float32
    x = jax.random.normal(k[0], (BATCH, SEQ, D_MODEL), f32)
    offset = jax.random.randint(k[1], (BATCH, 1), 0, 4096, dtype=jnp.int32)
    positions = (jnp.arange(SEQ, dtype=jnp.int32)[None, :] + offset).astype(jnp.int32)
    norm_pre = 1.0 + 0.1 * jax.random.normal(k[2], (DEPTH, D_MODEL), f32)
    norm_post = 1.0 + 0.1 * jax.random.normal(k[3], (DEPTH, D_MODEL), f32)
    w_in = jax.random.normal(k[4], (DEPTH, D_MODEL, D_IN), f32) * D_MODEL ** -0.5
    q_norm = 1.0 + 0.1 * jax.random.normal(k[5], (DEPTH, Q_LORA_RANK), f32)
    w_uq = jax.random.normal(k[6], (DEPTH, Q_LORA_RANK, MLA_HEADS * (QK_NOPE_DIM + QK_ROPE_DIM)), f32) * Q_LORA_RANK ** -0.5
    kv_norm = 1.0 + 0.1 * jax.random.normal(k[7], (DEPTH, KV_LORA_RANK), f32)
    w_ukv = jax.random.normal(k[8], (DEPTH, KV_LORA_RANK, MLA_HEADS * (QK_NOPE_DIM + V_HEAD_DIM)), f32) * KV_LORA_RANK ** -0.5
    ssm_a_re = -0.5 * jnp.exp(0.05 * jax.random.normal(k[9], (DEPTH, SSM_GROUPS, SSM_STATE), f32))
    ssm_a_im = (math.pi * jnp.arange(SSM_STATE, dtype=f32)[None, None, :]
                + 0.01 * jax.random.normal(k[10], (DEPTH, SSM_GROUPS, SSM_STATE), f32))
    b_scale = (SSM_GROUP_CH ** -0.5) / math.sqrt(2.0)
    c_scale = (SSM_STATE ** -0.5) / math.sqrt(2.0)
    ssm_b_re = jax.random.normal(k[11], (DEPTH, SSM_GROUPS, SSM_STATE, SSM_GROUP_CH), f32) * b_scale
    ssm_b_im = jax.random.normal(k[12], (DEPTH, SSM_GROUPS, SSM_STATE, SSM_GROUP_CH), f32) * b_scale
    ssm_c_re = jax.random.normal(k[13], (DEPTH, SSM_GROUPS, SSM_GROUP_CH, SSM_STATE), f32) * c_scale
    ssm_c_im = jax.random.normal(k[14], (DEPTH, SSM_GROUPS, SSM_GROUP_CH, SSM_STATE), f32) * c_scale
    ssm_d = jax.random.normal(k[15], (DEPTH, D_SSM), f32)
    ssm_log_step = jax.random.uniform(k[16], (DEPTH, SSM_GROUPS), f32,
                                      minval=math.log(STEP_MIN), maxval=math.log(STEP_MAX))
    w_glu = jax.random.normal(k[17], (DEPTH, D_SSM, 2 * D_SSM), f32) * D_SSM ** -0.5
    w_out = jax.random.normal(k[18], (DEPTH, D_MIX, D_MODEL), f32) * D_MIX ** -0.5
    return {'x': x, 'positions': positions, 'norm_pre': norm_pre, 'norm_post': norm_post,
            'w_in': w_in, 'q_norm': q_norm, 'w_uq': w_uq, 'kv_norm': kv_norm, 'w_ukv': w_ukv,
            'ssm_a_re': ssm_a_re, 'ssm_a_im': ssm_a_im, 'ssm_b_re': ssm_b_re, 'ssm_b_im': ssm_b_im,
            'ssm_c_re': ssm_c_re, 'ssm_c_im': ssm_c_im, 'ssm_d': ssm_d, 'ssm_log_step': ssm_log_step,
            'w_glu': w_glu, 'w_out': w_out}

def reference(x, positions, norm_pre, norm_post, w_in, q_norm, w_uq, kv_norm, w_ukv,
              ssm_a_re, ssm_a_im, ssm_b_re, ssm_b_im, ssm_c_re, ssm_c_im, ssm_d,
              ssm_log_step, w_glu, w_out):
    h = x
    for i in range(DEPTH):
        h = _layer(h, positions, norm_pre[i], norm_post[i], w_in[i], q_norm[i], w_uq[i],
                   kv_norm[i], w_ukv[i], ssm_a_re[i], ssm_a_im[i], ssm_b_re[i], ssm_b_im[i],
                   ssm_c_re[i], ssm_c_im[i], ssm_d[i], ssm_log_step[i], w_glu[i], w_out[i])
    return h


_drawn_inputs = setup_inputs


def setup_inputs(seed=0):
    import zlib

    import numpy as np

    out = dict(_drawn_inputs(seed))
    spreads = {}
    factors = {'ssm_a_re': 200.0,
     'ssm_a_im': 30.616,
     'ssm_b_re': 42.104,
     'ssm_b_im': 42.344,
     'ssm_c_re': 42.112,
     'ssm_c_im': 42.376,
     'ssm_log_step': 33.128}
    for name, (base, spread) in spreads.items():
        noise = np.random.default_rng([zlib.crc32(name.encode()), seed]).standard_normal(out[name].shape)
        drawn = base * np.exp(spread * noise) if base else spread * noise
        out[name] = __import__('jax').numpy.asarray(drawn.astype(out[name].dtype))
    for name, factor in factors.items():
        out[name] = (out[name] * factor).astype(out[name].dtype)
    return out
```

```python
from contextlib import ExitStack

import concourse.bass as bass
from concourse import mybir

F32 = mybir.dt.float32
F32R = mybir.dt.float32r
I32 = mybir.dt.int32
ALU = mybir.AluOpType
ACT = mybir.ActivationFunctionType
AX = mybir.AxisListType

P = 128
SEQ = 512
D = 2048
HEADS = 8
NOPE = 128
ROPE = 64
QR = 512
KVR = 256
CH = 1024
GC = 16
STATES = 64
PAIRS = CH // GC // 2
L = 8
NQ = SEQ // L
KT = D // P
TT = SEQ // P
EPS = 1e-6
SCALE = 1.0 / float(NOPE + ROPE) ** 0.5
TWO_PI = 6.283185307179586
PI_A, PI_B, PI_C = 6.28125, 0.0019350051879882812, 3.0199159819e-07
ROUND = 12582912.0
PI_SAFE = 3.1415925
HALF_PI = 1.5707963267948966

COL_CKV = QR
COL_KR = QR + KVR
COL_GM = COL_KR + ROPE
COL_U = COL_GM + CH
COL_GS = COL_U + CH

UNIT = 1024
RING = 4
GRP = 256
BATCH = 8
NB = PAIRS // BATCH
PADK = (L - 1) * GC + P

N_U, N_GM, N_GS, N_CQ, N_CKV, N_KR = 0, 4, 8, 12, 14, 15
W_KR = 4 * N_KR
W_KN = W_KR + 1
W_V = W_KN + 2
W_Q = W_V + 2
W_ROPE = W_Q + 4
W_GLU = W_ROPE + 2
W_OUT = W_GLU + 16
W_END = W_OUT + 32

C_ID, C_MASK, C_FREQ, C_SIGN, C_COLS = 0, P, 2 * P, 2 * P + 1, 2 * P + 2
(R_ARE, R_AIM, R_STEP, R_ZR, R_ZI, R_ER, R_TH, R_V, R_N, R_R, R_M, R_S, R_C, R_S2, R_NR, R_NI, R_X, R_Y,
 R_DEN, R_FR, R_FI) = range(21)


def hybrid_layer(nc, a, out):
    ctx = ExitStack()
    with ctx:
        def sb(name, shape, dt=F32, scope=ctx):
            return scope.enter_context(nc.sbuf_tensor(name, shape, dt))

        def sem(name):
            return ctx.enter_context(nc.semaphore(name))

        u_dram = nc.dram_tensor("u_scratch", [CH, SEQ], F32, kind="Internal").ap()
        gm_dram = nc.dram_tensor("gate_mla_scratch", [CH, SEQ], F32, kind="Internal").ap()
        gs_dram = nc.dram_tensor("gate_ssm_scratch", [CH, SEQ], F32, kind="Internal").ap()
        y_dram = nc.dram_tensor("y_scratch", [CH, SEQ], F32, kind="Internal").ap()
        taps_dram = nc.dram_tensor("taps_scratch", [2 * GC, PAIRS, PADK], F32, kind="Internal").ap()

        stage = sb("stage", [P, RING, UNIT])
        w_hi = sb("w_hi", [P, RING, UNIT], F32R)
        w_lo = sb("w_lo", [P, RING, UNIT], F32R)
        consts = sb("consts", [P, C_COLS])
        ident = consts[:, C_ID:C_ID + P]
        mask = consts[:, C_MASK:C_MASK + P]
        inv_freq = consts[:, C_FREQ:C_FREQ + 1]
        rope_sign = consts[:, C_SIGN:C_SIGN + 1]
        ones = sb("ones", [P, P])
        eps = sb("eps", [P, 1])
        cos = sb("cos", [P, SEQ])
        sin = sb("sin", [P, SEQ])
        k_rot = sb("k_rot", [P, SEQ])
        lat = sb("lat", [P, 6, SEQ])
        g_lat = sb("g_lat", [P, 6])
        small = sb("small", [P, 3, TT])
        soft = sb("soft", [P, 3, TT])
        fin = sb("fin", [P, TT, 7])

        part1 = ExitStack()
        h_hi = sb("h_hi", [P, KT, SEQ], F32R, part1)
        h_lo = sb("h_lo", [P, KT, SEQ], F32R, part1)
        ev = sb("ev", [P, 2, SEQ], F32, part1)
        prm = sb("prm", [P, 21, PAIRS], F32, part1)
        powers = sb("powers", [P, L + 1, 3, PAIRS], F32, part1)
        bbar = sb("bbar", [P, 2, PAIRS, GC], F32, part1)
        ct = sb("ct", [P, 2, PAIRS, GC], F32, part1)
        chunk_a = sb("chunk_a", [P, 2, 2, PAIRS], F32, part1)
        araw = sb("araw", [PAIRS, 3, P], F32, part1)
        lsraw = sb("lsraw", [PAIRS, 2], F32, part1)
        draw = sb("draw", [PAIRS, 2 * GC], F32, part1)
        dsk = sb("dsk", [2 * GC, PAIRS], F32, part1)
        part0 = ExitStack()
        xt = sb("xt", [P, TT, D], F32, part0)
        g_pre = sb("g_pre", [P, D], F32, part0)
        junk = sb("junk", [P, D], F32, part0)
        part0.close()
        ssm = ExitStack()
        raws = ExitStack()
        braw = sb("braw", [P, 2, PAIRS, GC], F32, raws)
        craw = sb("craw", [P, 2, BATCH, STATES], F32, raws)
        ang = sb("ang", [P, 4, SEQ], F32, raws)
        pos = sb("pos", [P, SEQ], I32, raws)
        raws.close()
        states = sb("states", [P, NQ + 1, 2, PAIRS], F32, ssm)
        cw = sb("cw", [P, BATCH, 2, L + 1, GC], F32, ssm)
        tmp = sb("tmp", [P, 2, BATCH, L + 1, GC], F32, ssm)
        mats = sb("mats", [P, 2 * BATCH, P], F32, ssm)
        u2 = sb("u2", [P, 2 * BATCH, NQ], F32, ssm)
        yb = sb("yb", [P, 2 * BATCH, NQ], F32, ssm)
        bd = sb("bd", [P, BATCH, 2, 2 * GC], F32, ssm)
        sw = sb("sw", [P, 2, 2, PAIRS], F32, ssm)
        st = sb("st", [P, 2, PAIRS], F32, ssm)
        dm = sb("dm", [2 * GC, BATCH, GC], F32, ssm)
        same_ch = sb("same_ch", [2 * GC, GC], F32, ssm)
        zeros = sb("zeros", [2 * GC, PADK - P], F32, ssm)
        ssm.close()
        taps = tmp[0:2 * GC].rearrange("p a b c d -> p (a b c d)")[:, 0:BATCH * P].rearrange(
            "p (g n) -> p g n", g=BATCH)
        part1.close()

        part2 = ExitStack()
        mixed_hi = sb("mixed_hi", [P, KT, SEQ], F32R, part2)
        mixed_lo = sb("mixed_lo", [P, KT, SEQ], F32R, part2)
        lat_hi, lat_lo = mixed_hi[:, 0:6], mixed_lo[:, 0:6]
        y_hi, y_lo = mixed_hi[:, 0:8], mixed_lo[:, 0:8]
        part3 = ExitStack()
        kn = sb("kn", [P, HEADS, SEQ], F32, part3)
        vv = sb("vv", [P, TT, CH], F32, part3)
        qn = sb("qn", [P, HEADS, SEQ], F32, part3)
        qr = sb("qr", [P, HEADS // 2, SEQ], F32, part3)
        glu_in = ExitStack()
        yraw = sb("yraw", [P, 8, SEQ], F32, glu_in)
        glu_in.close()
        pt = sb("pt", [P, 2, TT, SEQ], F32, part3)
        glu_t = sb("glu_t", [P, 2, SEQ], F32, part3)
        part3.close()
        og = sb("og", [P, TT, D], F32, part2)
        xr = sb("xr", [P, TT, D], F32, part2)
        g_post = sb("g_post", [P, D], F32, part2)
        part2.close()

        ps = ctx.enter_context(nc.psum_tensor("ps", [P, 8, 512], F32))

        class Sems:
            pass

        S = Sems()
        S.consts_in = sem("consts_in")
        S.g_pre_in = sem("g_pre_in")
        S.prm_in = sem("prm_in")
        S.bc_in = sem("bc_in")
        S.pos_in = sem("pos_in")
        S.hi_done = sem("hi_done")
        S.lo_done = sem("lo_done")
        S.w_used = sem("w_used")
        S.const_done = sem("const_done")
        S.x_sq = sem("x_sq")
        S.x_rms = sem("x_rms")
        S.x_rinv = sem("x_rinv")
        S.x_normed = sem("x_normed")
        S.xT_done = sem("xT_done")
        S.xhi_done = sem("xhi_done")
        S.xlo_done = sem("xlo_done")
        S.prm_links = sem("prm_links")
        S.prmT_done = sem("prmT_done")
        S.ls_ready = sem("ls_ready")
        S.step_done = sem("step_done")
        S.z_ready = sem("z_ready")
        S.z_acts = sem("z_acts")
        S.angle_ready = sem("angle_ready")
        S.trig_done = sem("trig_done")
        S.rope_angle = sem("rope_angle")
        S.rope_trig = sem("rope_trig")
        S.ctT_done = sem("ctT_done")
        S.b_done = sem("b_done")
        S.proj_done = sem("proj_done")
        S.proj_evac = sem("proj_evac")
        S.ev_done = sem("ev_done")
        S.ev_stored = sem("ev_stored")
        S.cwr_step = sem("cwr_step")
        S.cwi_step = sem("cwi_step")
        S.bxT_done = sem("bxT_done")
        S.bx_ready = sem("bx_ready")
        S.u2_in = sem("u2_in")
        S.vin_done = sem("vin_done")
        S.vin_evac = sem("vin_evac")
        S.scan_step = sem("scan_step")
        S.bd_done = sem("bd_done")
        S.taps_done = sem("taps_done")
        S.taps_step = sem("taps_step")
        S.taps_ready = sem("taps_ready")
        S.taps_stored = sem("taps_stored")
        S.zero_stored = sem("zero_stored")
        S.toep_in = sem("toep_in")
        S.y_done = sem("y_done")
        S.y_ready = sem("y_ready")
        S.y_stored = sem("y_stored")
        S.lat_sq = sem("lat_sq")
        S.lat_sum = sem("lat_sum")
        S.lat_ssq = sem("lat_ssq")
        S.lat_rms = sem("lat_rms")
        S.lat_link = sem("lat_link")
        S.lat_normed = sem("lat_normed")
        S.lat_hi_done = sem("lat_hi_done")
        S.lat_lo_done = sem("lat_lo_done")
        S.kr_evac = sem("kr_evac")
        S.kr_link = sem("kr_link")
        S.kr_done = sem("kr_done")
        S.head_done = sem("head_done")
        S.head_evac = sem("head_evac")
        S.rope_mul = sem("rope_mul")
        S.rope_done = sem("rope_done")
        S.yhi_done = sem("yhi_done")
        S.ylo_done = sem("ylo_done")
        S.glu_done = sem("glu_done")
        S.sig_done = sem("sig_done")
        S.glu_val = sem("glu_val")
        S.glu_prod = sem("glu_prod")
        S.ghi_done = sem("ghi_done")
        S.glo_done = sem("glo_done")
        S.s_done = sem("s_done")
        S.s_link = sem("s_link")
        S.s_max = sem("s_max")
        S.exp_done = sem("exp_done")
        S.den_done = sem("den_done")
        S.p_done = sem("p_done")
        S.pT_done = sem("pT_done")
        S.pT_evac = sem("pT_evac")
        S.o_done = sem("o_done")
        S.o_gated = sem("o_gated")
        S.ohi_done = sem("ohi_done")
        S.olo_done = sem("olo_done")
        S.out_done = sem("out_done")
        S.out_sq = sem("out_sq")
        S.og_done = sem("og_done")
        S.fin_sum = sem("fin_sum")
        S.fin_root = sem("fin_root")
        S.fin_inv = sem("fin_inv")
        S.fin_done = sem("fin_done")
        S.xr_in = sem("xr_in")
        S.g_post_in = sem("g_post_in")
        S.out_stored = sem("out_stored")
        x_in = [sem(f"x_in{t}") for t in range(TT)]
        w_in = [sem(f"w_in{s}") for s in range(RING)]
        yraw_in = [sem(f"yraw_in{s}") for s in range(2)]
        gs_in = [sem(f"gs_in{s}") for s in range(2)]
        gm_in = [sem(f"gm_in{s}") for s in range(2)]

        block = ctx.enter_context(nc.Block())

        def unit_in(w, col):
            u = w % 4
            return a["w_in"][u * 512:(u + 1) * 512, bass.ds(col, GRP)].rearrange("(k p) n -> p k n", p=P)

        def pieces(w):
            return 1 if w < W_KN or w >= W_OUT else 4 if W_ROPE <= w < W_GLU else 2

        def loaded(w):
            return 16 * sum(pieces(x) for x in range(w % RING, w + 1, RING))

        def tiles_of(w):
            return 4 if w < W_Q else 2

        def used(w):
            if W_KN <= w < W_GLU:
                return S.head_done, sum(tiles_of(x) for x in range(W_KN, w + 1))
            return S.w_used, w + 1 - (W_GLU - W_KN if w >= W_GLU else 0)

        def load(sp, slot, src, turn, first=False):
            if not first:
                sp.wait_ge(S.lo_done, 4 * turn + (slot - 3))
            sp.dma_start(stage[:, slot, :].rearrange("p (k n) -> p k n", k=src.shape[1]), src
                         ).then_inc(w_in[slot], 16)

        def split_hi(act, slot, turn):
            act.wait_ge(w_in[slot], 16 * turn + 16)
            act.wait_ge(S.w_used, 4 * turn + (slot - 3))
            round_unit(act, slot)

        def split_hi_at(act, w):
            act.wait_ge(w_in[w % RING], loaded(w))
            if w >= RING:
                act.wait_ge(*used(w - RING))
            round_unit(act, w % RING)

        def round_unit(act, slot):
            act.activation(w_hi[:, slot, :], stage[:, slot, :], ACT.Copy).then_inc(S.hi_done, 1)

        def split_lo(pool, slot, turn):
            pool.wait_ge(S.hi_done, 4 * turn + (slot + 1))
            pool.tensor_tensor(w_lo[:, slot, :], stage[:, slot, :], w_hi[:, slot, :].bitcast(F32),
                               ALU.subtract).then_inc(S.lo_done, 1)

        def split_lo_at(pool, w):
            split_lo(pool, w % RING, w // RING)

        def three(pe, o, s_hi, s_lo, m_hi, m_lo, start, stop):
            pe.matmul(o, s_hi, m_hi, start=start, stop=False)
            pe.matmul(o, s_hi, m_lo, start=False, stop=False)
            return pe.matmul(o, s_lo, m_hi, start=False, stop=stop)

        def x_rows(ap, t, jj):
            return ap.rearrange("(q j) d -> j q d", j=L)[2 * t + jj]

        def natural(ap):
            return ap.rearrange("p (q j) -> p j q", j=L)

        def steps(ap):
            return ap.rearrange("p (j q) -> p j q", j=L)

        nonc = nc.allow_non_contiguous_dma(reason="rows of one SSM group")
        ctx.enter_context(nonc)

        @block.sync
        def _(sp):
            def load_x(t):
                for jj in range(2):
                    sp.dma_start(xt[64 * jj:64 * jj + 64, t, :], x_rows(a["x"], t, jj)).then_inc(x_in[t], 16)

            def load_w(w, col):
                load(sp, w % 4, unit_in(w, col), w // 4, first=w < 4)

            load_x(0)
            sp.dma_start(g_pre[:, :], a["norm_pre"].to_broadcast([P, D])).then_inc(S.g_pre_in, 16)
            sp.dma_start(consts[:, :], a["consts"]).then_inc(S.consts_in, 16)
            for t in range(1, TT):
                load_x(t)
                load_w(t - 1, COL_U)
            load_w(3, COL_U)
            sp.dma_start(araw[:, 0, :], a["ssm_a_re"].rearrange("(g h) n -> g (h n)", h=2)).then_inc(S.prm_in, 16)
            sp.dma_start(araw[:, 1, :], a["ssm_a_im"].rearrange("(g h) n -> g (h n)", h=2)).then_inc(S.prm_in, 16)
            sp.dma_start(lsraw[:, :], a["ssm_log_step"].rearrange("a (g h) -> (a g) h", h=2)).then_inc(S.prm_in, 16)
            sp.dma_start(draw[:, :], a["ssm_d"].rearrange("a (g c) -> (a g) c", c=2 * GC)).then_inc(S.prm_in, 16)
            for i, (g, n) in enumerate((("q_norm", 4), ("kv_norm", 2))):
                sp.dma_start(g_lat[:, 4 * i:4 * i + n], a[g].rearrange("a (k p) -> p (a k)", p=P)).then_inc(S.prm_in, 16)
            sp.wait_ge(S.xT_done, 16)
            for i, n in enumerate(("ssm_b_re", "ssm_b_im")):
                sp.dma_start(braw[:, i], a[n].rearrange("(g h) n c -> (h n) g c", h=2)).then_inc(S.bc_in, 16)
            for i, n in enumerate(("ssm_c_re", "ssm_c_im")):
                sp.dma_start(craw[:, i], a[n].rearrange("(b g) c n -> (g c) b n", b=BATCH)).then_inc(S.bc_in, 16)
            sp.dma_start(pos[:, :], a["positions"].to_broadcast([P, SEQ])).then_inc(S.pos_in, 16)
            for w in range(4, 8):
                load_w(w, COL_U + GRP)

            def load_u2(b):
                for r in range(L):
                    src = u_dram[bass.ds(b * (2 * BATCH * GC), 2 * BATCH * GC), (L - 1 - r) * NQ:(L - r) * NQ]
                    sp.dma_start(u2[GC * r:GC * r + GC], src.rearrange("(g c) q -> c g q", c=GC)).then_inc(S.u2_in, 16)

            with sp.Fori(0, 2) as i:
                for par in range(2):
                    for u in range(4):
                        col = (COL_GM - COL_U - 2 * GRP) * i + (COL_U + 2 * GRP + par * GRP)
                        load(sp, u, unit_in(u, col), 2 * i + (2 + par))
            sp.wait_ge(S.ev_stored, 16 * 4)
            with sp.Fori(0, 2) as i:
                for par in range(2):
                    sp.wait_ge(S.vin_evac, 4 * i + (2 * par + 1))
                    load_u2(2 * i + par)
                    for u in range(4):
                        col = (COL_GS - COL_GM - 2 * GRP) * i + (COL_GM + 2 * GRP + par * GRP)
                        load(sp, u, unit_in(u, col), 2 * i + (6 + par))
            sp.wait_ge(S.vin_done, NB)
            load_u2(0)
            sp.dma_start(taps_dram[:, :, 0:PADK - P],
                         zeros[:, :].unsqueeze(1).to_broadcast([2 * GC, PAIRS, PADK - P])).then_inc(S.zero_stored, 16)
            with sp.Fori(0, 2) as i:
                for par in range(2):
                    for u in range(4):
                        col = (0 - COL_GS - 2 * GRP) * i + (COL_GS + 2 * GRP + par * GRP)
                        load(sp, u, unit_in(u, col), 2 * i + (10 + par))

            def load_toeplitz(b):
                sp.wait_ge(S.taps_ready, 2 * b + 2)
                sp.dma_start(taps_dram[:, b * BATCH:(b + 1) * BATCH, PADK - P:PADK], taps).then_inc(S.taps_stored, 16)
                sp.wait_ge(S.taps_stored, 16 * b + 16)
                if b == 0:
                    sp.wait_ge(S.zero_stored, 16)
                if b == 0:
                    sp.wait_ge(S.vin_done, NB)
                else:
                    sp.wait_ge(S.y_done, b)
                dst = mats[:, :, :].rearrange("p (g h) n -> p h g n", h=2)
                for r in range(L):
                    for h in range(2):
                        sp.dma_start(dst[GC * r:GC * r + GC, h],
                                     taps_dram[GC * h:GC * h + GC, b * BATCH:(b + 1) * BATCH, GC * r:GC * r + P]
                                     ).then_inc(S.toep_in, 16)

            def unit_pieces(w):
                slot = stage[:, w % RING, :]
                if w < W_KN:
                    src = unit_in(w, COL_CKV) if w < W_KR else a["w_in"][:, COL_KR:COL_GM].rearrange(
                        "(k p) n -> p k n", p=P)
                    return [(slot.rearrange("p (k n) -> p k n", k=src.shape[1]), src)]
                if w < W_Q:
                    v, i = divmod(w - W_KN, 2)
                    src = a["w_ukv"].rearrange("(k p) (h e n) -> k e p h n", p=P, e=2, n=NOPE)
                    dst = slot.rearrange("p (k h n) -> p k h n", k=2, n=NOPE)
                    return [(dst[:, k], src[k, v][:, 4 * i:4 * i + 4]) for k in range(2)]
                if w < W_GLU:
                    src = a["w_uq"].rearrange("(k p) (h n) -> p k h n", p=P, h=HEADS)
                    if w < W_ROPE:
                        i = w - W_Q
                        dst = slot.rearrange("p (k h n) -> p k h n", k=4, n=NOPE)
                        return [(dst[:, :, h], src[:, :, 2 * i + h, 0:NOPE]) for h in range(2)]
                    dst = slot.rearrange("p (k h n) -> p k h n", k=4, n=32)
                    c = NOPE + 32 * (w - W_ROPE)
                    return [(dst[:, k], src[:, k, :, c:c + 32]) for k in range(4)]
                if w < W_OUT:
                    m, u = divmod(w - W_GLU, 2)
                    src = a["w_glu"].rearrange("(k p) n -> p k n", p=P)[:, 4 * (1 - u):4 * (1 - u) + 4]
                    dst = slot.rearrange("p (k e n) -> p k e n", k=4, e=2)
                    return [(dst[:, :, e], src[:, :, CH * e + P * m:CH * e + P * m + P]) for e in range(2)]
                c, u = divmod(w - W_OUT, 8)
                return [(slot.rearrange("p (k n) -> p k n", k=2),
                         a["w_out"].rearrange("(k p) n -> p k n", p=P)[:, 2 * u:2 * u + 2, 512 * c:512 * c + 512])]

            def load_gs(m):
                sp.wait_ge(S.glu_prod, m - 1) if m >= 2 else None
                sp.dma_start(lat[:, 4 + m % 2], gs_dram[P * m:P * m + P]).then_inc(gs_in[m % 2], 16)

            def load_gm(h):
                if h < 2:
                    sp.wait_ge(S.glu_prod, 7 + h)
                else:
                    sp.wait_ge(S.o_gated, h - 1)
                sp.dma_start(lat[:, 4 + h % 2], gm_dram[P * h:P * h + P]).then_inc(gm_in[h % 2], 16)

            beside = {
                56: lambda: load_toeplitz(0),
                59: lambda: (sp.wait_ge(S.y_done, 1), load_u2(1), load_toeplitz(1)),
                63: lambda: (sp.wait_ge(S.y_done, 2), load_u2(2), load_toeplitz(2)),
                66: lambda: (sp.wait_ge(S.y_done, 3), load_u2(3), load_toeplitz(3)),
                70: lambda: (sp.wait_ge(S.y_stored, 16 * L * NB),
                             sp.dma_start(yraw[:, 4:8], y_dram[4 * P:8 * P].rearrange("(k p) n -> p k n", p=P)
                                          ).then_inc(yraw_in[0], 16),
                             sp.dma_start(yraw[:, 0:4], y_dram[0:4 * P].rearrange("(k p) n -> p k n", p=P)
                                          ).then_inc(yraw_in[1], 16)),
                73: lambda: (sp.wait_ge(S.lat_lo_done, 6), sp.wait_ge(S.ev_stored, 16 * 12), load_gs(0), load_gs(1)),
                96: lambda: (sp.wait_ge(S.o_gated, HEADS), sp.wait_ge(S.o_done, HEADS),
                             sp.dma_start(g_post[:, :], a["norm_post"].to_broadcast([P, D])).then_inc(S.g_post_in, 16),
                             [sp.dma_start(xr[64 * jj:64 * jj + 64, t, :], x_rows(a["x"], t, jj)).then_inc(S.xr_in, 16)
                              for t in range(TT) for jj in range(2)]),
            }
            for m in range(2, 8):
                beside[W_GLU + 2 * m + 3] = lambda m=m: load_gs(m)
            beside[W_OUT + RING] = lambda: [load_gm(h) for h in range(HEADS)]
            for w in range(4 * 14, W_END):
                if w in beside:
                    beside[w]()
                sp.wait_ge(S.lo_done, w - 3)
                for dst, src in unit_pieces(w):
                    sp.dma_start(dst, src).then_inc(w_in[w % RING], 16)
            for t in range(TT):
                sp.wait_ge(S.fin_done, t + 1)
                for jj in range(2):
                    sp.dma_start(x_rows(out, t, jj), og[64 * jj:64 * jj + 64, t, :]).then_inc(S.out_stored, 16)
            sp.wait_ge(S.out_stored, 16 * 2 * TT)

        @block.scalar
        def _(act):
            def x_tile(t):
                for k in range(4):
                    act.wait_ge(S.xT_done, 4 * t + k + 1)
                    act.activation(h_hi[:, 4 * k:4 * k + 4, P * t:P * t + P],
                                   ps[:, 4 * ((t + 1) % 2) + k].rearrange("p (k n) -> p k n", k=4),
                                   ACT.Copy).then_inc(S.xhi_done, 1)

            act.wait_ge(S.const_done, 2)
            for t in range(TT):
                act.wait_ge(x_in[t], 32)
                if t:
                    act.wait_ge(S.x_sq, t)
                act.activation(junk[:, :], xt[:, t, :], ACT.Square, accum_out=small[:, 0, t:t + 1]).then_inc(S.x_sq, 1)
                act.wait_ge(S.x_sq, t + 1)
                act.activation(small[:, 1, t:t + 1], small[:, 0, t:t + 1], ACT.Sqrt, bias=eps[:, :],
                               scale=1.0 / D).then_inc(S.x_rms, 1)
                if t:
                    x_tile(t - 1)
                    split_hi_at(act, t - 1)
            x_tile(TT - 1)
            split_hi_at(act, 3)
            act.wait_ge(S.ls_ready, 2)
            act.activation(prm[:, R_STEP], prm[:, R_STEP], ACT.Exp).then_inc(S.step_done, 1)
            act.wait_ge(S.z_ready, 2)
            act.activation(prm[:, R_ER], prm[:, R_ZR], ACT.Exp).then_inc(S.z_acts, 1)
            act.activation(prm[:, R_TH], prm[:, R_ZR], ACT.Tanh, scale=0.5).then_inc(S.z_acts, 1)
            act.wait_ge(S.angle_ready, 1)
            act.activation(prm[:, R_S], prm[:, R_R], ACT.Sin).then_inc(S.trig_done, 1)
            act.activation(prm[:, R_C], prm[:, R_M], ACT.Sin).then_inc(S.trig_done, 1)
            act.wait_ge(S.rope_angle, 1)
            act.activation(sin[:, :], ang[:, 2], ACT.Sin).then_inc(S.rope_trig, 1)
            act.activation(cos[:, :], ang[:, 3], ACT.Sin).then_inc(S.rope_trig, 1)

            def evacuate(n, par, func, dram, row):
                act.wait_ge(S.w_used, 4 * n + 4)
                for m in range(2):
                    act.activation(ev[:, m], ps[:, 2 * par + m], func).then_inc(S.proj_evac, 1)
                act.wait_ge(S.proj_evac, 2 * n + 2)
                act.dma_start(dram[bass.ds(row, GRP)].rearrange("(m p) n -> p m n", p=P), ev[:, :, :]
                              ).then_inc(S.ev_stored, 16)
                act.wait_ge(S.ev_stored, 16 * n + 16)

            for n0, func, dram in ((N_U, ACT.Copy, u_dram), (N_GM, ACT.Silu, gm_dram), (N_GS, ACT.Silu, gs_dram)):
                with act.Fori(0, 2) as i:
                    for par in range(2):
                        for u in range(4):
                            split_hi(act, u, 2 * i + (n0 + par + 1))
                        evacuate(2 * i + (n0 + par), par, func, dram, (2 * GRP) * i + par * GRP)

            def gelu(b):
                act.wait_ge(S.y_done, b + 1)
                if b:
                    act.wait_ge(S.y_stored, 16 * L * b)
                for m in range(2):
                    act.activation(yb[:, :, :].rearrange("p (g h) q -> p h g q", h=2)[:, m],
                                   ps[:, 6 + m].rearrange("p (g q) -> p g q", q=NQ),
                                   ACT.Gelu_apprx_tanh).then_inc(S.y_ready, 1)
                act.wait_ge(S.y_ready, 2 * b + 2)
                dst = y_dram[2 * BATCH * GC * b:2 * BATCH * GC * (b + 1)].rearrange("(g c) (j q) -> j c g q", c=GC, j=L)
                for j in range(L):
                    act.dma_start(dst[j], yb[GC * j:GC * j + GC]).then_inc(S.y_stored, 16)

            def latent(n, first, consumed):
                act.wait_ge(S.w_used, 4 * n + 4)
                act.wait_ge(*consumed)
                for m in range(2):
                    bank = ps[:, 2 * (n % 2) + m]
                    act.activation(natural(ev[:, m]), steps(bank), ACT.Square).then_inc(S.lat_sq, 1)
                    act.activation(natural(lat[:, first + m]), steps(bank), ACT.Copy).then_inc(S.proj_evac, 1)

            for n, first, consumed in ((12, 0, (S.ev_stored, 16 * 12)), (13, 2, (S.lat_sum, 1)),
                                       (14, 4, (S.lat_sum, 3))):
                for w in (4 * n + 4, 4 * n + 5):
                    split_hi_at(act, w)
                gelu(n - 12)
                if n == 14:
                    act.wait_ge(S.lat_ssq, 1)
                    act.activation(k_rot[:, :], ps[:, 4], ACT.Sqrt, bias=eps[:, :], scale=1.0 / QR
                                   ).then_inc(S.lat_rms, 1)
                for w in (4 * n + 6, 4 * n + 7):
                    split_hi_at(act, w)
                latent(n, first, consumed)
            act.wait_ge(S.lat_ssq, 2)
            act.activation(ev[:, 0], ps[:, 5], ACT.Sqrt, bias=eps[:, :], scale=1.0 / KVR).then_inc(S.lat_rms, 1)
            split_hi_at(act, 64)
            act.wait_ge(S.w_used, W_KR + 1)
            for i, k in enumerate((4, 5, 0, 1, 2, 3)):
                act.wait_ge(S.lat_normed, 6 if k > 3 else 4)
                act.activation(lat_hi[:, k], lat[:, k], ACT.Copy).then_inc(S.lat_hi_done, 1)
            gelu(3)

            def head_tile(j):
                act.wait_ge(S.head_done, j + 1)
                i = j % 8
                src = ps[:, j % 4]
                if j < 8:
                    act.activation(kn[:, i], src, ACT.Copy).then_inc(S.head_evac, 1)
                elif j < 16:
                    act.activation(vv[:, i % 4, 512 * (i // 4):512 * (i // 4) + 512], src, ACT.Copy
                                   ).then_inc(S.head_evac, 1)
                else:
                    act.activation(qn[:, i], src, ACT.Copy, scale=SCALE).then_inc(S.head_evac, 1)

            tiles = iter(range(24))
            act.wait_ge(S.y_stored, 16 * L * NB)
            act.wait_ge(S.kr_done, 1)
            for w in range(W_KN, W_ROPE):
                split_hi_at(act, w + 4)
                for _ in range(4 if w < W_Q else 2):
                    head_tile(next(tiles))

            def y_tile(k):
                act.wait_ge(yraw_in[0 if k > 3 else 1], 16)
                act.activation(y_hi[:, k], yraw[:, k], ACT.Copy).then_inc(S.yhi_done, 1)

            y_tile(6)
            y_tile(7)
            for w in range(W_ROPE, W_GLU):
                split_hi_at(act, w + 4)
            for k in (4, 5, 0, 1, 2, 3):
                act.wait_ge(*used(W_GLU - 1))
                y_tile(k)

            def glu(m):
                for w in (W_GLU + 4 + 2 * m, W_GLU + 5 + 2 * m):
                    split_hi_at(act, w)
                act.wait_ge(*used(W_GLU + 2 * m + 1))
                if m:
                    act.wait_ge(S.glu_val, m)
                act.activation(glu_t[:, 0], ps[:, 2 * (m % 2) + 1], ACT.Sigmoid).then_inc(S.sig_done, 1)
                act.wait_ge(S.glu_prod, m + 1)
                act.activation(mixed_hi[:, 8 + m], glu_t[:, 1], ACT.Copy).then_inc(S.ghi_done, 1)

            for m in range(8):
                glu(m)

            def softmax_exp(h, i):
                n = P * (i + 1)
                act.wait_ge(S.s_max, 4 * h + i + 1)
                if h:
                    act.wait_ge(S.pT_done, 4 * (h - 1) + i + 1)
                act.activation(lat[:, i, 0:n], ps[:, i, 0:n], ACT.Exp, bias=soft[:, 0, i:i + 1],
                               accum_out=soft[:, 1, i:i + 1]).then_inc(S.exp_done, 1)

            def transposed(h, i):
                act.wait_ge(S.pT_done, 4 * h + i + 1)
                if h >= 2:
                    act.wait_ge(S.o_done, h - 1)
                act.activation(pt[:, h % 2, 0:i + 1, P * i:P * i + P],
                               ps[:, 4 + i % 2, 0:P * (i + 1)].rearrange("p (k n) -> p k n", n=P),
                               ACT.Copy).then_inc(S.pT_evac, 1)

            def gated(h):
                act.wait_ge(S.o_gated, h + 1)
                act.activation(mixed_hi[:, h], glu_t[:, h % 2], ACT.Copy).then_inc(S.ohi_done, 1)

            for h in range(HEADS + 1):
                for i in range(TT):
                    if h < HEADS:
                        softmax_exp(h, i)
                    if h:
                        transposed(h - 1, i)
                if h:
                    gated(h - 1)

            def out_squares(c):
                act.wait_ge(*used(W_OUT + 8 * c + 7))
                for t in range(TT):
                    if 4 * c + t:
                        act.wait_ge(S.out_sq, 4 * c + t)
                    act.activation(glu_t[:, 0], ps[:, 4 * (c % 2) + t], ACT.Square, accum_out=fin[:, t, c:c + 1]
                                   ).then_inc(S.out_sq, 1)

            for c in range(4):
                for w in range(W_OUT + 8 * c + 4, min(W_OUT + 8 * c + 12, W_END)):
                    split_hi_at(act, w)
                out_squares(c)
            for t in range(TT):
                act.wait_ge(S.fin_sum, t + 1)
                act.activation(fin[:, t, 5:6], fin[:, t, 4:5], ACT.Sqrt, bias=eps[:, :], scale=1.0 / D
                               ).then_inc(S.fin_root, 1)

        def weights_view(x, b, ri, n):
            v = x[:, 0:n, ri, bass.ds(b * BATCH, BATCH)].rearrange("p k g -> p g k")
            return v.unsqueeze(3).to_broadcast([P, BATCH, n, GC])

        def table_view(x, b, ri, n):
            return x[:, ri, bass.ds(b * BATCH, BATCH)].unsqueeze(2).to_broadcast([P, BATCH, n, GC])

        def weights_real(v, table, b, n, count):
            v.tensor_tensor(cw[:, :, 0, 0:n], weights_view(powers, b, 0, n), table_view(table, b, 0, n),
                            ALU.mult).then_inc(S.cwr_step, 1)
            v.tensor_tensor(tmp[:, 0, :, 0:n], weights_view(powers, b, 1, n), table_view(table, b, 1, n),
                            ALU.mult).then_inc(S.cwr_step, 1)
            v.wait_ge(S.cwr_step, count + 2)
            v.tensor_tensor(cw[:, :, 0, 0:n], cw[:, :, 0, 0:n], tmp[:, 0, :, 0:n], ALU.subtract
                            ).then_inc(S.cwr_step, 1)

        def weights_imag(pool, table, b, n, count, sign):
            pool.tensor_tensor(cw[:, :, 1, 0:n], weights_view(powers, b, 1 if sign > 0 else 2, n),
                               table_view(table, b, 0, n), ALU.mult).then_inc(S.cwi_step, 1)
            pool.tensor_tensor(tmp[:, 1, :, 0:n], weights_view(powers, b, 0, n), table_view(table, b, 1, n),
                               ALU.mult).then_inc(S.cwi_step, 1)
            pool.wait_ge(S.cwi_step, count + 2)
            pool.tensor_tensor(cw[:, :, 1, 0:n], cw[:, :, 1, 0:n], tmp[:, 1, :, 0:n],
                               ALU.add if sign > 0 else ALU.subtract).then_inc(S.cwi_step, 1)

        @block.gpsimd
        def _(pool):
            for w in range(4):
                split_lo(pool, w, 0)
            with pool.Fori(0, 2) as i:
                for par in range(2):
                    for u in range(4):
                        split_lo(pool, u, 2 * i + (par + 1))
            pool.wait_ge(S.b_done, 1)
            with pool.Fori(0, 2) as i:
                for par in range(2):
                    weights_imag(pool, bbar, 2 * i + par, L, 6 * i + 3 * par, 1)
                    for u in range(4):
                        split_lo(pool, u, 2 * i + (N_GM + par + 1))
                    pool.wait_ge(S.bxT_done, 8 * i + (4 * par + 4))

            weights_imag(pool, ct, 0, L + 1, 3 * NB, -1)
            with pool.Fori(0, 2) as i:
                for par in range(2):
                    for u in range(4):
                        split_lo(pool, u, 2 * i + (N_GS + par + 1))

            def add(o, x, y):
                pool.tensor_tensor(o, x, y, ALU.add).then_inc(S.lat_sum, 1)

            for n in (12, 13, 14):
                b = n - 11
                for w in (4 * n + 4, 4 * n + 5):
                    split_lo_at(pool, w)
                pool.wait_ge(S.y_done, b)
                weights_imag(pool, ct, b, L + 1, 3 * (NB + b), -1)
                for w in (4 * n + 6, 4 * n + 7):
                    split_lo_at(pool, w)
                pool.wait_ge(S.lat_sq, 2 * (n - 11))
                if n == 12:
                    add(k_rot[:, :], ev[:, 0], ev[:, 1])
                elif n == 13:
                    pool.wait_ge(S.lat_sum, 1)
                    add(k_rot[:, :], k_rot[:, :], ev[:, 0])
                    pool.wait_ge(S.lat_sum, 2)
                    add(k_rot[:, :], k_rot[:, :], ev[:, 1])
                else:
                    add(ev[:, 0], ev[:, 0], ev[:, 1])
            split_lo_at(pool, 64)
            for w in range(W_KN, W_GLU):
                split_lo_at(pool, w + 4)
            for i, k in enumerate((6, 7, 4, 5, 0, 1, 2, 3)):
                pool.wait_ge(S.yhi_done, i + 1)
                pool.tensor_tensor(y_lo[:, k], yraw[:, k], y_hi[:, k].bitcast(F32), ALU.subtract
                                   ).then_inc(S.ylo_done, 1)
            for m in range(8):
                for w in (W_GLU + 4 + 2 * m, W_GLU + 5 + 2 * m):
                    split_lo_at(pool, w)
                pool.wait_ge(S.ghi_done, m + 1)
                pool.tensor_tensor(mixed_lo[:, 8 + m], glu_t[:, 1], mixed_hi[:, 8 + m].bitcast(F32), ALU.subtract
                                   ).then_inc(S.glo_done, 1)
            for h in range(HEADS):
                pool.wait_ge(S.ohi_done, h + 1)
                pool.tensor_tensor(mixed_lo[:, h], glu_t[:, h % 2], mixed_hi[:, h].bitcast(F32), ALU.subtract
                                   ).then_inc(S.olo_done, 1)
            for w in range(W_OUT + 4, W_END):
                split_lo_at(pool, w)

        @block.vector
        def _(v):
            v.memset(ones[:, :], 1.0).then_inc(S.const_done, 1)
            v.memset(eps[:, :], EPS).then_inc(S.const_done, 1)

            def x_remainder(t):
                for k in range(4):
                    v.wait_ge(S.xhi_done, 4 * t + k + 1)
                    o = (slice(None), slice(4 * k, 4 * k + 4), slice(P * t, P * t + P))
                    v.tensor_tensor(h_lo[o], ps[:, 4 * ((t + 1) % 2) + k].rearrange("p (k n) -> p k n", k=4),
                                    h_hi[o].bitcast(F32), ALU.subtract).then_inc(S.xlo_done, 1)

            v.wait_ge(S.g_pre_in, 16)
            for t in range(TT):
                v.wait_ge(S.x_rms, t + 1)
                v.reciprocal(small[:, 2, t:t + 1], small[:, 1, t:t + 1]).then_inc(S.x_rinv, 1)
                v.wait_ge(S.x_rinv, t + 1)
                v.scalar_tensor_tensor(xt[:, t, :], xt[:, t, :], small[:, 2, t:t + 1], g_pre[:, :], ALU.mult, ALU.mult
                                       ).then_inc(S.x_normed, 1)
                if t:
                    x_remainder(t - 1)
            v.wait_ge(S.prm_in, 16 * 6)
            v.tensor_copy(araw[:, 2].rearrange("g (h n) -> g h n", h=2),
                          lsraw[:, :].unsqueeze(2).to_broadcast([PAIRS, 2, STATES])).then_inc(S.ls_ready, 1)
            x_remainder(TT - 1)

            links = [0]

            def link(ins):
                links[0] += 1
                ins.then_inc(S.prm_links, 1)
                v.wait_ge(S.prm_links, links[0])

            def angle(x, n, r, m, last):
                link(v.tensor_scalar(n, x, 1.0 / TWO_PI, ROUND, ALU.mult, ALU.add))
                link(v.tensor_scalar(n, n, ROUND, None, ALU.subtract))
                link(v.scalar_tensor_tensor(r, n, -PI_A, x, ALU.mult, ALU.add))
                link(v.scalar_tensor_tensor(r, n, -PI_B, r, ALU.mult, ALU.add))
                link(v.scalar_tensor_tensor(r, n, -PI_C, r, ALU.mult, ALU.add))
                link(v.tensor_scalar(r, r, PI_SAFE, -PI_SAFE, ALU.min, ALU.max))
                link(v.scalar_tensor_tensor(m, r, -1.0, r, ALU.mult, ALU.max))
                v.tensor_scalar(m, m, -1.0, HALF_PI, ALU.mult, ALU.add).then_inc(last, 1)

            def R(i):
                return prm[:, i]

            def tt(o, x, y, op):
                link(v.tensor_tensor(o, x, y, op))

            v.wait_ge(S.prmT_done, 1)
            v.tensor_copy(prm[:, R_ARE:R_STEP + 1].rearrange("p r g -> p (r g)"), ps[:, 4, 0:3 * PAIRS]
                          ).then_inc(S.ls_ready, 1)
            link(v.tensor_copy(dsk[:, :], ps[0:2 * GC, 4, 3 * PAIRS:4 * PAIRS]))
            v.wait_ge(S.step_done, 1)
            v.tensor_tensor(R(R_ZR), R(R_ARE), R(R_STEP), ALU.mult).then_inc(S.z_ready, 1)
            v.tensor_tensor(R(R_ZI), R(R_AIM), R(R_STEP), ALU.mult).then_inc(S.z_ready, 1)
            v.wait_ge(S.z_ready, 2)
            link(v.tensor_scalar(R(R_V), R(R_ZI), 0.5, None, ALU.mult))
            angle(R(R_V), R(R_N), R(R_R), R(R_M), S.angle_ready)
            v.wait_ge(S.z_acts, 2)
            link(v.tensor_scalar(R(R_X), R(R_ER), 1.0, None, ALU.add))
            tt(R(R_NR), R(R_X), R(R_TH), ALU.mult)
            v.wait_ge(S.trig_done, 2)
            link(v.scalar_tensor_tensor(R(R_S2), R(R_S), 2.0, R(R_S), ALU.mult, ALU.mult))
            tt(R(R_X), R(R_ER), R(R_S2), ALU.mult)
            tt(R(R_NR), R(R_NR), R(R_X), ALU.subtract)
            link(v.scalar_tensor_tensor(R(R_Y), R(R_S), 2.0, R(R_C), ALU.mult, ALU.mult))
            tt(R(R_NI), R(R_ER), R(R_Y), ALU.mult)
            for ri in range(3):
                link(v.memset(powers[:, 0, ri], 0.0 if ri else 1.0))
            tt(powers[:, 1, 0], R(R_ER), R(R_X), ALU.subtract)
            link(v.tensor_copy(powers[:, 1, 1], R(R_NI)))
            tt(R(R_DEN), R(R_ARE), R(R_ARE), ALU.mult)
            tt(R(R_X), R(R_AIM), R(R_AIM), ALU.mult)
            tt(R(R_DEN), R(R_DEN), R(R_X), ALU.add)
            link(v.reciprocal(R(R_DEN), R(R_DEN)))
            tt(R(R_X), R(R_NR), R(R_ARE), ALU.mult)
            tt(R(R_Y), R(R_NI), R(R_AIM), ALU.mult)
            tt(R(R_X), R(R_X), R(R_Y), ALU.add)
            tt(R(R_FR), R(R_X), R(R_DEN), ALU.mult)
            tt(R(R_X), R(R_NI), R(R_ARE), ALU.mult)
            tt(R(R_Y), R(R_NR), R(R_AIM), ALU.mult)
            tt(R(R_X), R(R_X), R(R_Y), ALU.subtract)
            tt(R(R_FI), R(R_X), R(R_DEN), ALU.mult)
            v.wait_ge(S.pos_in, 16)
            link(v.tensor_copy(ang[:, 0], pos[:, :]))
            link(v.tensor_scalar(ang[:, 0], ang[:, 0], inv_freq, None, ALU.mult))
            angle(ang[:, 0], ang[:, 1], ang[:, 2], ang[:, 3], S.rope_angle)
            scratch = prm[:, R_ZR:R_ZR + 4]
            for k in (1, 2, 4):
                src = [powers[:, 1:k + 1, ri] for ri in range(2)]
                by = [powers[:, k, ri].unsqueeze(1).to_broadcast([P, k, PAIRS]) for ri in range(2)]
                new = [powers[:, k + 1:2 * k + 1, ri] for ri in range(2)]
                s4 = scratch[:, 0:k]
                tt(new[0], src[0], by[0], ALU.mult)
                tt(s4, src[1], by[1], ALU.mult)
                tt(new[0], new[0], s4, ALU.subtract)
                tt(new[1], src[0], by[1], ALU.mult)
                tt(s4, src[1], by[0], ALU.mult)
                tt(new[1], new[1], s4, ALU.add)
            link(v.tensor_scalar(powers[:, 1:L + 1, 2], powers[:, 1:L + 1, 1], -1.0, None, ALU.mult))
            link(v.tensor_copy(chunk_a[:, 0, 0], powers[:, L, 0]))
            link(v.tensor_copy(chunk_a[:, 1, 1], powers[:, L, 0]))
            link(v.tensor_copy(chunk_a[:, 0, 1], powers[:, L, 2]))
            link(v.tensor_copy(chunk_a[:, 1, 0], powers[:, L, 1]))
            v.wait_ge(S.bc_in, 64)
            fr = R(R_FR).unsqueeze(2).to_broadcast([P, PAIRS, GC])
            fi = R(R_FI).unsqueeze(2).to_broadcast([P, PAIRS, GC])
            t0 = tmp[:, 0].rearrange("p g k c -> p (g k c)")[:, 0:PAIRS * GC].rearrange("p (g c) -> p g c", c=GC)
            tt(bbar[:, 0], braw[:, 0], fr, ALU.mult)
            tt(t0, braw[:, 1], fi, ALU.mult)
            tt(bbar[:, 0], bbar[:, 0], t0, ALU.subtract)
            tt(bbar[:, 1], braw[:, 1], fr, ALU.mult)
            tt(t0, braw[:, 0], fi, ALU.mult)
            v.tensor_tensor(bbar[:, 1], bbar[:, 1], t0, ALU.add).then_inc(S.b_done, 1)
            v.wait_ge(S.b_done, 1)
            v.wait_ge(S.ctT_done, 1)
            for ri in range(2):
                v.tensor_copy(ct[:, ri].rearrange("p g c -> p (g c)"), ps[:, 5 + ri]).then_inc(S.b_done, 1)
            v.wait_ge(S.b_done, 3)
            tt(same_ch[:, :], ident[0:2 * GC, 0:GC], ident[0:2 * GC, GC:2 * GC], ALU.add)
            link(v.memset(zeros[:, :], 0.0))
            v.wait_ge(S.rope_trig, 2)
            v.memset(states[:, 0], 0.0).then_inc(S.vin_evac, 1)

            with v.Fori(0, 2) as i:
                for par in range(2):
                    b = 2 * i + par
                    weights_real(v, bbar, b, L, 6 * i + 3 * par)
                    for k in range(4):
                        v.wait_ge(S.bxT_done, 8 * i + (4 * par + k + 1))
                        v.tensor_copy(mats[:, 4 * k:4 * k + 4].rearrange("p g n -> p (g n)"), ps[:, 4 + k]
                                      ).then_inc(S.bx_ready, 1)
                    v.wait_ge(S.vin_done, 2 * i + (par + 1))
                    for m in range(2):
                        v.tensor_copy(
                            states[:, 1:NQ + 1, :, bass.ds(b * BATCH + 4 * m, 4)].rearrange("p q r g -> p g r q"),
                            ps[:, 4 + m].rearrange("p (g r q) -> p g r q", g=4, r=2)).then_inc(S.vin_evac, 1)
            def block_diagonal(b):
                if b:
                    v.wait_ge(S.taps_done, b)
                for h in range(2):
                    v.tensor_copy(bd[64 * h:64 * h + 64, :, :, GC * h:GC * h + GC],
                                     bbar[64 * h:64 * h + 64, :, b * BATCH:(b + 1) * BATCH].rearrange(
                                         "p r g c -> p g r c")).then_inc(S.bd_done, 1)

            v.memset(bd[:, :, :, :], 0.0).then_inc(S.bd_done, 1)
            v.wait_ge(S.bd_done, 1)
            block_diagonal(0)
            v.wait_ge(S.bxT_done, 4 * NB)
            weights_real(v, ct, 0, L + 1, 3 * NB)
            v.wait_ge(S.vin_evac, 2 * NB + 1)
            with v.Fori(0, NQ - 2) as i:
                v.tensor_tensor(sw[:, :, :, :], chunk_a[:, :, :, :],
                                states[:, bass.ds(i + 1, 1)].to_broadcast([P, 2, 2, PAIRS]), ALU.mult
                                ).then_inc(S.scan_step, 1)
                v.wait_ge(S.scan_step, 3 * i + 1)
                v.tensor_tensor(st[:, :, :], sw[:, :, 0], sw[:, :, 1], ALU.add).then_inc(S.scan_step, 1)
                v.wait_ge(S.scan_step, 3 * i + 2)
                nxt = states[:, bass.ds(i + 2, 1)].rearrange("p a r g -> p (a r) g")
                v.tensor_tensor(nxt, nxt, st[:, :, :], ALU.add).then_inc(S.scan_step, 1)
                v.wait_ge(S.scan_step, 3 * i + 3)

            def taps_of(b):
                v.tensor_tensor(dm[:, :, :], same_ch[:, :].unsqueeze(1).to_broadcast([2 * GC, BATCH, GC]),
                                dsk[:, b * BATCH:(b + 1) * BATCH].unsqueeze(2).to_broadcast([2 * GC, BATCH, GC]),
                                ALU.mult).then_inc(S.taps_step, 1)
                v.wait_ge(S.taps_step, b + 1)
                v.wait_ge(S.taps_done, b + 1)
                src = ps[0:2 * GC, 4:6].rearrange("p b (g n) -> p (b g) n", g=4)
                v.tensor_copy(taps[:, :, GC:P], src[:, :, GC:P]).then_inc(S.taps_ready, 1)
                v.tensor_tensor(taps[:, :, 0:GC], src[:, :, 0:GC], dm[:, :, :], ALU.add).then_inc(S.taps_ready, 1)

            def output_weights(b):
                v.wait_ge(S.y_done, b)
                v.wait_ge(S.taps_stored, 16 * b)
                weights_real(v, ct, b, L + 1, 3 * (NB + b))
                block_diagonal(b)

            def normalise(tiles, rms, root):
                v.wait_ge(S.lat_rms, root)
                v.reciprocal(rms, rms).then_inc(S.lat_link, 1)
                v.wait_ge(S.lat_link, root)
                for k in tiles:
                    v.scalar_tensor_tensor(lat[:, k], lat[:, k], g_lat[:, k:k + 1], rms, ALU.mult, ALU.mult
                                           ).then_inc(S.lat_normed, 1)

            taps_of(0)
            for b in (1, 2):
                output_weights(b)
                taps_of(b)
            output_weights(3)
            normalise(range(4), k_rot[:, :], 1)
            taps_of(3)
            normalise((4, 5), ev[:, 0], 2)
            for i, k in enumerate((4, 5, 0, 1, 2, 3)):
                v.wait_ge(S.lat_hi_done, i + 1)
                v.tensor_tensor(lat_lo[:, k], lat[:, k], lat_hi[:, k].bitcast(F32), ALU.subtract
                                ).then_inc(S.lat_lo_done, 1)
                if i == 1:
                    for to, of, n, m in ((0, 0, 64, 0), (64, 0, 64, 0), (0, 32, 32, 1), (32, 0, 32, 1),
                                         (64, 32, 32, 1), (96, 0, 32, 1)):
                        v.tensor_copy(natural(ev[to:to + n, m]), steps(ps[of:of + n, 2])).then_inc(S.kr_evac, 1)
            v.wait_ge(S.kr_evac, 6)
            v.tensor_tensor(ev[:, 0], ev[:, 0], cos[:, :], ALU.mult).then_inc(S.kr_link, 1)
            v.scalar_tensor_tensor(ev[:, 1], ev[:, 1], rope_sign, sin[:, :], ALU.mult, ALU.mult
                                   ).then_inc(S.kr_link, 1)
            v.wait_ge(S.kr_link, 2)
            v.tensor_tensor(k_rot[:, :], ev[:, 0], ev[:, 1], ALU.add).then_inc(S.kr_done, 1)

            for quad in range(2):
                v.wait_ge(S.head_done, 27 + quad)
                if quad:
                    v.wait_ge(S.rope_done, 8)
                for k, (bank, table) in enumerate(((4, cos), (6, sin), (6, cos), (4, sin))):
                    v.scalar_tensor_tensor(lat[:, k], ps[:, bank + quad], SCALE, table[:, :], ALU.mult, ALU.mult
                                           ).then_inc(S.rope_mul, 1)
                v.wait_ge(S.rope_mul, 4 * quad + 4)
                for hq in range(4):
                    h = 4 * quad + hq
                    rows = slice(32 * hq, 32 * hq + 32)
                    to = 64 * (h % 2)
                    v.tensor_tensor(qr[to:to + 32, h // 2], lat[rows, 0], lat[rows, 1], ALU.subtract
                                    ).then_inc(S.rope_done, 1)
                    v.tensor_tensor(qr[to + 32:to + 64, h // 2], lat[rows, 2], lat[rows, 3], ALU.add
                                    ).then_inc(S.rope_done, 1)

            def glu(m, par, turn):
                v.wait_ge(S.sig_done, m + 1)
                v.tensor_tensor(glu_t[:, 1], ps[:, 2 * par], glu_t[:, 0], ALU.mult).then_inc(S.glu_val, 1)
                v.wait_ge(S.glu_val, m + 1)
                v.wait_ge(gs_in[par], 16 * turn + 16)
                v.tensor_tensor(glu_t[:, 1], glu_t[:, 1], lat[:, 4 + par], ALU.mult).then_inc(S.glu_prod, 1)
                v.wait_ge(S.ghi_done, m + 1)
                v.wait_ge(S.glo_done, m + 1)

            with v.Fori(0, 4) as i:
                for par in range(2):
                    glu(2 * i + par, par, i)

            def row_max(h, i):
                n = P * (i + 1)
                diag = ps[:, i, P * i:n]
                v.wait_ge(S.s_done, 4 * h + i + 1)
                v.tensor_tensor(diag, diag, mask, ALU.add).then_inc(S.s_link, 1)
                v.wait_ge(S.s_link, 4 * h + i + 1)
                if h:
                    v.wait_ge(S.exp_done, 4 * (h - 1) + i + 1)
                v.tensor_reduce(soft[:, 0, i:i + 1], ps[:, i, 0:n], AX.X, ALU.max, negate=True).then_inc(S.s_max, 1)

            def normalised(h, i):
                v.wait_ge(S.exp_done, 4 * h + i + 1)
                v.reciprocal(soft[:, 2, i:i + 1], soft[:, 1, i:i + 1]).then_inc(S.den_done, 1)
                v.wait_ge(S.den_done, 4 * h + i + 1)
                v.tensor_scalar(lat[:, i, 0:P * (i + 1)], lat[:, i, 0:P * (i + 1)], soft[:, 2, i:i + 1], None,
                                ALU.mult).then_inc(S.p_done, 1)

            def gate(h):
                v.wait_ge(S.o_done, h + 1)
                v.wait_ge(gm_in[h % 2], 16 * (h // 2) + 16)
                if h >= 2:
                    v.wait_ge(S.ohi_done, h - 1)
                    v.wait_ge(S.olo_done, h - 1)
                v.tensor_tensor(steps(glu_t[:, h % 2]), natural(ps[:, 6 + h % 2]), steps(lat[:, 4 + h % 2]), ALU.mult
                                ).then_inc(S.o_gated, 1)

            for h in range(HEADS + 1):
                if h < HEADS:
                    for i in range(TT):
                        row_max(h, i)
                        if i:
                            normalised(h, i - 1)
                    normalised(h, TT - 1)
                if h:
                    gate(h - 1)

            v.wait_ge(S.g_post_in, 16)
            for c in range(4):
                for t in range(TT):
                    v.wait_ge(S.out_sq, 4 * c + t + 1)
                    v.tensor_tensor(og[:, t, 512 * c:512 * c + 512], ps[:, 4 * (c % 2) + t],
                                    g_post[:, 512 * c:512 * c + 512], ALU.mult).then_inc(S.og_done, 1)
            for t in range(TT):
                v.tensor_reduce(fin[:, t, 4:5], fin[:, t, 0:4], AX.X, ALU.add).then_inc(S.fin_sum, 1)
            v.wait_ge(S.xr_in, 16 * 2 * TT)
            v.wait_ge(S.og_done, 16)
            for t in range(TT):
                v.wait_ge(S.fin_root, t + 1)
                v.reciprocal(fin[:, t, 6:7], fin[:, t, 5:6]).then_inc(S.fin_inv, 1)
                v.wait_ge(S.fin_inv, t + 1)
                v.scalar_tensor_tensor(og[:, t, :], og[:, t, :], fin[:, t, 6:7], xr[:, t, :], ALU.mult, ALU.add
                                       ).then_inc(S.fin_done, 1)

        @block.tensor
        def _(pe):
            pe.wait_ge(S.consts_in, 16)
            for t in range(TT):
                pe.wait_ge(S.x_normed, t + 1)
                for k in range(KT):
                    if t >= 2 and k % 4 == 0:
                        pe.wait_ge(S.xlo_done, 4 * (t - 2) + k // 4 + 1)
                    m = pe.transpose(ps[:, 4 * ((t + 1) % 2) + k // 4, P * (k % 4):P * (k % 4) + P],
                                     xt[:, t, P * k:P * k + P], ident)
                    if k % 4 == 3:
                        m.then_inc(S.xT_done, 1)
            pe.wait_ge(S.ls_ready, 1)
            pe.wait_ge(S.xlo_done, 12)
            for i in range(3):
                pe.transpose(ps[:, 4, PAIRS * i:PAIRS * (i + 1)], araw[:, i], ident[0:PAIRS, 0:PAIRS])
            pe.transpose(ps[0:2 * GC, 4, 3 * PAIRS:4 * PAIRS], draw[:, :], ident[0:PAIRS, 0:PAIRS]
                         ).then_inc(S.prmT_done, 1)
            pe.wait_ge(S.xlo_done, 16)

            def group(n, par, between=None, first=False):
                if not first:
                    pe.wait_ge(S.proj_evac, 2 * n - 2)
                for u in range(4):
                    pe.wait_ge(S.lo_done, 4 * n + u + 1)
                    for k in range(4):
                        for m in range(2):
                            cols = slice(GRP * k + P * m, GRP * k + P * m + P)
                            mm = three(pe, ps[:, 2 * par + m], w_hi[:, u, cols], w_lo[:, u, cols],
                                       h_hi[:, 4 * u + k], h_lo[:, 4 * u + k], u == 0 and k == 0, u == 3 and k == 3)
                    mm.then_inc(S.w_used, 1)
                    if u == 1 and between:
                        between()

            for n in range(4):
                group(n, n % 2, first=n < 2)
                if n == 0:
                    pe.wait_ge(S.bc_in, 64)
                    pe.wait_ge(S.ls_ready, 2)
                    for ri in range(2):
                        for blk in range(BATCH):
                            for h in range(2):
                                m = pe.matmul(ps[64 * h:64 * h + 64, 5 + ri, 64 * blk:64 * blk + 64],
                                              craw[:, ri, blk],
                                              ident.rearrange("p (g h c) -> p h g c", h=2, c=GC)[:, h],
                                              start=True, stop=True)
                    m.then_inc(S.ctT_done, 1)

            def transpose_inputs(b, first):
                pe.wait_ge(S.cwr_step, 3 * b + 3)
                pe.wait_ge(S.cwi_step, 3 * b + 3)
                pe.wait_ge(S.vin_evac, 2 * b + 1)
                pe.wait_ge(S.b_done, 3)
                for k in range(16):
                    m = pe.transpose(ps[:, 4 + k // 4, P * (k % 4):P * (k % 4) + P],
                                     cw[:, k // 2, k % 2, 0:L].rearrange("p k c -> p (k c)"), ident)
                    if k % 4 == 3:
                        m.then_inc(S.bxT_done, 1)

            def chunk_inputs(b):
                pe.wait_ge(S.bx_ready, 4 * b + 4)
                pe.wait_ge(S.u2_in, 16 * L * b + 16 * L)
                for k in range(16):
                    for h in range(2):
                        m = pe.matmul(ps[64 * h:64 * h + 64, 4 + k // 8, NQ * (k % 8):NQ * (k % 8) + NQ],
                                      mats[:, k, 64 * h:64 * h + 64], u2[:, 2 * (k // 2) + h], start=True, stop=True)
                m.then_inc(S.vin_done, 1)

            with pe.Fori(0, 2) as i:
                for par in range(2):
                    b = 2 * i + par
                    group(2 * i + (N_GM + par), par, lambda: transpose_inputs(b, False))
                    chunk_inputs(b)
            with pe.Fori(0, 2) as i:
                for par in range(2):
                    group(2 * i + (N_GS + par), par)

            def taps_mm(b):
                pe.wait_ge(S.cwr_step, 3 * (NB + b) + 3)
                pe.wait_ge(S.cwi_step, 3 * (NB + b) + 3)
                pe.wait_ge(S.bd_done, 2 * b + 3)
                if b == 0:
                    pe.wait_ge(S.vin_evac, 2 * NB + 1)
                else:
                    pe.wait_ge(S.taps_ready, 2 * b)
                if b == 3:
                    pe.wait_ge(S.lat_rms, 1)
                for g in range(BATCH):
                    for ri in range(2):
                        m = pe.matmul(ps[0:2 * GC, 4 + g // 4, P * (g % 4):P * (g % 4) + P], bd[:, g, ri],
                                      cw[:, g, ri, 0:L].rearrange("p k c -> p (k c)"), start=ri == 0, stop=ri == 1)
                m.then_inc(S.taps_done, 1)

            def outputs(b):
                pe.wait_ge(S.toep_in, 256 * b + 256)
                pe.wait_ge(S.u2_in, 16 * L * (NB + b + 1))
                if b == 0:
                    pe.wait_ge(S.scan_step, 3 * (NQ - 2))
                else:
                    pe.wait_ge(S.y_ready, 2 * b)
                for h in range(2):
                    for pair in range(BATCH):
                        for mh in range(2):
                            pe.matmul(ps[64 * mh:64 * mh + 64, 6 + h, NQ * pair:NQ * pair + NQ],
                                      mats[:, 2 * pair + h, 64 * mh:64 * mh + 64], u2[:, 2 * pair + h],
                                      start=pair == 0, stop=False, skip_group_check=True)
                for pair in range(BATCH):
                    for mh in range(2):
                        for ri in range(2):
                            for h in range(2):
                                rows = slice(64 * h, 64 * h + 64)
                                m = pe.matmul(ps[64 * mh:64 * mh + 64, 6 + h, NQ * pair:NQ * pair + NQ],
                                              cw[rows, pair, ri, 1 + 4 * mh:5 + 4 * mh].rearrange("p k c -> p (k c)"),
                                              states[rows, 0:NQ, ri, b * BATCH + pair], start=False, stop=ri == 1,
                                              skip_group_check=True)
                m.then_inc(S.y_done, 1)

            def latent_squares(i):
                pe.wait_ge(S.lat_sum, 3 + i)
                pe.wait_ge(S.taps_ready, 6 + 2 * i)
                pe.matmul(ps[:, 4 + i], ones[:, :], ev[:, 0] if i else k_rot[:, :], start=True, stop=True
                          ).then_inc(S.lat_ssq, 1)

            taps_mm(0)
            group(12, 0, lambda: outputs(0))
            taps_mm(1)
            group(13, 1, lambda: outputs(1))
            taps_mm(2)
            group(14, 0, lambda: (outputs(2), latent_squares(0)))
            taps_mm(3)
            pe.wait_ge(S.lo_done, W_KR + 1)
            pe.wait_ge(S.proj_evac, 28)
            for k in range(KT):
                cols = slice(ROPE * k, ROPE * k + ROPE)
                mm = three(pe, ps[0:ROPE, 2], w_hi[:, 0, cols], w_lo[:, 0, cols], h_hi[:, k], h_lo[:, k], k == 0,
                           k == KT - 1)
                if k == 7:
                    latent_squares(1)
            mm.then_inc(S.w_used, 1)
            outputs(3)

            def head_bank(j):
                if j >= 24:
                    if j == 24:
                        pe.wait_ge(S.lat_rms, 2)
                        pe.wait_ge(S.y_ready, 8)
                    return ps[:, 4 + j - 24]
                if j == 0:
                    pe.wait_ge(S.proj_evac, 30)
                elif j == 2:
                    pe.wait_ge(S.kr_evac, 6)
                elif j >= 4:
                    pe.wait_ge(S.head_evac, j - 3)
                return ps[:, j % 4]

            def head_tile(j, slot, width, m0, kts, vals=False):
                o = head_bank(j)
                for i, k in enumerate(kts):
                    if vals:
                        tok = slice(P * m0, P * m0 + P)
                        cols = slice(512 * i, 512 * i + 512)
                        pe.matmul(o, lat_hi[:, k, tok], w_hi[:, slot, cols], start=i == 0, stop=False)
                        pe.matmul(o, lat_hi[:, k, tok], w_lo[:, slot, cols], start=False, stop=False)
                        mm = pe.matmul(o, lat_lo[:, k, tok], w_hi[:, slot, cols], start=False, stop=i == len(kts) - 1)
                    else:
                        cols = slice(width * i + P * m0, width * i + P * m0 + P)
                        mm = three(pe, o, w_hi[:, slot, cols], w_lo[:, slot, cols], lat_hi[:, k], lat_lo[:, k], i == 0,
                                   i == len(kts) - 1)
                return mm

            j = 0
            for w in range(W_KN, W_GLU):
                pe.wait_ge(S.lo_done, w + 1)
                slot = w % 4
                if w == W_KN:
                    pe.wait_ge(S.lat_hi_done, 2)
                    pe.wait_ge(S.lat_lo_done, 2)
                if w == W_Q:
                    pe.wait_ge(S.lat_hi_done, 6)
                    pe.wait_ge(S.lat_lo_done, 6)
                for m in range(4 if w < W_Q else 2):
                    if w < W_V:
                        mm = head_tile(j, slot, 512, m, (4, 5))
                    elif w < W_Q:
                        mm = head_tile(j, slot, 512, m, (4, 5), True)
                    else:
                        mm = head_tile(j, slot, 256, m, (0, 1, 2, 3))
                    mm.then_inc(S.head_done, 1)
                    j += 1

            for m in range(8):
                if m < 2:
                    pe.wait_ge(S.head_evac, 24)
                else:
                    pe.wait_ge(S.sig_done, m - 1)
                    pe.wait_ge(S.glu_val, m - 1)
                for i, k in enumerate((6, 7, 4, 5, 0, 1, 2, 3)):
                    u = i // 4
                    slot = (W_GLU + 2 * m + u) % RING
                    if i % 4 == 0:
                        pe.wait_ge(S.lo_done, W_GLU + 2 * m + u + 1)
                    if m == 0:
                        pe.wait_ge(S.yhi_done, i + 1)
                        pe.wait_ge(S.ylo_done, i + 1)
                    for e in range(2):
                        cols = slice(2 * P * (k % 4) + P * e, 2 * P * (k % 4) + P * e + P)
                        mm = three(pe, ps[:, 2 * (m % 2) + e], w_hi[:, slot, cols], w_lo[:, slot, cols], y_hi[:, k],
                                   y_lo[:, k], i == 0, i == 7)
                    if i % 4 == 3:
                        mm.then_inc(S.w_used, 1)

            def scores(h):
                half = slice(64 * (h % 2), 64 * (h % 2) + 64)
                for i in range(TT):
                    n = P * (i + 1)
                    q = slice(P * i, n)
                    if h:
                        pe.wait_ge(S.exp_done, 4 * (h - 1) + i + 1)
                    pe.matmul(ps[:, i, 0:n], qn[:, h, q], kn[:, h, 0:n], start=True, stop=False)
                    pe.matmul(ps[:, i, 0:n], qr[half, h // 2, q], k_rot[half, 0:n], start=False, stop=True
                              ).then_inc(S.s_done, 1)

            def attend(h):
                for i in range(TT):
                    pe.wait_ge(S.p_done, 4 * h + i + 1)
                    if 4 * h + i >= 2:
                        pe.wait_ge(S.pT_evac, 4 * h + i - 1)
                    for k in range(i + 1):
                        m = pe.transpose(ps[:, 4 + i % 2, P * k:P * k + P], lat[:, i, P * k:P * k + P], ident)
                    m.then_inc(S.pT_done, 1)
                pe.wait_ge(S.pT_evac, 4 * h + 4)
                if h >= 2:
                    pe.wait_ge(S.o_gated, h - 1)
                for k in range(TT):
                    m = pe.matmul(ps[:, 6 + h % 2, P * k:SEQ], vv[:, k, P * h:P * h + P], pt[:, h % 2, k, P * k:SEQ],
                                  start=k == 0, stop=k == TT - 1)
                m.then_inc(S.o_done, 1)

            pe.wait_ge(S.sig_done, 8)
            pe.wait_ge(S.glu_val, 8)
            pe.wait_ge(S.kr_done, 1)
            pe.wait_ge(S.rope_done, 16)
            for h in range(HEADS + 1):
                if h < HEADS:
                    scores(h)
                if h:
                    attend(h - 1)

            for c in range(4):
                if c == 0:
                    pe.wait_ge(S.exp_done, 4 * HEADS)
                elif c == 1:
                    pe.wait_ge(S.pT_evac, 4 * HEADS)
                    pe.wait_ge(S.o_gated, HEADS)
                else:
                    pe.wait_ge(S.og_done, 4 * (c - 1))
                for u in range(8):
                    w = W_OUT + 8 * c + u
                    pe.wait_ge(S.lo_done, w + 1)
                    for i in range(2):
                        k = 2 * u + i
                        if c == 0:
                            hi, lo, n = (S.ohi_done, S.olo_done, k + 1) if k < 8 else (S.ghi_done, S.glo_done, k - 7)
                            pe.wait_ge(hi, n)
                            pe.wait_ge(lo, n)
                        cols = slice(512 * i, 512 * i + 512)
                        for t in range(TT):
                            o = ps[:, 4 * (c % 2) + t]
                            tok = slice(P * t, P * t + P)
                            pe.matmul(o, mixed_hi[:, k, tok], w_hi[:, w % 4, cols], start=k == 0, stop=False)
                            pe.matmul(o, mixed_hi[:, k, tok], w_lo[:, w % 4, cols], start=False, stop=False)
                            mm = pe.matmul(o, mixed_lo[:, k, tok], w_hi[:, w % 4, cols], start=False, stop=k == KT - 1)
                    mm.then_inc(S.w_used, 1)


_INS = ['x', 'positions', 'norm_pre', 'norm_post', 'w_in', 'q_norm', 'w_uq', 'kv_norm', 'w_ukv', 'ssm_a_re',
        'ssm_a_im', 'ssm_b_re', 'ssm_b_im', 'ssm_c_re', 'ssm_c_im', 'ssm_d', 'ssm_log_step', 'w_glu', 'w_out']
_MATRICES = ('x', 'w_in', 'w_uq', 'w_ukv', 'ssm_a_re', 'ssm_a_im', 'ssm_b_re', 'ssm_b_im', 'ssm_c_re', 'ssm_c_im',
             'w_glu', 'w_out')


def _constants():
    import numpy as np

    c = np.zeros((P, C_COLS), np.float32)
    c[:, C_ID:C_ID + P] = np.eye(P)
    c[:, C_MASK:C_MASK + P] = np.where(np.tri(P, dtype=bool), 0.0, -3e38)
    r = np.arange(P)
    c[:, C_FREQ] = (np.float32(10000.0) ** (-np.arange(0, ROPE, 2, dtype=np.float32) / np.float32(ROPE)))[r % 32]
    c[:, C_SIGN] = np.where(r // 32 % 2, 1.0, -1.0)
    return c


def kernel(**inputs):
    import numpy as _np
    import concourse.bacc as _bacc
    from concourse import mybir as _mybir
    from concourse.bass_utils import run_bass_kernel_spmd as _run

    nc = _bacc.Bacc("TRN2", target_bir_lowering=False, num_devices=1)
    arrays, aps = {}, {}
    for name in _INS:
        v = _np.ascontiguousarray(inputs[name])
        if name in _MATRICES:
            v = v.reshape(v.shape[1:])
        arrays[f"in_{name}_dram"] = v
    arrays["in_consts_dram"] = _constants()
    for key, v in arrays.items():
        aps[key[3:-5]] = nc.dram_tensor(key, v.shape, _mybir.dt.from_np(v.dtype), kind="ExternalInput").ap()
    out = nc.dram_tensor("out_0_dram", (SEQ, D), F32, kind="ExternalOutput").ap()
    hybrid_layer(nc, aps, out)
    r = _run(nc, [arrays], core_ids=[0])
    return r.results[0]["out_0_dram"].reshape(1, SEQ, D)
```

```python
from contextlib import ExitStack

import concourse.bass as bass
from concourse import mybir

F32 = mybir.dt.float32
F32R = mybir.dt.float32r
I32 = mybir.dt.int32
ALU = mybir.AluOpType
ACT = mybir.ActivationFunctionType
AX = mybir.AxisListType

P = 128
SEQ = 512
D = 2048
HEADS = 8
NOPE = 128
ROPE = 64
QR = 512
KVR = 256
CH = 1024
GC = 16
STATES = 64
PAIRS = CH // GC // 2
L = 8
NQ = SEQ // L
KT = D // P
TT = SEQ // P
EPS = 1e-6
SCALE = 1.0 / float(NOPE + ROPE) ** 0.5
TWO_PI = 6.283185307179586
PI_A, PI_B, PI_C = 6.28125, 0.0019350051879882812, 3.0199159819e-07
ROUND = 12582912.0
PI_SAFE = 3.1415925
HALF_PI = 1.5707963267948966

COL_CKV = QR
COL_KR = QR + KVR
COL_GM = COL_KR + ROPE
COL_U = COL_GM + CH
COL_GS = COL_U + CH

UNIT = 1024
RING = 4
GRP = 256
BATCH = 8
NB = PAIRS // BATCH
PADK = (L - 1) * GC + P

N_U, N_GM, N_GS, N_CKV, N_CQ, N_KR = 0, 4, 8, 12, 13, 15
W_KR = 4 * N_KR
W_KN = W_KR + 1
W_V = W_KN + 2
W_Q = W_V + 2
W_ROPE = W_Q + 4
W_GLU = W_ROPE + 2
W_OUT = W_GLU + 16
W_END = W_OUT + 32

C_ID, C_MASK, C_FREQ, C_SIGN, C_COLS = 0, P, 2 * P, 2 * P + 1, 2 * P + 2
(R_ARE, R_AIM, R_STEP, R_ZR, R_ZI, R_ER, R_TH, R_V, R_N, R_R, R_M, R_S, R_C, R_S2, R_NR, R_NI, R_X, R_Y,
 R_DEN, R_FR, R_FI) = range(21)


def hybrid_layer(nc, a, out):
    ctx = ExitStack()
    with ctx:
        def sb(name, shape, dt=F32, scope=ctx):
            return scope.enter_context(nc.sbuf_tensor(name, shape, dt))

        def sem(name):
            return ctx.enter_context(nc.semaphore(name))

        u_dram = nc.dram_tensor("u_scratch", [CH, SEQ], F32, kind="Internal").ap()
        gm_dram = nc.dram_tensor("gate_mla_scratch", [CH, SEQ], F32, kind="Internal").ap()
        gs_dram = nc.dram_tensor("gate_ssm_scratch", [CH, SEQ], F32, kind="Internal").ap()
        y_dram = nc.dram_tensor("y_scratch", [CH, SEQ], F32, kind="Internal").ap()
        taps_dram = nc.dram_tensor("taps_scratch", [GC, NB, 2 * BATCH, PADK], F32, kind="Internal").ap()

        stage = sb("stage", [P, RING, UNIT])
        w_hi = sb("w_hi", [P, RING, UNIT], F32R)
        w_lo = sb("w_lo", [P, RING, UNIT], F32R)
        consts = sb("consts", [P, C_COLS])
        ident = consts[:, C_ID:C_ID + P]
        mask = consts[:, C_MASK:C_MASK + P]
        inv_freq = consts[:, C_FREQ:C_FREQ + 1]
        rope_sign = consts[:, C_SIGN:C_SIGN + 1]
        ones = sb("ones", [P, P])
        eps = sb("eps", [P, 1])
        cos = sb("cos", [P, SEQ])
        sin = sb("sin", [P, SEQ])
        k_rot = sb("k_rot", [P, SEQ])
        lat = sb("lat", [P, 6, SEQ])
        g_lat = sb("g_lat", [P, 6])
        small = sb("small", [P, 3, TT])
        soft = sb("soft", [P, 3, TT])
        fin = sb("fin", [P, TT, 7])

        part1 = ExitStack()
        h_hi = sb("h_hi", [P, KT, SEQ], F32R, part1)
        h_lo = sb("h_lo", [P, KT, SEQ], F32R, part1)
        ev = sb("ev", [P, 2, SEQ], F32, part1)
        prm = sb("prm", [P, 21, PAIRS], F32, part1)
        powers = sb("powers", [P, L + 1, 3, PAIRS], F32, part1)
        bbar = sb("bbar", [P, 2, PAIRS, GC], F32, part1)
        ct = sb("ct", [P, 2, PAIRS, GC], F32, part1)
        chunk_a = sb("chunk_a", [P, 2, 2, PAIRS], F32, part1)
        araw = sb("araw", [PAIRS, 3, P], F32, part1)
        lsraw = sb("lsraw", [PAIRS, 2], F32, part1)
        draw = sb("draw", [PAIRS, 2 * GC], F32, part1)
        dsk = sb("dsk", [2 * GC, PAIRS], F32, part1)
        part0 = ExitStack()
        xt = sb("xt", [P, TT, D], F32, part0)
        g_pre = sb("g_pre", [P, D], F32, part0)
        junk = sb("junk", [P, D], F32, part0)
        part0.close()
        ssm = ExitStack()
        raws = ExitStack()
        braw = sb("braw", [P, 2, PAIRS, GC], F32, raws)
        craw = sb("craw", [P, 2, BATCH, STATES], F32, raws)
        ang = sb("ang", [P, 4, SEQ], F32, raws)
        pos = sb("pos", [P, SEQ], I32, raws)
        raws.close()
        states = sb("states", [P, NQ + 1, 2, PAIRS], F32, ssm)
        cw = sb("cw", [P, BATCH, 2, L + 1, GC], F32, ssm)
        tmp = sb("tmp", [P, 2, BATCH, L + 1, GC], F32, ssm)
        mats = sb("mats", [P, 2 * BATCH, P], F32, ssm)
        u2 = sb("u2", [P, 2 * BATCH, NQ], F32, ssm)
        bd = sb("bd", [P, BATCH, 2, 2 * GC], F32, ssm)
        sw = sb("sw", [P, 2, 2, PAIRS], F32, ssm)
        st = sb("st", [P, 2, PAIRS], F32, ssm)
        dm = sb("dm", [2 * GC, BATCH, GC], F32, ssm)
        same_ch = sb("same_ch", [2 * GC, GC], F32, ssm)
        zeros = sb("zeros", [GC, PADK - P], F32, ssm)
        yb = sb("yb", [P, 2 * BATCH, NQ], F32, ssm)
        ssm.close()
        taps = tmp[0:2 * GC].rearrange("p a b c d -> p (a b c d)")[:, 0:BATCH * P].rearrange(
            "p (g n) -> p g n", g=BATCH)
        part1.close()

        part2 = ExitStack()
        mixed_hi = sb("mixed_hi", [P, KT, SEQ], F32R, part2)
        mixed_lo = sb("mixed_lo", [P, KT, SEQ], F32R, part2)
        LAT = (10, 11, 12, 13, 8, 9)
        y_hi, y_lo = mixed_hi[:, 0:8], mixed_lo[:, 0:8]
        part3 = ExitStack()
        glu_t = sb("glu_t", [P, 2, SEQ], F32, part3)
        kn = sb("kn", [P, HEADS, SEQ], F32, part3)
        vv = sb("vv", [P, TT, CH], F32, part3)
        qn = sb("qn", [P, HEADS, SEQ], F32, part3)
        qr = sb("qr", [P, HEADS // 2, SEQ], F32, part3)
        glu_in = ExitStack()
        yraw = sb("yraw", [P, 8, SEQ], F32, glu_in)
        glu_in.close()
        pt = sb("pt", [P, 2, TT, SEQ], F32, part3)
        part3.close()
        og = sb("og", [P, TT, D], F32, part2)
        xr = sb("xr", [P, TT, D], F32, part2)
        g_post = sb("g_post", [P, D], F32, part2)
        part2.close()

        ps = ctx.enter_context(nc.psum_tensor("ps", [P, 8, 512], F32))

        class Sems:
            pass

        S = Sems()
        S.consts_in = sem("consts_in")
        S.g_pre_in = sem("g_pre_in")
        S.prm_in = sem("prm_in")
        S.bc_in = sem("bc_in")
        S.pos_in = sem("pos_in")
        S.hi_done = sem("hi_done")
        S.lo_done = sem("lo_done")
        S.w_used = sem("w_used")
        S.const_done = sem("const_done")
        S.x_sq = sem("x_sq")
        S.first_hi = sem("first_hi")
        S.cwi_part = sem("cwi_part")
        S.kr_first = sem("kr_first")
        S.tile_done = sem("tile_done")
        S.x_rms = sem("x_rms")
        S.x_rinv = sem("x_rinv")
        S.x_normed = sem("x_normed")
        S.xT_done = sem("xT_done")
        S.xhi_done = sem("xhi_done")
        S.xlo_done = sem("xlo_done")
        S.prm_links = sem("prm_links")
        S.prmT_done = sem("prmT_done")
        S.ls_ready = sem("ls_ready")
        S.step_done = sem("step_done")
        S.z_ready = sem("z_ready")
        S.z_acts = sem("z_acts")
        S.angle_ready = sem("angle_ready")
        S.trig_done = sem("trig_done")
        S.rope_angle = sem("rope_angle")
        S.rope_trig = sem("rope_trig")
        S.ctT_done = sem("ctT_done")
        S.b_done = sem("b_done")
        S.proj_done = sem("proj_done")
        S.proj_evac = sem("proj_evac")
        S.ev_done = sem("ev_done")
        S.ev_stored = sem("ev_stored")
        S.cwr_step = sem("cwr_step")
        S.cwi_step = sem("cwi_step")
        S.bxT_done = sem("bxT_done")
        S.bx_ready = sem("bx_ready")
        S.u2_in = sem("u2_in")
        S.vin_done = sem("vin_done")
        S.vin_evac = sem("vin_evac")
        S.scan_step = sem("scan_step")
        S.bd_done = sem("bd_done")
        S.taps_done = sem("taps_done")
        S.taps_step = sem("taps_step")
        S.taps_ready = sem("taps_ready")
        S.taps_stored = sem("taps_stored")
        S.zero_stored = sem("zero_stored")
        S.toep_in = sem("toep_in")
        S.y_done = sem("y_done")
        S.y_ready = sem("y_ready")
        S.y_stored = sem("y_stored")
        S.lat_sq = sem("lat_sq")
        S.lat_sum = sem("lat_sum")
        S.lat_ssq = sem("lat_ssq")
        S.lat_rms = sem("lat_rms")
        S.lat_link = sem("lat_link")
        S.lat_normed = sem("lat_normed")
        S.lat_hi_done = sem("lat_hi_done")
        S.lat_lo_done = sem("lat_lo_done")
        S.kr_evac = sem("kr_evac")
        S.kr_link = sem("kr_link")
        S.kr_done = sem("kr_done")
        S.head_done = sem("head_done")
        S.head_evac = sem("head_evac")
        S.rope_mul = sem("rope_mul")
        S.rope_done = sem("rope_done")
        S.yhi_done = sem("yhi_done")
        S.ylo_done = sem("ylo_done")
        S.glu_done = sem("glu_done")
        S.sig_done = sem("sig_done")
        S.glu_val = sem("glu_val")
        S.glu_prod = sem("glu_prod")
        S.ghi_done = sem("ghi_done")
        S.glo_done = sem("glo_done")
        S.s_done = sem("s_done")
        S.s_link = sem("s_link")
        S.s_max = sem("s_max")
        S.exp_done = sem("exp_done")
        S.den_done = sem("den_done")
        S.p_done = sem("p_done")
        S.pT_done = sem("pT_done")
        S.pT_evac = sem("pT_evac")
        S.o_done = sem("o_done")
        S.o_gated = sem("o_gated")
        S.ohi_done = sem("ohi_done")
        S.olo_done = sem("olo_done")
        S.out_done = sem("out_done")
        S.out_sq = sem("out_sq")
        S.og_done = sem("og_done")
        S.fin_sum = sem("fin_sum")
        S.fin_root = sem("fin_root")
        S.fin_inv = sem("fin_inv")
        S.fin_done = sem("fin_done")
        S.xr_in = sem("xr_in")
        S.g_post_in = sem("g_post_in")
        S.out_stored = sem("out_stored")
        x_in = [sem(f"x_in{t}") for t in range(TT)]
        w_in = [sem(f"w_in{s}") for s in range(RING)]
        yraw_in = [sem(f"yraw_in{s}") for s in range(2)]
        gs_in = [sem(f"gs_in{s}") for s in range(2)]
        gm_in = [sem(f"gm_in{s}") for s in range(2)]

        PT = ((4, 0), (4, P), (5, 0), (7, 0))

        block = ctx.enter_context(nc.Block())

        def unit_in(w, col):
            u = w % 4
            return a["w_in"][u * 512:(u + 1) * 512, bass.ds(col, GRP)].rearrange("(k p) n -> p k n", p=P)

        def pieces(w):
            return 1 if w < W_KN or w >= W_OUT else 4 if W_ROPE <= w < W_GLU else 2

        def loaded(w):
            return 16 * sum(pieces(x) for x in range(w % RING, w + 1, RING))

        def tiles_of(w):
            return 4 if w < W_Q else 2

        def used(w):
            if W_KN <= w < W_GLU:
                return S.head_done, sum(tiles_of(x) for x in range(W_KN, w + 1))
            return S.w_used, w + 1 - (W_GLU - W_KN if w >= W_GLU else 0)

        def load(sp, slot, src, turn, first=False):
            if not first:
                sp.wait_ge(S.lo_done, 4 * turn + (slot - 3))
            sp.dma_start(stage[:, slot, :].rearrange("p (k n) -> p k n", k=src.shape[1]), src
                         ).then_inc(w_in[slot], 16)

        def split_hi(act, slot, turn):
            act.wait_ge(w_in[slot], 16 * turn + 16)
            act.wait_ge(S.w_used, 4 * turn + (slot - 3))
            round_unit(act, slot)

        def split_hi_at(act, w):
            act.wait_ge(w_in[w % RING], loaded(w))
            act.wait_ge(*used(w - RING))
            round_unit(act, w % RING)

        def round_unit(act, slot):
            act.activation(w_hi[:, slot, :], stage[:, slot, :], ACT.Copy).then_inc(S.hi_done, 1)

        def split_lo(pool, slot, turn):
            pool.wait_ge(S.hi_done, 4 * turn + (slot - 3))
            pool.tensor_tensor(w_lo[:, slot, :], stage[:, slot, :], w_hi[:, slot, :].bitcast(F32),
                               ALU.subtract).then_inc(S.lo_done, 1)

        def split_first(pool, slot):
            pool.wait_ge(w_in[slot], 16)
            pool.tensor_copy(w_hi[:, slot, :], stage[:, slot, :]).then_inc(S.first_hi, 1)
            pool.wait_ge(S.first_hi, slot + 1)
            pool.tensor_tensor(w_lo[:, slot, :], stage[:, slot, :], w_hi[:, slot, :].bitcast(F32),
                               ALU.subtract).then_inc(S.lo_done, 1)

        def split_lo_at(pool, w):
            split_lo(pool, w % RING, w // RING)

        def three(pe, o, s_hi, s_lo, m_hi, m_lo, start, stop):
            pe.matmul(o, s_hi, m_hi, start=start, stop=False)
            pe.matmul(o, s_hi, m_lo, start=False, stop=False)
            return pe.matmul(o, s_lo, m_hi, start=False, stop=stop)

        def x_rows(ap, t, jj):
            return ap.rearrange("(q j) d -> j q d", j=L)[2 * t + jj]

        def natural(ap):
            return ap.rearrange("p (q j) -> p j q", j=L)

        def steps(ap):
            return ap.rearrange("p (j q) -> p j q", j=L)

        nonc = nc.allow_non_contiguous_dma(reason="rows of one SSM group")
        ctx.enter_context(nonc)

        @block.sync
        def _(sp):
            def load_x(t):
                for jj in range(2):
                    sp.dma_start(xt[64 * jj:64 * jj + 64, t, :], x_rows(a["x"], t, jj)).then_inc(x_in[t], 16)

            def load_w(w, col):
                load(sp, w % 4, unit_in(w, col), w // 4, first=w < 4)

            load_x(0)
            sp.dma_start(g_pre[:, :], a["norm_pre"].to_broadcast([P, D])).then_inc(S.g_pre_in, 16)
            sp.dma_start(consts[:, :], a["consts"]).then_inc(S.consts_in, 16)
            for t in range(1, TT):
                load_x(t)
                load_w(t - 1, COL_U)
            load_w(3, COL_U)
            sp.dma_start(araw[:, 0, :], a["ssm_a_re"].rearrange("(g h) n -> g (h n)", h=2)).then_inc(S.prm_in, 16)
            sp.dma_start(araw[:, 1, :], a["ssm_a_im"].rearrange("(g h) n -> g (h n)", h=2)).then_inc(S.prm_in, 16)
            sp.dma_start(lsraw[:, :], a["ssm_log_step"].rearrange("a (g h) -> (a g) h", h=2)).then_inc(S.prm_in, 16)
            sp.dma_start(draw[:, :], a["ssm_d"].rearrange("a (g c) -> (a g) c", c=2 * GC)).then_inc(S.prm_in, 16)
            for i, (g, n) in enumerate((("q_norm", 4), ("kv_norm", 2))):
                sp.dma_start(g_lat[:, 4 * i:4 * i + n], a[g].rearrange("a (k p) -> p (a k)", p=P)).then_inc(S.prm_in, 16)
            sp.wait_ge(S.xT_done, 16)
            for i, n in enumerate(("ssm_b_re", "ssm_b_im")):
                sp.dma_start(braw[:, i], a[n].rearrange("(g h) n c -> (h n) g c", h=2)).then_inc(S.bc_in, 16)
            for i, n in enumerate(("ssm_c_re", "ssm_c_im")):
                sp.dma_start(craw[:, i], a[n].rearrange("(b g) c n -> (g c) b n", b=BATCH)).then_inc(S.bc_in, 16)
            sp.dma_start(pos[:, :], a["positions"].to_broadcast([P, SEQ])).then_inc(S.pos_in, 16)
            for w in range(4, 8):
                load_w(w, COL_U + GRP)

            def load_u2(b):
                for r in range(L):
                    src = u_dram[bass.ds(b * (2 * BATCH * GC), 2 * BATCH * GC), (L - 1 - r) * NQ:(L - r) * NQ]
                    sp.dma_start(u2[GC * r:GC * r + GC], src.rearrange("(g c) q -> c g q", c=GC)).then_inc(S.u2_in, 16)

            with sp.Fori(0, 2) as i:
                for par in range(2):
                    for u in range(4):
                        col = (COL_GM - COL_U - 2 * GRP) * i + (COL_U + 2 * GRP + par * GRP)
                        load(sp, u, unit_in(u, col), 2 * i + (2 + par))
            sp.wait_ge(S.ev_stored, 16 * 4)
            with sp.Fori(0, 2) as i:
                for par in range(2):
                    sp.wait_ge(S.vin_evac, 4 * i + (2 * par + 1))
                    load_u2(2 * i + par)
                    for u in range(4):
                        col = (COL_GS - COL_GM - 2 * GRP) * i + (COL_GM + 2 * GRP + par * GRP)
                        load(sp, u, unit_in(u, col), 2 * i + (6 + par))
            sp.wait_ge(S.vin_done, NB)
            load_u2(0)
            sp.dma_start(taps_dram[:, :, :, 0:PADK - P].rearrange("c b g n -> c (b g) n"),
                         zeros[:, :].unsqueeze(1).to_broadcast([GC, 2 * PAIRS, PADK - P])).then_inc(S.zero_stored, 16)
            with sp.Fori(0, 2) as i:
                for par in range(2):
                    for u in range(4):
                        first, then = COL_GS + 2 * GRP + par * GRP, (1 - par) * COL_CKV
                        col = (then - first) * i + first
                        load(sp, u, unit_in(u, col), 2 * i + (10 + par))

            def load_toeplitz(b):
                sp.wait_ge(S.taps_ready, 2 * b + 2)
                for h in range(2):
                    sp.dma_start(taps_dram[:, b, BATCH * h:BATCH * (h + 1), PADK - P:PADK],
                                 taps[GC * h:GC * h + GC]).then_inc(S.taps_stored, 16)
                sp.wait_ge(S.taps_stored, 32 * b + 32)
                if b == 0:
                    sp.wait_ge(S.zero_stored, 16)
                    sp.wait_ge(S.vin_done, NB)
                else:
                    sp.wait_ge(S.y_done, b)
                for r in range(L):
                    sp.dma_start(mats[GC * r:GC * r + GC], taps_dram[:, b, :, GC * r:GC * r + P]
                                 ).then_inc(S.toep_in, 16)

            def unit_pieces(w):
                slot = stage[:, w % RING, :]
                if w < W_KN:
                    src = unit_in(w, GRP) if w < W_KR else a["w_in"][:, COL_KR:COL_GM].rearrange(
                        "(k p) n -> p k n", p=P)
                    return [(slot.rearrange("p (k n) -> p k n", k=src.shape[1]), src)]
                if w < W_Q:
                    v, i = divmod(w - W_KN, 2)
                    src = a["w_ukv"].rearrange("(k p) (h e n) -> k e p h n", p=P, e=2, n=NOPE)
                    dst = slot.rearrange("p (k h n) -> p k h n", k=2, n=NOPE)
                    return [(dst[:, k], src[k, v][:, 4 * i:4 * i + 4]) for k in range(2)]
                if w < W_GLU:
                    src = a["w_uq"].rearrange("(k p) (h n) -> p k h n", p=P, h=HEADS)
                    if w < W_ROPE:
                        i = w - W_Q
                        dst = slot.rearrange("p (k h n) -> p k h n", k=4, n=NOPE)
                        return [(dst[:, :, h], src[:, :, 2 * i + h, 0:NOPE]) for h in range(2)]
                    dst = slot.rearrange("p (k h n) -> p k h n", k=4, n=32)
                    c = NOPE + 32 * (w - W_ROPE)
                    return [(dst[:, k], src[:, k, :, c:c + 32]) for k in range(4)]
                if w < W_OUT:
                    m, u = divmod(w - W_GLU, 2)
                    src = a["w_glu"].rearrange("(k p) n -> p k n", p=P)[:, 4 * (1 - u):4 * (1 - u) + 4]
                    dst = slot.rearrange("p (k e n) -> p k e n", k=4, e=2)
                    return [(dst[:, :, e], src[:, :, CH * e + P * m:CH * e + P * m + P]) for e in range(2)]
                c, u = divmod(w - W_OUT, 8)
                u = (u + 4) % 8 if c == 0 else u
                return [(slot.rearrange("p (k n) -> p k n", k=2),
                         a["w_out"].rearrange("(k p) n -> p k n", p=P)[:, 2 * u:2 * u + 2, 512 * c:512 * c + 512])]

            def load_gs(m):
                sp.wait_ge(S.glu_prod, m - 1) if m >= 2 else None
                sp.dma_start(lat[:, 4 + m % 2], gs_dram[P * m:P * m + P]).then_inc(gs_in[m % 2], 16)

            def load_gm(h):
                if h < 2:
                    sp.wait_ge(S.glu_prod, 7 + h)
                else:
                    sp.wait_ge(S.o_gated, h - 1)
                sp.dma_start(lat[:, 4 + h % 2], gm_dram[P * h:P * h + P]).then_inc(gm_in[h % 2], 16)

            beside = {
                56: lambda: load_toeplitz(0),
                60: lambda: (sp.wait_ge(S.y_done, 1), load_u2(1), load_toeplitz(1)),
                64: lambda: (sp.wait_ge(S.y_done, 2), load_u2(2), load_toeplitz(2)),
                68: lambda: (sp.wait_ge(S.y_done, 3), load_u2(3), load_toeplitz(3)),
                73: lambda: (sp.wait_ge(S.y_stored, 16 * L * NB),
                             sp.dma_start(yraw[:, 4:8], y_dram[4 * P:8 * P].rearrange("(k p) n -> p k n", p=P)
                                          ).then_inc(yraw_in[0], 16),
                             sp.dma_start(yraw[:, 0:4], y_dram[0:4 * P].rearrange("(k p) n -> p k n", p=P)
                                          ).then_inc(yraw_in[1], 16)),
                75: lambda: (sp.wait_ge(S.lat_lo_done, 6), sp.wait_ge(S.ev_stored, 16 * 12), load_gs(0), load_gs(1)),
                98: lambda: (sp.wait_ge(S.o_gated, HEADS), sp.wait_ge(S.o_done, HEADS),
                             sp.dma_start(g_post[:, :], a["norm_post"].to_broadcast([P, D])).then_inc(S.g_post_in, 16),
                             [sp.dma_start(xr[64 * jj:64 * jj + 64, t, :], x_rows(a["x"], t, jj)).then_inc(S.xr_in, 16)
                              for t in range(TT) for jj in range(2)]),
            }
            for m in range(2, 8):
                beside[W_GLU + 2 * m + 3] = lambda m=m: load_gs(m)
            beside[W_OUT + RING] = lambda: [load_gm(h) for h in range(HEADS)]
            for w in range(4 * 14, W_END):
                if w in beside:
                    beside[w]()
                sp.wait_ge(S.lo_done, w - 3)
                for dst, src in unit_pieces(w):
                    sp.dma_start(dst, src).then_inc(w_in[w % RING], 16)
            for n, (t, c0, c1) in enumerate([(t, 0, D) for t in range(TT - 1)] + [(TT - 1, 0, D // 2), (TT - 1, D // 2, D)]):
                sp.wait_ge(S.fin_done, n + 1)
                for jj in range(2):
                    sp.dma_start(x_rows(out, t, jj)[:, c0:c1], og[64 * jj:64 * jj + 64, t, c0:c1]
                                 ).then_inc(S.out_stored, 16)
            sp.wait_ge(S.out_stored, 16 * 2 * (TT + 1))

        @block.scalar
        def _(act):
            def x_tile(t):
                for k in range(4):
                    act.wait_ge(S.xT_done, 4 * t + k + 1)
                    act.activation(h_hi[:, 4 * k:4 * k + 4, P * t:P * t + P],
                                   ps[:, 4 * ((t + 1) % 2) + k].rearrange("p (k n) -> p k n", k=4),
                                   ACT.Copy).then_inc(S.xhi_done, 1)

            act.wait_ge(S.const_done, 2)
            act.activation(fin[:, 0, 6:7], eps[:, :], ACT.Sqrt)
            for t in range(TT):
                act.wait_ge(x_in[t], 32)
                if t:
                    act.wait_ge(S.x_sq, t)
                act.activation(junk[:, :], xt[:, t, :], ACT.Square, accum_out=small[:, 0, t:t + 1]).then_inc(S.x_sq, 1)
                act.wait_ge(S.x_sq, t + 1)
                act.activation(small[:, 1, t:t + 1], small[:, 0, t:t + 1], ACT.Sqrt, bias=eps[:, :],
                               scale=1.0 / D).then_inc(S.x_rms, 1)
                if t:
                    x_tile(t - 1)
            x_tile(TT - 1)
            act.wait_ge(S.ls_ready, 2)
            act.activation(prm[:, R_STEP], prm[:, R_STEP], ACT.Exp).then_inc(S.step_done, 1)
            act.wait_ge(S.z_ready, 2)
            act.activation(prm[:, R_ER], prm[:, R_ZR], ACT.Exp).then_inc(S.z_acts, 1)
            act.activation(prm[:, R_TH], prm[:, R_ZR], ACT.Tanh, scale=0.5).then_inc(S.z_acts, 1)
            act.wait_ge(S.angle_ready, 1)
            act.activation(prm[:, R_S], prm[:, R_R], ACT.Sin).then_inc(S.trig_done, 1)
            act.activation(prm[:, R_C], prm[:, R_M], ACT.Sin).then_inc(S.trig_done, 1)
            act.wait_ge(S.rope_angle, 1)
            act.activation(sin[:, :], ang[:, 2], ACT.Sin).then_inc(S.rope_trig, 1)
            act.activation(cos[:, :], ang[:, 3], ACT.Sin).then_inc(S.rope_trig, 1)

            def evacuate(n, par, func, dram, row):
                act.wait_ge(S.w_used, 4 * n + 4)
                for m in range(2):
                    act.activation(ev[:, m], ps[:, 2 * par + m], func).then_inc(S.proj_evac, 1)
                act.wait_ge(S.proj_evac, 2 * n + 2)
                act.dma_start(dram[bass.ds(row, GRP)].rearrange("(m p) n -> p m n", p=P), ev[:, :, :]
                              ).then_inc(S.ev_stored, 16)
                act.wait_ge(S.ev_stored, 16 * n + 16)

            for n0, func, dram in ((N_U, ACT.Copy, u_dram), (N_GM, ACT.Silu, gm_dram), (N_GS, ACT.Silu, gs_dram)):
                with act.Fori(0, 2) as i:
                    for par in range(2):
                        for u in range(4):
                            split_hi(act, u, 2 * i + (n0 + par + 1))
                        evacuate(2 * i + (n0 + par), par, func, dram, (2 * GRP) * i + par * GRP)

            def gelu(b):
                act.wait_ge(S.y_done, b + 1)
                if b:
                    act.wait_ge(S.y_stored, 16 * L * b)
                for m in range(2):
                    act.activation(yb[:, :, :].rearrange("p (g h) q -> p h g q", h=2)[:, m],
                                   ps[:, 6 + m].rearrange("p (g q) -> p g q", q=NQ),
                                   ACT.Gelu_apprx_tanh).then_inc(S.y_ready, 1)
                act.wait_ge(S.y_ready, 2 * b + 2)
                dst = y_dram[2 * BATCH * GC * b:2 * BATCH * GC * (b + 1)].rearrange("(g c) (j q) -> j c g q", c=GC, j=L)
                for j in range(L):
                    act.dma_start(dst[j], yb[GC * j:GC * j + GC]).then_inc(S.y_stored, 16)

            def latent(n, first, consumed):
                act.wait_ge(S.w_used, 4 * n + 4)
                act.wait_ge(*consumed)
                for m in range(2):
                    bank = ps[:, 2 * (n % 2) + m]
                    act.activation(natural(ev[:, m]), steps(bank), ACT.Square).then_inc(S.lat_sq, 1)
                    act.activation(natural(lat[:, first + m]), steps(bank), ACT.Copy).then_inc(S.proj_evac, 1)

            def root_of(i, n):
                act.wait_ge(S.lat_ssq, i + 1)
                act.activation(k_rot[:, :], ps[:, 4 + i], ACT.Sqrt, bias=eps[:, :], scale=1.0 / n
                               ).then_inc(S.lat_rms, 1)

            for n, first, consumed in ((12, 4, (S.ev_stored, 16 * 12)), (13, 0, (S.lat_sum, 1)),
                                       (14, 2, (S.lat_sum, 2))):
                for w in (4 * n + 4, 4 * n + 5):
                    split_hi_at(act, w)
                if n == 13:
                    root_of(0, KVR)
                gelu(n - 12)
                for w in (4 * n + 6, 4 * n + 7):
                    split_hi_at(act, w)
                latent(n, first, consumed)

            def lat_tile(k):
                act.activation(mixed_hi[:, LAT[k]], lat[:, k], ACT.Copy).then_inc(S.lat_hi_done, 1)

            act.wait_ge(S.kr_first, 1)
            act.wait_ge(S.lat_normed, 2)
            for k in (4, 5):
                lat_tile(k)
            split_hi_at(act, 64)
            root_of(1, QR)

            def head_tile(j):
                act.wait_ge(S.head_done, j + 1)
                i = j % 8
                src = ps[:, j % 4]
                if j < 8:
                    act.activation(kn[:, i], src, ACT.Copy).then_inc(S.head_evac, 1)
                elif j < 16:
                    act.activation(vv[:, i % 4, 512 * (i // 4):512 * (i // 4) + 512], src, ACT.Copy
                                   ).then_inc(S.head_evac, 1)
                else:
                    act.activation(qn[:, i], src, ACT.Copy, scale=SCALE).then_inc(S.head_evac, 1)

            def y_tile(k):
                act.wait_ge(yraw_in[0 if k > 3 else 1], 16)
                act.activation(y_hi[:, k], yraw[:, k], ACT.Copy).then_inc(S.yhi_done, 1)

            tiles = iter(range(24))
            act.wait_ge(S.taps_ready, 8)
            y_tiles = {W_Q + 2: (6, 7), W_Q + 3: (4, 5), W_ROPE: (0, 1), W_ROPE + 1: (2, 3)}
            for w in range(W_KN, W_GLU):
                if w == W_V:
                    gelu(3)
                if w < W_ROPE:
                    for _ in range(4 if w < W_Q else 2):
                        head_tile(next(tiles))
                split_hi_at(act, w + 4)
                if w == W_KN:
                    act.wait_ge(S.lat_normed, 6)
                    for k in range(4):
                        lat_tile(k)
                for k in y_tiles.get(w, ()):
                    y_tile(k)
            act.wait_ge(S.kr_done, 1)

            def glu(m):
                for w in (W_GLU + 4 + 2 * m, W_GLU + 5 + 2 * m):
                    split_hi_at(act, w)
                act.wait_ge(*used(W_GLU + 2 * m + 1))
                if m:
                    act.wait_ge(S.glu_val, m)
                act.activation(glu_t[:, 0], ps[:, 2 * (m % 2) + 1], ACT.Sigmoid).then_inc(S.sig_done, 1)
                act.wait_ge(S.glu_prod, m + 1)
                act.activation(mixed_hi[:, 8 + m], glu_t[:, 1], ACT.Copy).then_inc(S.ghi_done, 1)

            for m in range(8):
                glu(m)

            def softmax_exp(h, i):
                n = P * (i + 1)
                act.wait_ge(S.s_max, 4 * h + i + 1)
                if h:
                    act.wait_ge(S.pT_done, 4 * (h - 1) + i + 1)
                act.activation(lat[:, i, 0:n], ps[:, i, 0:n], ACT.Exp, bias=soft[:, 0, i:i + 1],
                               accum_out=soft[:, 1, i:i + 1]).then_inc(S.exp_done, 1)

            def transposed(h, i):
                act.wait_ge(S.pT_done, 4 * h + max(i + 1, 2))
                if h >= 2:
                    act.wait_ge(S.o_done, h - 1)
                bank, col = PT[i]
                act.activation(pt[:, h % 2, 0:i + 1, P * i:P * i + P],
                               ps[:, bank, col:col + P * (i + 1)].rearrange("p (k n) -> p k n", n=P),
                               ACT.Copy).then_inc(S.pT_evac, 1)

            def gated(h):
                act.wait_ge(S.o_gated, h + 1)
                act.activation(mixed_hi[:, h], glu_t[:, h % 2], ACT.Copy).then_inc(S.ohi_done, 1)

            for i in range(TT):
                softmax_exp(0, i)
            for h in range(1, HEADS + 1):
                for tiles_now in ((0, 1), (2,), (3,)):
                    if h < HEADS:
                        for i in tiles_now:
                            softmax_exp(h, i)
                    for i in tiles_now:
                        transposed(h - 1, i)
                if h >= 2:
                    gated(h - 2)
            split_hi_at(act, W_OUT + 4)
            gated(HEADS - 1)

            def out_squares(c):
                if c < 3:
                    act.wait_ge(*used(W_OUT + 8 * c + 7))
                for t in range(TT):
                    if c == 3:
                        act.wait_ge(S.tile_done, t + 1)
                    if 4 * c + t:
                        act.wait_ge(S.out_sq, 4 * c + t)
                    act.activation(lat[:, 0], ps[:, 4 * (c % 2) + t], ACT.Square, accum_out=fin[:, t, c:c + 1]
                                   ).then_inc(S.out_sq, 1)
                    if c == 3:
                        act.wait_ge(S.fin_sum, 2)
                        act.wait_ge(S.out_sq, 4 * c + t + 1)
                        act.activation(fin[:, t, 5:6], fin[:, t, 3:4], ACT.Sqrt, bias=fin[:, t, 4:5], scale=1.0 / D
                                       ).then_inc(S.fin_root, 1)

            for c in range(4):
                for w in range(W_OUT + 8 * c + (4 if c else 5), min(W_OUT + 8 * c + 12, W_END)):
                    split_hi_at(act, w)
                out_squares(c)
        def weights_view(x, b, ri, n):
            v = x[:, 0:n, ri, bass.ds(b * BATCH, BATCH)].rearrange("p k g -> p g k")
            return v.unsqueeze(3).to_broadcast([P, BATCH, n, GC])

        def table_view(x, b, ri, n):
            return x[:, ri, bass.ds(b * BATCH, BATCH)].unsqueeze(2).to_broadcast([P, BATCH, n, GC])

        def weights_real(v, table, b, n, count, sign):
            v.tensor_tensor(cw[:, :, 1, 0:n], weights_view(powers, b, 1 if sign > 0 else 2, n),
                            table_view(table, b, 0, n), ALU.mult).then_inc(S.cwi_part, 1)
            v.tensor_tensor(cw[:, :, 0, 0:n], weights_view(powers, b, 0, n), table_view(table, b, 0, n),
                            ALU.mult).then_inc(S.cwr_step, 1)
            v.tensor_tensor(tmp[:, 0, :, 0:n], weights_view(powers, b, 1, n), table_view(table, b, 1, n),
                            ALU.mult).then_inc(S.cwr_step, 1)
            v.wait_ge(S.cwr_step, count + 2)
            v.tensor_tensor(cw[:, :, 0, 0:n], cw[:, :, 0, 0:n], tmp[:, 0, :, 0:n], ALU.subtract
                            ).then_inc(S.cwr_step, 1)

        def weights_imag(pool, table, b, n, turn, sign):
            pool.tensor_tensor(tmp[:, 1, :, 0:n], weights_view(powers, b, 0, n), table_view(table, b, 1, n),
                               ALU.mult).then_inc(S.cwi_step, 1)
            pool.wait_ge(S.cwi_step, 2 * turn + 1)
            pool.wait_ge(S.cwi_part, turn + 1)
            pool.tensor_tensor(cw[:, :, 1, 0:n], cw[:, :, 1, 0:n], tmp[:, 1, :, 0:n],
                               ALU.add if sign > 0 else ALU.subtract).then_inc(S.cwi_step, 1)

        @block.gpsimd
        def _(pool):
            for w in range(RING):
                split_first(pool, w)
            with pool.Fori(0, 2) as i:
                for par in range(2):
                    for u in range(4):
                        split_lo(pool, u, 2 * i + (par + 1))
            pool.wait_ge(S.b_done, 1)
            with pool.Fori(0, 2) as i:
                for par in range(2):
                    weights_imag(pool, bbar, 2 * i + par, L, 2 * i + par, 1)
                    for u in range(4):
                        split_lo(pool, u, 2 * i + (N_GM + par + 1))
                    pool.wait_ge(S.bxT_done, 8 * i + (4 * par + 4))

            weights_imag(pool, ct, 0, L + 1, NB, -1)
            with pool.Fori(0, 2) as i:
                for par in range(2):
                    for u in range(4):
                        split_lo(pool, u, 2 * i + (N_GS + par + 1))

            def add(o, x, y):
                pool.tensor_tensor(o, x, y, ALU.add).then_inc(S.lat_sum, 1)

            for n in (12, 13, 14):
                b = n - 11
                for w in (4 * n + 4, 4 * n + 5):
                    split_lo_at(pool, w)
                weights_imag(pool, ct, b, L + 1, NB + b, -1)
                for w in (4 * n + 6, 4 * n + 7):
                    split_lo_at(pool, w)
                pool.wait_ge(S.lat_sq, 2 * (n - 11))
                if n == 12:
                    add(k_rot[:, :], ev[:, 0], ev[:, 1])
                elif n == 13:
                    pool.wait_ge(S.lat_normed, 2)
                    add(k_rot[:, :], ev[:, 0], ev[:, 1])
                else:
                    add(k_rot[:, :], k_rot[:, :], ev[:, 0])
                    pool.wait_ge(S.lat_sum, 3)
                    add(k_rot[:, :], k_rot[:, :], ev[:, 1])
            split_lo_at(pool, 64)
            for w in range(W_KN, W_GLU):
                split_lo_at(pool, w + 4)
            for m in range(8):
                for w in (W_GLU + 4 + 2 * m, W_GLU + 5 + 2 * m):
                    split_lo_at(pool, w)
                pool.wait_ge(S.ghi_done, m + 1)
                pool.tensor_tensor(mixed_lo[:, 8 + m], glu_t[:, 1], mixed_hi[:, 8 + m].bitcast(F32), ALU.subtract
                                   ).then_inc(S.glo_done, 1)
            for h in range(HEADS):
                if h == HEADS - 1:
                    split_lo_at(pool, W_OUT + 4)
                pool.wait_ge(S.ohi_done, h + 1)
                pool.tensor_tensor(mixed_lo[:, h], glu_t[:, h % 2], mixed_hi[:, h].bitcast(F32), ALU.subtract
                                   ).then_inc(S.olo_done, 1)
            for w in range(W_OUT + 5, W_END):
                split_lo_at(pool, w)

        @block.vector
        def _(v):
            v.memset(ones[:, :], 1.0).then_inc(S.const_done, 1)
            v.memset(eps[:, :], EPS).then_inc(S.const_done, 1)

            def x_remainder(t):
                for k in range(4):
                    v.wait_ge(S.xhi_done, 4 * t + k + 1)
                    o = (slice(None), slice(4 * k, 4 * k + 4), slice(P * t, P * t + P))
                    v.tensor_tensor(h_lo[o], ps[:, 4 * ((t + 1) % 2) + k].rearrange("p (k n) -> p k n", k=4),
                                    h_hi[o].bitcast(F32), ALU.subtract).then_inc(S.xlo_done, 1)

            v.wait_ge(S.g_pre_in, 16)
            for t in range(TT):
                v.wait_ge(S.x_rms, t + 1)
                v.reciprocal(small[:, 2, t:t + 1], small[:, 1, t:t + 1]).then_inc(S.x_rinv, 1)
                v.wait_ge(S.x_rinv, t + 1)
                v.scalar_tensor_tensor(xt[:, t, :], xt[:, t, :], small[:, 2, t:t + 1], g_pre[:, :], ALU.mult, ALU.mult
                                       ).then_inc(S.x_normed, 1)
                if t:
                    x_remainder(t - 1)
            v.wait_ge(S.prm_in, 16 * 6)
            v.tensor_copy(araw[:, 2].rearrange("g (h n) -> g h n", h=2),
                          lsraw[:, :].unsqueeze(2).to_broadcast([PAIRS, 2, STATES])).then_inc(S.ls_ready, 1)
            x_remainder(TT - 1)

            links = [0]

            def link(ins):
                links[0] += 1
                ins.then_inc(S.prm_links, 1)
                v.wait_ge(S.prm_links, links[0])

            def angle(x, n, r, m, last):
                link(v.tensor_scalar(n, x, 1.0 / TWO_PI, ROUND, ALU.mult, ALU.add))
                link(v.tensor_scalar(n, n, ROUND, None, ALU.subtract))
                link(v.scalar_tensor_tensor(r, n, -PI_A, x, ALU.mult, ALU.add))
                link(v.scalar_tensor_tensor(r, n, -PI_B, r, ALU.mult, ALU.add))
                link(v.scalar_tensor_tensor(r, n, -PI_C, r, ALU.mult, ALU.add))
                link(v.tensor_scalar(r, r, PI_SAFE, -PI_SAFE, ALU.min, ALU.max))
                link(v.scalar_tensor_tensor(m, r, -1.0, r, ALU.mult, ALU.max))
                v.tensor_scalar(m, m, -1.0, HALF_PI, ALU.mult, ALU.add).then_inc(last, 1)

            def R(i):
                return prm[:, i]

            def tt(o, x, y, op):
                link(v.tensor_tensor(o, x, y, op))

            v.wait_ge(S.prmT_done, 1)
            v.tensor_copy(prm[:, R_ARE:R_STEP + 1].rearrange("p r g -> p (r g)"), ps[:, 4, 0:3 * PAIRS]
                          ).then_inc(S.ls_ready, 1)
            link(v.tensor_copy(dsk[:, :], ps[0:2 * GC, 4, 3 * PAIRS:4 * PAIRS]))
            v.wait_ge(S.step_done, 1)
            v.tensor_tensor(R(R_ZR), R(R_ARE), R(R_STEP), ALU.mult).then_inc(S.z_ready, 1)
            v.tensor_tensor(R(R_ZI), R(R_AIM), R(R_STEP), ALU.mult).then_inc(S.z_ready, 1)
            v.wait_ge(S.z_ready, 2)
            link(v.tensor_scalar(R(R_V), R(R_ZI), 0.5, None, ALU.mult))
            angle(R(R_V), R(R_N), R(R_R), R(R_M), S.angle_ready)
            v.wait_ge(S.z_acts, 2)
            link(v.tensor_scalar(R(R_X), R(R_ER), 1.0, None, ALU.add))
            tt(R(R_NR), R(R_X), R(R_TH), ALU.mult)
            v.wait_ge(S.trig_done, 2)
            link(v.scalar_tensor_tensor(R(R_S2), R(R_S), 2.0, R(R_S), ALU.mult, ALU.mult))
            tt(R(R_X), R(R_ER), R(R_S2), ALU.mult)
            tt(R(R_NR), R(R_NR), R(R_X), ALU.subtract)
            link(v.scalar_tensor_tensor(R(R_Y), R(R_S), 2.0, R(R_C), ALU.mult, ALU.mult))
            tt(R(R_NI), R(R_ER), R(R_Y), ALU.mult)
            for ri in range(3):
                link(v.memset(powers[:, 0, ri], 0.0 if ri else 1.0))
            tt(powers[:, 1, 0], R(R_ER), R(R_X), ALU.subtract)
            link(v.tensor_copy(powers[:, 1, 1], R(R_NI)))
            tt(R(R_DEN), R(R_ARE), R(R_ARE), ALU.mult)
            tt(R(R_X), R(R_AIM), R(R_AIM), ALU.mult)
            tt(R(R_DEN), R(R_DEN), R(R_X), ALU.add)
            link(v.reciprocal(R(R_DEN), R(R_DEN)))
            tt(R(R_X), R(R_NR), R(R_ARE), ALU.mult)
            tt(R(R_Y), R(R_NI), R(R_AIM), ALU.mult)
            tt(R(R_X), R(R_X), R(R_Y), ALU.add)
            tt(R(R_FR), R(R_X), R(R_DEN), ALU.mult)
            tt(R(R_X), R(R_NI), R(R_ARE), ALU.mult)
            tt(R(R_Y), R(R_NR), R(R_AIM), ALU.mult)
            tt(R(R_X), R(R_X), R(R_Y), ALU.subtract)
            tt(R(R_FI), R(R_X), R(R_DEN), ALU.mult)
            v.wait_ge(S.pos_in, 16)
            link(v.tensor_copy(ang[:, 0], pos[:, :]))
            link(v.tensor_scalar(ang[:, 0], ang[:, 0], inv_freq, None, ALU.mult))
            angle(ang[:, 0], ang[:, 1], ang[:, 2], ang[:, 3], S.rope_angle)
            scratch = prm[:, R_ZR:R_ZR + 4]
            for k in (1, 2, 4):
                src = [powers[:, 1:k + 1, ri] for ri in range(2)]
                by = [powers[:, k, ri].unsqueeze(1).to_broadcast([P, k, PAIRS]) for ri in range(2)]
                new = [powers[:, k + 1:2 * k + 1, ri] for ri in range(2)]
                s4 = scratch[:, 0:k]
                tt(new[0], src[0], by[0], ALU.mult)
                tt(s4, src[1], by[1], ALU.mult)
                tt(new[0], new[0], s4, ALU.subtract)
                tt(new[1], src[0], by[1], ALU.mult)
                tt(s4, src[1], by[0], ALU.mult)
                tt(new[1], new[1], s4, ALU.add)
            link(v.tensor_scalar(powers[:, 1:L + 1, 2], powers[:, 1:L + 1, 1], -1.0, None, ALU.mult))
            link(v.tensor_copy(chunk_a[:, 0, 0], powers[:, L, 0]))
            link(v.tensor_copy(chunk_a[:, 1, 1], powers[:, L, 0]))
            link(v.tensor_copy(chunk_a[:, 0, 1], powers[:, L, 2]))
            link(v.tensor_copy(chunk_a[:, 1, 0], powers[:, L, 1]))
            v.wait_ge(S.bc_in, 64)
            fr = R(R_FR).unsqueeze(2).to_broadcast([P, PAIRS, GC])
            fi = R(R_FI).unsqueeze(2).to_broadcast([P, PAIRS, GC])
            t0 = tmp[:, 0].rearrange("p g k c -> p (g k c)")[:, 0:PAIRS * GC].rearrange("p (g c) -> p g c", c=GC)
            tt(bbar[:, 0], braw[:, 0], fr, ALU.mult)
            tt(t0, braw[:, 1], fi, ALU.mult)
            tt(bbar[:, 0], bbar[:, 0], t0, ALU.subtract)
            tt(bbar[:, 1], braw[:, 1], fr, ALU.mult)
            tt(t0, braw[:, 0], fi, ALU.mult)
            v.tensor_tensor(bbar[:, 1], bbar[:, 1], t0, ALU.add).then_inc(S.b_done, 1)
            v.wait_ge(S.b_done, 1)
            v.wait_ge(S.ctT_done, 1)
            for ri in range(2):
                v.tensor_copy(ct[:, ri].rearrange("p g c -> p (g c)"), ps[:, 5 + ri]).then_inc(S.b_done, 1)
            v.wait_ge(S.b_done, 3)
            tt(same_ch[:, :], ident[0:2 * GC, 0:GC], ident[0:2 * GC, GC:2 * GC], ALU.add)
            link(v.memset(zeros[:, :], 0.0))
            v.wait_ge(S.rope_trig, 2)
            v.memset(states[:, 0], 0.0).then_inc(S.vin_evac, 1)

            with v.Fori(0, 2) as i:
                for par in range(2):
                    b = 2 * i + par
                    weights_real(v, bbar, b, L, 6 * i + 3 * par, 1)
                    for k in range(4):
                        v.wait_ge(S.bxT_done, 8 * i + (4 * par + k + 1))
                        v.tensor_copy(mats[:, 4 * k:4 * k + 4].rearrange("p g n -> p (g n)"), ps[:, 4 + k]
                                      ).then_inc(S.bx_ready, 1)
                    v.wait_ge(S.vin_done, 2 * i + (par + 1))
                    for m in range(2):
                        v.tensor_copy(
                            states[:, 1:NQ + 1, :, bass.ds(b * BATCH + 4 * m, 4)].rearrange("p q r g -> p g r q"),
                            ps[:, 4 + m].rearrange("p (g r q) -> p g r q", g=4, r=2)).then_inc(S.vin_evac, 1)
            def block_diagonal(b):
                if b:
                    v.wait_ge(S.taps_done, b)
                for h in range(2):
                    v.tensor_copy(bd[64 * h:64 * h + 64, :, :, GC * h:GC * h + GC],
                                     bbar[64 * h:64 * h + 64, :, b * BATCH:(b + 1) * BATCH].rearrange(
                                         "p r g c -> p g r c")).then_inc(S.bd_done, 1)

            v.memset(bd[:, :, :, :], 0.0).then_inc(S.bd_done, 1)
            v.wait_ge(S.bd_done, 1)
            block_diagonal(0)
            v.wait_ge(S.bxT_done, 4 * NB)
            weights_real(v, ct, 0, L + 1, 3 * NB, -1)
            def taps_of(b):
                v.tensor_tensor(dm[:, :, :], same_ch[:, :].unsqueeze(1).to_broadcast([2 * GC, BATCH, GC]),
                                dsk[:, b * BATCH:(b + 1) * BATCH].unsqueeze(2).to_broadcast([2 * GC, BATCH, GC]),
                                ALU.mult).then_inc(S.taps_step, 1)
                v.wait_ge(S.taps_step, b + 1)
                v.wait_ge(S.taps_done, b + 1)
                src = ps[0:2 * GC, 4:6].rearrange("p b (g n) -> p (b g) n", g=4)
                v.tensor_copy(taps[:, :, GC:P], src[:, :, GC:P]).then_inc(S.taps_ready, 1)
                v.tensor_tensor(taps[:, :, 0:GC], src[:, :, 0:GC], dm[:, :, :], ALU.add).then_inc(S.taps_ready, 1)

            taps_of(0)
            v.wait_ge(S.vin_evac, 2 * NB + 1)
            with v.Fori(0, (NQ - 2) // 2) as i:
                for s in range(2):
                    v.tensor_tensor(sw[:, :, :, :], chunk_a[:, :, :, :],
                                    states[:, bass.ds(2 * i + (s + 1), 1)].to_broadcast([P, 2, 2, PAIRS]), ALU.mult
                                    ).then_inc(S.scan_step, 1)
                    v.wait_ge(S.scan_step, 6 * i + (3 * s + 1))
                    v.tensor_tensor(st[:, :, :], sw[:, :, 0], sw[:, :, 1], ALU.add).then_inc(S.scan_step, 1)
                    v.wait_ge(S.scan_step, 6 * i + (3 * s + 2))
                    nxt = states[:, bass.ds(2 * i + (s + 2), 1)].rearrange("p a r g -> p (a r) g")
                    v.tensor_tensor(nxt, nxt, st[:, :, :], ALU.add).then_inc(S.scan_step, 1)
                    v.wait_ge(S.scan_step, 6 * i + (3 * s + 3))

            def output_weights(b):
                v.wait_ge(S.y_done, b)
                v.wait_ge(S.taps_stored, 32 * b)
                weights_real(v, ct, b, L + 1, 3 * (NB + b), -1)
                block_diagonal(b)

            def normalise(tiles, root):
                v.wait_ge(S.lat_rms, root)
                v.reciprocal(k_rot[:, :], k_rot[:, :]).then_inc(S.lat_link, 1)
                v.wait_ge(S.lat_link, root)
                for k in tiles:
                    v.scalar_tensor_tensor(lat[:, k], lat[:, k], g_lat[:, k:k + 1], k_rot[:, :], ALU.mult, ALU.mult
                                           ).then_inc(S.lat_normed, 1)

            def lat_remainder(k, n):
                v.wait_ge(S.lat_hi_done, n)
                v.tensor_tensor(mixed_lo[:, LAT[k]], lat[:, k], mixed_hi[:, LAT[k]].bitcast(F32), ALU.subtract
                                ).then_inc(S.lat_lo_done, 1)

            output_weights(1)
            taps_of(1)
            normalise((4, 5), 1)
            output_weights(2)
            taps_of(2)
            output_weights(3)
            taps_of(3)
            lat_remainder(4, 1)
            lat_remainder(5, 2)
            v.wait_ge(S.w_used, W_KR + 1)
            v.wait_ge(S.lat_sum, 4)
            for to, of, n, m in ((0, 0, 64, 0), (64, 0, 64, 0), (0, 32, 32, 1), (32, 0, 32, 1),
                                 (64, 32, 32, 1), (96, 0, 32, 1)):
                v.tensor_copy(natural(ev[to:to + n, m]), steps(ps[of:of + n, 3])).then_inc(S.kr_evac, 1)
            normalise(range(4), 2)
            for k in range(4):
                lat_remainder(k, 3 + k)
            v.wait_ge(S.kr_evac, 6)
            v.tensor_tensor(ev[:, 0], ev[:, 0], cos[:, :], ALU.mult).then_inc(S.kr_link, 1)
            v.scalar_tensor_tensor(ev[:, 1], ev[:, 1], rope_sign, sin[:, :], ALU.mult, ALU.mult
                                   ).then_inc(S.kr_link, 1)
            v.wait_ge(S.kr_link, 2)
            v.tensor_tensor(k_rot[:, :], ev[:, 0], ev[:, 1], ALU.add).then_inc(S.kr_done, 1)
            for i, k in enumerate((6, 7, 4, 5, 0, 1, 2, 3)):
                v.wait_ge(S.yhi_done, i + 1)
                v.tensor_tensor(y_lo[:, k], yraw[:, k], y_hi[:, k].bitcast(F32), ALU.subtract
                                ).then_inc(S.ylo_done, 1)

            for quad in range(2):
                v.wait_ge(S.head_done, 27 + quad)
                if quad:
                    v.wait_ge(S.rope_done, 8)
                for k, (bank, table) in enumerate(((4, cos), (6, sin), (6, cos), (4, sin))):
                    v.scalar_tensor_tensor(lat[:, k], ps[:, bank + quad], SCALE, table[:, :], ALU.mult, ALU.mult
                                           ).then_inc(S.rope_mul, 1)
                v.wait_ge(S.rope_mul, 4 * quad + 4)
                for hq in range(4):
                    h = 4 * quad + hq
                    rows = slice(32 * hq, 32 * hq + 32)
                    to = 64 * (h % 2)
                    v.tensor_tensor(qr[to:to + 32, h // 2], lat[rows, 0], lat[rows, 1], ALU.subtract
                                    ).then_inc(S.rope_done, 1)
                    v.tensor_tensor(qr[to + 32:to + 64, h // 2], lat[rows, 2], lat[rows, 3], ALU.add
                                    ).then_inc(S.rope_done, 1)

            def glu(m, par, turn):
                v.wait_ge(S.sig_done, m + 1)
                v.tensor_tensor(glu_t[:, 1], ps[:, 2 * par], glu_t[:, 0], ALU.mult).then_inc(S.glu_val, 1)
                v.wait_ge(S.glu_val, m + 1)
                v.wait_ge(gs_in[par], 16 * turn + 16)
                v.tensor_tensor(glu_t[:, 1], glu_t[:, 1], lat[:, 4 + par], ALU.mult).then_inc(S.glu_prod, 1)
                v.wait_ge(S.ghi_done, m + 1)
                v.wait_ge(S.glo_done, m + 1)

            with v.Fori(0, 4) as i:
                for par in range(2):
                    glu(2 * i + par, par, i)

            def row_max(h, i):
                n = P * (i + 1)
                diag = ps[:, i, P * i:n]
                v.wait_ge(S.s_done, 4 * h + i + 1)
                v.tensor_tensor(diag, diag, mask, ALU.add).then_inc(S.s_link, 1)
                v.wait_ge(S.s_link, 4 * h + i + 1)
                if h:
                    v.wait_ge(S.exp_done, 4 * (h - 1) + i + 1)
                v.tensor_reduce(soft[:, 0, i:i + 1], ps[:, i, 0:n], AX.X, ALU.max, negate=True).then_inc(S.s_max, 1)

            def normalised(h, i):
                v.wait_ge(S.exp_done, 4 * h + i + 1)
                v.reciprocal(soft[:, 2, i:i + 1], soft[:, 1, i:i + 1]).then_inc(S.den_done, 1)
                v.wait_ge(S.den_done, 4 * h + i + 1)
                v.tensor_scalar(lat[:, i, 0:P * (i + 1)], lat[:, i, 0:P * (i + 1)], soft[:, 2, i:i + 1], None,
                                ALU.mult).then_inc(S.p_done, 1)

            def gate(h):
                v.wait_ge(S.o_done, h + 1)
                v.wait_ge(gm_in[h % 2], 16 * (h // 2) + 16)
                if h >= 2:
                    v.wait_ge(S.ohi_done, h - 1)
                    v.wait_ge(S.olo_done, h - 1)
                v.tensor_tensor(steps(glu_t[:, h % 2]), natural(ps[:, 6]), steps(lat[:, 4 + h % 2]), ALU.mult
                                ).then_inc(S.o_gated, 1)

            for h in range(HEADS + 2):
                if h < HEADS:
                    for i in range(TT):
                        row_max(h, i)
                if h >= 2:
                    gate(h - 2)
                if h < HEADS:
                    for i in range(TT):
                        normalised(h, i)

            v.wait_ge(S.g_post_in, 16)
            for c in range(4):
                for t in range(TT):
                    v.wait_ge(S.out_sq, 4 * c + t + 1)
                    v.tensor_tensor(og[:, t, 512 * c:512 * c + 512], ps[:, 4 * (c % 2) + t],
                                    g_post[:, 512 * c:512 * c + 512], ALU.mult).then_inc(S.og_done, 1)
                    if c == 3:
                        if t == 0:
                            v.wait_ge(S.xr_in, 16 * 2 * TT)
                        v.wait_ge(S.fin_root, t + 1)
                        v.reciprocal(fin[:, t, 6:7], fin[:, t, 5:6]).then_inc(S.fin_inv, 1)
                        v.wait_ge(S.fin_inv, t + 1)
                        v.wait_ge(S.og_done, 4 * c + t + 1)
                        parts = 2 if t == TT - 1 else 1
                        for n in range(parts):
                            cols = slice(D // parts * n, D // parts * (n + 1))
                            v.scalar_tensor_tensor(og[:, t, cols], og[:, t, cols], fin[:, t, 6:7], xr[:, t, cols],
                                                   ALU.mult, ALU.add).then_inc(S.fin_done, 1)
                if c == 2:
                    v.tensor_reduce(fin[:, :, 4], fin[:, :, 0:3], AX.X, ALU.add).then_inc(S.fin_sum, 1)
                    v.wait_ge(S.fin_sum, 1)
                    v.tensor_scalar(fin[:, :, 4], fin[:, :, 4], 1.0 / D, EPS, ALU.mult, ALU.add
                                    ).then_inc(S.fin_sum, 1)

        @block.tensor
        def _(pe):
            pe.wait_ge(S.consts_in, 16)
            for t in range(TT):
                pe.wait_ge(S.x_normed, t + 1)
                for k in range(KT):
                    if t >= 2 and k % 4 == 0:
                        pe.wait_ge(S.xlo_done, 4 * (t - 2) + k // 4 + 1)
                    m = pe.transpose(ps[:, 4 * ((t + 1) % 2) + k // 4, P * (k % 4):P * (k % 4) + P],
                                     xt[:, t, P * k:P * k + P], ident)
                    if k % 4 == 3:
                        m.then_inc(S.xT_done, 1)
            pe.wait_ge(S.ls_ready, 1)
            pe.wait_ge(S.xlo_done, 12)
            for i in range(3):
                pe.transpose(ps[:, 4, PAIRS * i:PAIRS * (i + 1)], araw[:, i], ident[0:PAIRS, 0:PAIRS])
            pe.transpose(ps[0:2 * GC, 4, 3 * PAIRS:4 * PAIRS], draw[:, :], ident[0:PAIRS, 0:PAIRS]
                         ).then_inc(S.prmT_done, 1)
            pe.wait_ge(S.xlo_done, 16)

            def group(n, par, between=None, first=False, at=(1, 3)):
                if not first:
                    pe.wait_ge(S.proj_evac, 2 * n - 2)
                for u in range(4):
                    pe.wait_ge(S.lo_done, 4 * n + u + 1)
                    for k in range(4):
                        for m in range(2):
                            cols = slice(GRP * k + P * m, GRP * k + P * m + P)
                            mm = three(pe, ps[:, 2 * par + m], w_hi[:, u, cols], w_lo[:, u, cols],
                                       h_hi[:, 4 * u + k], h_lo[:, 4 * u + k], u == 0 and k == 0, u == 3 and k == 3)
                        if (u, k) == at and between and k < 3:
                            between()
                    mm.then_inc(S.w_used, 1)
                    if (u, 3) == at and between:
                        between()

            for n in range(4):
                group(n, n % 2, first=n < 2)
                if n == 0:
                    pe.wait_ge(S.bc_in, 64)
                    pe.wait_ge(S.ls_ready, 2)
                    for ri in range(2):
                        for blk in range(BATCH):
                            for h in range(2):
                                m = pe.matmul(ps[64 * h:64 * h + 64, 5 + ri, 64 * blk:64 * blk + 64],
                                              craw[:, ri, blk],
                                              ident.rearrange("p (g h c) -> p h g c", h=2, c=GC)[:, h],
                                              start=True, stop=True)
                    m.then_inc(S.ctT_done, 1)

            def transpose_inputs(b):
                pe.wait_ge(S.cwr_step, 3 * b + 3)
                pe.wait_ge(S.cwi_step, 2 * b + 2)
                pe.wait_ge(S.vin_evac, 2 * b + 1)
                pe.wait_ge(S.b_done, 3)
                for k in range(16):
                    m = pe.transpose(ps[:, 4 + k // 4, P * (k % 4):P * (k % 4) + P],
                                     cw[:, k // 2, k % 2, 0:L].rearrange("p k c -> p (k c)"), ident)
                    if k % 4 == 3:
                        m.then_inc(S.bxT_done, 1)

            def chunk_inputs(b):
                pe.wait_ge(S.bx_ready, 4 * b + 4)
                pe.wait_ge(S.u2_in, 16 * L * b + 16 * L)
                for k in range(16):
                    for h in range(2):
                        m = pe.matmul(ps[64 * h:64 * h + 64, 4 + k // 8, NQ * (k % 8):NQ * (k % 8) + NQ],
                                      mats[:, k, 64 * h:64 * h + 64], u2[:, 2 * (k // 2) + h], start=True, stop=True)
                m.then_inc(S.vin_done, 1)

            with pe.Fori(0, 2) as i:
                for par in range(2):
                    b = 2 * i + par
                    group(2 * i + (N_GM + par), par, lambda: transpose_inputs(b))
                    chunk_inputs(b)
            def taps_mm(b):
                pe.wait_ge(S.cwr_step, 3 * (NB + b) + 3)
                pe.wait_ge(S.cwi_step, 2 * (NB + b) + 2)
                pe.wait_ge(S.bd_done, 2 * b + 3)
                if b == 0:
                    pe.wait_ge(S.vin_evac, 2 * NB + 1)
                else:
                    pe.wait_ge(S.taps_ready, 2 * b)
                if b == 2:
                    pe.wait_ge(S.lat_rms, 1)
                for g in range(BATCH):
                    for ri in range(2):
                        m = pe.matmul(ps[0:2 * GC, 4 + g // 4, P * (g % 4):P * (g % 4) + P], bd[:, g, ri],
                                      cw[:, g, ri, 0:L].rearrange("p k c -> p (k c)"), start=ri == 0, stop=ri == 1)
                m.then_inc(S.taps_done, 1)

            def outputs(b):
                pe.wait_ge(S.toep_in, 128 * b + 128)
                pe.wait_ge(S.u2_in, 16 * L * (NB + b + 1))
                if b == 0:
                    pe.wait_ge(S.scan_step, 3 * (NQ - 2))
                else:
                    pe.wait_ge(S.y_ready, 2 * b)
                for h in range(2):
                    for pair in range(BATCH):
                        for mh in range(2):
                            pe.matmul(ps[64 * mh:64 * mh + 64, 6 + h, NQ * pair:NQ * pair + NQ],
                                      mats[:, BATCH * h + pair, 64 * mh:64 * mh + 64], u2[:, 2 * pair + h],
                                      start=pair == 0, stop=False, skip_group_check=True)
                for pair in range(BATCH):
                    for mh in range(2):
                        for ri in range(2):
                            for h in range(2):
                                rows = slice(64 * h, 64 * h + 64)
                                m = pe.matmul(ps[64 * mh:64 * mh + 64, 6 + h, NQ * pair:NQ * pair + NQ],
                                              cw[rows, pair, ri, 1 + 4 * mh:5 + 4 * mh].rearrange("p k c -> p (k c)"),
                                              states[rows, 0:NQ, ri, b * BATCH + pair], start=False, stop=ri == 1,
                                              skip_group_check=True)
                m.then_inc(S.y_done, 1)

            def latent_squares(i):
                pe.wait_ge(S.lat_sum, 4 if i else 1)
                pe.wait_ge(S.taps_ready, 8 if i else 4)
                pe.matmul(ps[:, 4 + i], ones[:, :], k_rot[:, :], start=True, stop=True).then_inc(S.lat_ssq, 1)

            for n in range(N_GS, N_CKV):
                group(n, n % 2, (lambda: taps_mm(0)) if n == N_GS else None)
            group(N_CKV, 0, lambda: outputs(0), at=(2, 1))
            taps_mm(1)
            group(N_CQ, 1, lambda: (latent_squares(0), outputs(1)), at=(2, 1))
            taps_mm(2)
            group(N_CQ + 1, 0, lambda: outputs(2), at=(2, 1))
            taps_mm(3)
            pe.wait_ge(S.lo_done, W_KR + 1)
            pe.wait_ge(S.proj_evac, 28)
            for i, k in enumerate((8, 9, *range(8), *range(10, KT))):
                cols = slice(ROPE * k, ROPE * k + ROPE)
                mm = three(pe, ps[0:ROPE, 3], w_hi[:, 0, cols], w_lo[:, 0, cols], h_hi[:, k], h_lo[:, k], i == 0,
                           i == KT - 1)
                if i == 1:
                    mm.then_inc(S.kr_first, 1)
            mm.then_inc(S.w_used, 1)
            latent_squares(1)

            def head_bank(j):
                if j >= 24:
                    if j == 24:
                        pe.wait_ge(S.lat_rms, 2)
                        pe.wait_ge(S.y_ready, 8)
                    return ps[:, 4 + j - 24]
                if j == 0:
                    pe.wait_ge(S.proj_evac, 30)
                elif j == 3:
                    pe.wait_ge(S.kr_evac, 6)
                elif j >= 4:
                    pe.wait_ge(S.head_evac, j - 3)
                return ps[:, j % 4]

            def head_tile(j, slot, width, m0, kts, vals=False):
                o = head_bank(j)
                for i, k in enumerate(kts):
                    if vals:
                        tok = slice(P * m0, P * m0 + P)
                        cols = slice(512 * i, 512 * i + 512)
                        pe.matmul(o, mixed_hi[:, LAT[k], tok], w_hi[:, slot, cols], start=i == 0, stop=False)
                        pe.matmul(o, mixed_hi[:, LAT[k], tok], w_lo[:, slot, cols], start=False, stop=False)
                        mm = pe.matmul(o, mixed_lo[:, LAT[k], tok], w_hi[:, slot, cols], start=False, stop=i == len(kts) - 1)
                    else:
                        cols = slice(width * i + P * m0, width * i + P * m0 + P)
                        mm = three(pe, o, w_hi[:, slot, cols], w_lo[:, slot, cols], mixed_hi[:, LAT[k]],
                                   mixed_lo[:, LAT[k]], i == 0,
                                   i == len(kts) - 1)
                return mm

            j = 0
            for w in range(W_KN, W_GLU):
                pe.wait_ge(S.lo_done, w + 1)
                slot = w % 4
                if w == W_KN:
                    pe.wait_ge(S.lat_hi_done, 2)
                    pe.wait_ge(S.lat_lo_done, 2)
                if w == W_Q:
                    pe.wait_ge(S.lat_hi_done, 6)
                    pe.wait_ge(S.lat_lo_done, 6)
                for m in range(4 if w < W_Q else 2):
                    if w < W_V:
                        mm = head_tile(j, slot, 512, m, (4, 5))
                    elif w < W_Q:
                        mm = head_tile(j, slot, 512, m, (4, 5), True)
                    else:
                        mm = head_tile(j, slot, 256, m, (0, 1, 2, 3))
                    mm.then_inc(S.head_done, 1)
                    j += 1
                if w == W_KN + 1:
                    outputs(3)

            for m in range(8):
                if m < 2:
                    pe.wait_ge(S.head_evac, 24)
                else:
                    pe.wait_ge(S.sig_done, m - 1)
                    pe.wait_ge(S.glu_val, m - 1)
                for i, k in enumerate((6, 7, 4, 5, 0, 1, 2, 3)):
                    u = i // 4
                    slot = (W_GLU + 2 * m + u) % RING
                    if i % 4 == 0:
                        pe.wait_ge(S.lo_done, W_GLU + 2 * m + u + 1)
                    if m == 0:
                        pe.wait_ge(S.yhi_done, i + 1)
                        pe.wait_ge(S.ylo_done, i + 1)
                    for e in range(2):
                        cols = slice(2 * P * (k % 4) + P * e, 2 * P * (k % 4) + P * e + P)
                        mm = three(pe, ps[:, 2 * (m % 2) + e], w_hi[:, slot, cols], w_lo[:, slot, cols], y_hi[:, k],
                                   y_lo[:, k], i == 0, i == 7)
                    if i % 4 == 3:
                        mm.then_inc(S.w_used, 1)

            def scores(h):
                half = slice(64 * (h % 2), 64 * (h % 2) + 64)
                for i in range(TT):
                    n = P * (i + 1)
                    q = slice(P * i, n)
                    if h:
                        pe.wait_ge(S.exp_done, 4 * (h - 1) + i + 1)
                    else:
                        pe.wait_ge(S.sig_done, 7 + i // 2)
                        pe.wait_ge(S.glu_val, 7 + i // 2)
                    pe.matmul(ps[:, i, 0:n], qn[:, h, q], kn[:, h, 0:n], start=True, stop=False)
                    pe.matmul(ps[:, i, 0:n], qr[half, h // 2, q], k_rot[half, 0:n], start=False, stop=True
                              ).then_inc(S.s_done, 1)

            def transposes(h):
                for i in range(TT):
                    bank, col = PT[i]
                    pe.wait_ge(S.p_done, 4 * h + i + 1)
                    if h:
                        pe.wait_ge(S.pT_evac, 4 * (h - 1) + max(i + 1, 2))
                    for k in range(i + 1):
                        m = pe.transpose(ps[:, bank, col + P * k:col + P * k + P], lat[:, i, P * k:P * k + P], ident)
                    m.then_inc(S.pT_done, 1)

            def values(h):
                pe.wait_ge(S.pT_evac, 4 * h + 4)
                if h:
                    pe.wait_ge(S.o_gated, h)
                for k in range(TT):
                    m = pe.matmul(ps[:, 6, P * k:SEQ], vv[:, k, P * h:P * h + P], pt[:, h % 2, k, P * k:SEQ],
                                  start=k == 0, stop=k == TT - 1)
                m.then_inc(S.o_done, 1)

            pe.wait_ge(S.kr_done, 1)
            pe.wait_ge(S.rope_done, 16)
            scores(0)
            for h in range(1, HEADS):
                scores(h)
                if h >= 2:
                    values(h - 2)
                transposes(h - 1)

            def products(c, u, t, first, last):
                w = W_OUT + 8 * c + u
                for i in range(2):
                    k = 2 * ((u + 4) % 8 if c == 0 else u) + i
                    cols = slice(512 * i, 512 * i + 512)
                    o = ps[:, 4 * (c % 2) + t]
                    tok = slice(P * t, P * t + P)
                    pe.matmul(o, mixed_hi[:, k, tok], w_hi[:, w % 4, cols], start=first and i == 0, stop=False)
                    pe.matmul(o, mixed_hi[:, k, tok], w_lo[:, w % 4, cols], start=False, stop=False)
                    mm = pe.matmul(o, mixed_lo[:, k, tok], w_hi[:, w % 4, cols], start=False, stop=last and i == 1)
                return mm

            for c in range(4):
                if c == 1:
                    pe.wait_ge(S.pT_evac, 4 * HEADS)
                    pe.wait_ge(S.o_gated, HEADS)
                elif c >= 2:
                    pe.wait_ge(S.og_done, 4 * (c - 1))
                for u in range(8 if c < 3 else 4):
                    pe.wait_ge(S.lo_done, W_OUT + 8 * c + u + 1)
                    if c == 0:
                        hi, lo, n = (S.ghi_done, S.glo_done, 2 * u + 2) if u < 4 else (S.ohi_done, S.olo_done, 2 * u - 6)
                        pe.wait_ge(hi, n)
                        pe.wait_ge(lo, n)
                    for t in range(TT):
                        if c == 0 and u == 0:
                            pe.wait_ge(S.exp_done, 4 * (HEADS - 1) + t + 1)
                        mm = products(c, u, t, u == 0, u == 7)
                    mm.then_inc(S.w_used, 1)
                    if c == 0 and u == 0:
                        transposes(HEADS - 1)
                        values(HEADS - 2)
                    if c == 0 and u == 1:
                        values(HEADS - 1)
            for t in range(TT):
                for u in range(4, 8):
                    if t == 0:
                        pe.wait_ge(S.lo_done, W_OUT + 8 * 3 + u + 1)
                    mm = products(3, u, t, False, u == 7)
                mm.then_inc(S.tile_done, 1)


_INS = ['x', 'positions', 'norm_pre', 'norm_post', 'w_in', 'q_norm', 'w_uq', 'kv_norm', 'w_ukv', 'ssm_a_re',
        'ssm_a_im', 'ssm_b_re', 'ssm_b_im', 'ssm_c_re', 'ssm_c_im', 'ssm_d', 'ssm_log_step', 'w_glu', 'w_out']
_MATRICES = ('x', 'w_in', 'w_uq', 'w_ukv', 'ssm_a_re', 'ssm_a_im', 'ssm_b_re', 'ssm_b_im', 'ssm_c_re', 'ssm_c_im',
             'w_glu', 'w_out')


def _constants():
    import numpy as np

    c = np.zeros((P, C_COLS), np.float32)
    c[:, C_ID:C_ID + P] = np.eye(P)
    c[:, C_MASK:C_MASK + P] = np.where(np.tri(P, dtype=bool), 0.0, -3e38)
    r = np.arange(P)
    c[:, C_FREQ] = (np.float32(10000.0) ** (-np.arange(0, ROPE, 2, dtype=np.float32) / np.float32(ROPE)))[r % 32]
    c[:, C_SIGN] = np.where(r // 32 % 2, 1.0, -1.0)
    return c


def kernel(**inputs):
    import numpy as _np
    import concourse.bacc as _bacc
    from concourse import mybir as _mybir
    from concourse.bass_utils import run_bass_kernel_spmd as _run

    nc = _bacc.Bacc("TRN2", target_bir_lowering=False, num_devices=1)
    arrays, aps = {}, {}
    for name in _INS:
        v = _np.ascontiguousarray(inputs[name])
        if name in _MATRICES:
            v = v.reshape(v.shape[1:])
        arrays[f"in_{name}_dram"] = v
    arrays["in_consts_dram"] = _constants()
    for key, v in arrays.items():
        aps[key[3:-5]] = nc.dram_tensor(key, v.shape, _mybir.dt.from_np(v.dtype), kind="ExternalInput").ap()
    out = nc.dram_tensor("out_0_dram", (SEQ, D), F32, kind="ExternalOutput").ap()
    hybrid_layer(nc, aps, out)
    r = _run(nc, [arrays], core_ids=[0])
    return r.results[0]["out_0_dram"].reshape(1, SEQ, D)
```

```python
from contextlib import ExitStack

import concourse.bass as bass
from concourse import mybir

F32 = mybir.dt.float32
F32R = mybir.dt.float32r
I32 = mybir.dt.int32
ALU = mybir.AluOpType
ACT = mybir.ActivationFunctionType
AX = mybir.AxisListType

P = 128
SEQ = 512
D = 2048
HEADS = 8
NOPE = 128
ROPE = 64
QR = 512
KVR = 256
CH = 1024
GC = 16
STATES = 64
PAIRS = CH // GC // 2
L = 8
NQ = SEQ // L
KT = D // P
TT = SEQ // P
EPS = 1e-6
SCALE = 1.0 / float(NOPE + ROPE) ** 0.5
TWO_PI = 6.283185307179586
PI_A, PI_B, PI_C = 6.28125, 0.0019350051879882812, 3.0199159819e-07
ROUND = 12582912.0
PI_SAFE = 3.1415925
HALF_PI = 1.5707963267948966

COL_CKV = QR
COL_KR = QR + KVR
COL_GM = COL_KR + ROPE
COL_U = COL_GM + CH
COL_GS = COL_U + CH

UNIT = 1024
RING = 4
X_SPLIT = 3 * D // 4
GRP = 256
BATCH = 8
NB = PAIRS // BATCH
PADK = (L - 1) * GC + P

N_U, N_GM, N_GS, N_CKV, N_CQ, N_KR = 0, 4, 8, 12, 13, 15
W_KR = 4 * N_KR
W_KN = W_KR + 1
W_V = W_KN + 2
W_Q = W_V + 2
W_ROPE = W_Q + 4
W_GLU = W_ROPE + 2
W_OUT = W_GLU + 16
W_END = W_OUT + 32

C_ID, C_MASK, C_FREQ, C_SIGN, C_COLS = 0, P, 2 * P, 2 * P + 1, 2 * P + 2
(R_ARE, R_AIM, R_STEP, R_ZR, R_ZI, R_ER, R_TH, R_V, R_N, R_R, R_M, R_S, R_C, R_S2, R_NR, R_NI, R_X, R_Y,
 R_DEN, R_FR, R_FI) = range(21)


def hybrid_layer(nc, a, out):
    ctx = ExitStack()
    with ctx:
        def sb(name, shape, dt=F32, scope=ctx):
            return scope.enter_context(nc.sbuf_tensor(name, shape, dt))

        def sem(name):
            return ctx.enter_context(nc.semaphore(name))

        u_dram = nc.dram_tensor("u_scratch", [CH, SEQ], F32, kind="Internal").ap()
        gm_dram = nc.dram_tensor("gate_mla_scratch", [CH, SEQ], F32, kind="Internal").ap()
        gs_dram = nc.dram_tensor("gate_ssm_scratch", [CH, SEQ], F32, kind="Internal").ap()
        y_dram = nc.dram_tensor("y_scratch", [CH, SEQ], F32, kind="Internal").ap()
        taps_dram = nc.dram_tensor("taps_scratch", [NB, 2 * BATCH * GC, PADK], F32, kind="Internal").ap()

        stage = sb("stage", [P, RING, UNIT])
        w_hi = sb("w_hi", [P, RING, UNIT], F32R)
        w_lo = sb("w_lo", [P, RING, UNIT], F32R)
        consts = sb("consts", [P, C_COLS])
        ident = consts[:, C_ID:C_ID + P]
        mask = consts[:, C_MASK:C_MASK + P]
        inv_freq = consts[:, C_FREQ:C_FREQ + 1]
        rope_sign = consts[:, C_SIGN:C_SIGN + 1]
        ones = sb("ones", [P, P])
        eps = sb("eps", [P, 1])
        cos = sb("cos", [P, SEQ])
        sin = sb("sin", [P, SEQ])
        k_rot = sb("k_rot", [P, SEQ])
        lat = sb("lat", [P, 6, SEQ])
        g_lat = sb("g_lat", [P, 6])
        small = sb("small", [P, 3, TT])
        soft = sb("soft", [P, 3, TT])
        fin = sb("fin", [P, TT, 7])

        part1 = ExitStack()
        h_hi = sb("h_hi", [P, KT, SEQ], F32R, part1)
        h_lo = sb("h_lo", [P, KT, SEQ], F32R, part1)
        ev = sb("ev", [P, 2, SEQ], F32, part1)
        prm = sb("prm", [P, 21, PAIRS], F32, part1)
        powers = sb("powers", [P, L + 1, 3, PAIRS], F32, part1)
        bbar = sb("bbar", [P, 2, PAIRS, GC], F32, part1)
        ct = sb("ct", [P, 2, PAIRS, GC], F32, part1)
        chunk_a = sb("chunk_a", [P, 2, 2, PAIRS], F32, part1)
        araw = sb("araw", [PAIRS, 3, P], F32, part1)
        lsraw = sb("lsraw", [PAIRS, 2], F32, part1)
        draw = sb("draw", [CH // P, P], F32, part1)
        dsk = sb("dsk", [P, CH // P], F32, part1)
        part0 = ExitStack()
        xt = sb("xt", [P, TT, D], F32, part0)
        g_pre = sb("g_pre", [P, D], F32, part0)
        g_row = sb("g_row", [1, D], F32, part0)
        junk = w_lo[:, 2:4].rearrange("p s n -> p (s n)")
        part0.close()
        ssm = ExitStack()
        raws = ExitStack()
        braw = sb("braw", [P, 2, PAIRS, GC], F32, raws)
        craw = sb("craw", [P, 2, BATCH, STATES], F32, raws)
        ang = sb("ang", [P, 4, SEQ], F32, raws)
        pos = sb("pos", [P, SEQ], I32, raws)
        raws.close()
        states = sb("states", [P, NQ + 1, 2, PAIRS], F32, ssm)
        cw = sb("cw", [P, BATCH, 2, L + 1, GC], F32, ssm)
        tmp = sb("tmp", [P, 2, BATCH, L + 1, GC], F32, ssm)
        mats = sb("mats", [P, 2 * BATCH, P], F32, ssm)
        u2 = sb("u2", [P, 2 * BATCH, NQ], F32, ssm)
        bd = sb("bd", [P, BATCH, 2, 2 * GC], F32, ssm)
        sw = sb("sw", [P, 2, 2, PAIRS], F32, ssm)
        st = sb("st", [P, 2, PAIRS], F32, ssm)
        dm = sb("dm", [P, 2, GC], F32, ssm)
        same_ch = sb("same_ch", [P, GC], F32, ssm)
        zeros = sb("zeros", [P, PADK - P], F32, ssm)
        yb = sb("yb", [P, 2 * BATCH, NQ], F32, ssm)
        ssm.close()
        taps = tmp.rearrange("p a b c d -> p (a b c d)")[:, 0:2 * P].rearrange("p (s n) -> p s n", s=2)
        part1.close()

        part2 = ExitStack()
        mixed_hi = sb("mixed_hi", [P, KT, SEQ], F32R, part2)
        mixed_lo = sb("mixed_lo", [P, KT, SEQ], F32R, part2)
        LAT = (10, 11, 12, 13, 8, 9)
        y_hi, y_lo = mixed_hi[:, 0:8], mixed_lo[:, 0:8]
        part3 = ExitStack()
        glu_t = sb("glu_t", [P, 2, SEQ], F32, part3)
        kn = sb("kn", [P, HEADS, SEQ], F32, part3)
        vv = sb("vv", [P, TT, CH], F32, part3)
        qn = sb("qn", [P, HEADS, SEQ], F32, part3)
        qr = sb("qr", [P, HEADS // 2, SEQ], F32, part3)
        glu_in = ExitStack()
        yraw = sb("yraw", [P, 8, SEQ], F32, glu_in)
        glu_in.close()
        pt = sb("pt", [P, 2, TT, SEQ], F32, part3)
        part3.close()
        og = sb("og", [P, TT, D], F32, part2)
        xr = sb("xr", [P, TT, D], F32, part2)
        g_post = sb("g_post", [P, D], F32, part2)
        part2.close()

        ps = ctx.enter_context(nc.psum_tensor("ps", [P, 8, 512], F32))

        class Sems:
            pass

        S = Sems()
        S.consts_in = sem("consts_in")
        S.prm_in = sem("prm_in")
        S.bc_in = sem("bc_in")
        S.pos_in = sem("pos_in")
        S.hi_done = sem("hi_done")
        S.lo_done = sem("lo_done")
        S.w_used = sem("w_used")
        S.const_done = sem("const_done")
        S.x_sq = sem("x_sq")
        S.cwi_part = sem("cwi_part")
        S.kr_first = sem("kr_first")
        S.g_row_in = sem("g_row_in")
        S.g_bank = sem("g_bank")
        S.g_pre_done = sem("g_pre_done")
        S.x_tail = sem("x_tail")
        S.x_scaled = sem("x_scaled")
        S.tile_done = sem("tile_done")
        S.x_rms = sem("x_rms")
        S.x_rinv = sem("x_rinv")
        S.x_normed = sem("x_normed")
        S.xT_done = sem("xT_done")
        S.xhi_done = sem("xhi_done")
        S.xlo_done = sem("xlo_done")
        S.prm_links = sem("prm_links")
        S.prmT_done = sem("prmT_done")
        S.ls_ready = sem("ls_ready")
        S.step_done = sem("step_done")
        S.z_ready = sem("z_ready")
        S.z_acts = sem("z_acts")
        S.angle_ready = sem("angle_ready")
        S.trig_done = sem("trig_done")
        S.rope_angle = sem("rope_angle")
        S.rope_trig = sem("rope_trig")
        S.ctT_done = sem("ctT_done")
        S.b_done = sem("b_done")
        S.proj_evac = sem("proj_evac")
        S.ev_stored = sem("ev_stored")
        S.cwr_step = sem("cwr_step")
        S.cwi_step = sem("cwi_step")
        S.bxT_done = sem("bxT_done")
        S.bx_ready = sem("bx_ready")
        S.u2_in = sem("u2_in")
        S.vin_done = sem("vin_done")
        S.vin_evac = sem("vin_evac")
        S.scan_step = sem("scan_step")
        S.bd_done = sem("bd_done")
        S.taps_done = sem("taps_done")
        S.swap_step = sem("swap_step")
        S.taps_step = sem("taps_step")
        S.taps_ready = sem("taps_ready")
        S.taps_stored = sem("taps_stored")
        S.zero_stored = sem("zero_stored")
        S.toep_in = sem("toep_in")
        S.y_done = sem("y_done")
        S.y_ready = sem("y_ready")
        S.y_stored = sem("y_stored")
        S.lat_sq = sem("lat_sq")
        S.lat_sum = sem("lat_sum")
        S.lat_ssq = sem("lat_ssq")
        S.lat_rms = sem("lat_rms")
        S.lat_link = sem("lat_link")
        S.lat_normed = sem("lat_normed")
        S.lat_hi_done = sem("lat_hi_done")
        S.lat_lo_done = sem("lat_lo_done")
        S.kr_evac = sem("kr_evac")
        S.kr_link = sem("kr_link")
        S.kr_done = sem("kr_done")
        S.head_done = sem("head_done")
        S.head_evac = sem("head_evac")
        S.rope_mul = sem("rope_mul")
        S.rope_done = sem("rope_done")
        S.yhi_done = sem("yhi_done")
        S.ylo_done = sem("ylo_done")
        S.sig_done = sem("sig_done")
        S.glu_val = sem("glu_val")
        S.glu_prod = sem("glu_prod")
        S.ghi_done = sem("ghi_done")
        S.glo_done = sem("glo_done")
        S.s_done = sem("s_done")
        S.s_link = sem("s_link")
        S.s_max = sem("s_max")
        S.exp_done = sem("exp_done")
        S.den_done = sem("den_done")
        S.p_done = sem("p_done")
        S.pT_done = sem("pT_done")
        S.pT_evac = sem("pT_evac")
        S.o_done = sem("o_done")
        S.o_gated = sem("o_gated")
        S.ohi_done = sem("ohi_done")
        S.olo_done = sem("olo_done")
        S.out_sq = sem("out_sq")
        S.og_done = sem("og_done")
        S.fin_sum = sem("fin_sum")
        S.fin_root = sem("fin_root")
        S.fin_inv = sem("fin_inv")
        S.fin_done = sem("fin_done")
        S.xr_in = sem("xr_in")
        S.g_post_in = sem("g_post_in")
        S.out_stored = sem("out_stored")
        x_in = [sem(f"x_in{t}") for t in range(TT)]
        w_in = [sem(f"w_in{s}") for s in range(RING)]
        yraw_in = [sem(f"yraw_in{s}") for s in range(2)]
        gs_in = [sem(f"gs_in{s}") for s in range(2)]
        gm_in = [sem(f"gm_in{s}") for s in range(2)]

        XB = (4, 0, 4, 4)
        PT = ((4, 0), (4, P), (5, 0), (7, 0))

        FIN_PARTS = [(t, 0, D) for t in range(TT - 1)] + [(TT - 1, c0, c1) for c0, c1 in ((0, 512), (512, 1280), (1280, D))]

        block = ctx.enter_context(nc.Block())

        def unit_in(w, col):
            u = w % 4
            return a["w_in"][u * 512:(u + 1) * 512, bass.ds(col, GRP)].rearrange("(k p) n -> p k n", p=P)

        def pieces(w):
            return 1 if w < W_KN or w >= W_OUT else 4 if W_ROPE <= w < W_GLU else 2

        def loaded(w):
            return 16 * sum(pieces(x) for x in range(w % RING, w + 1, RING))

        def tiles_of(w):
            return 4 if w < W_Q else 2

        def used(w):
            if W_KN <= w < W_GLU:
                return S.head_done, sum(tiles_of(x) for x in range(W_KN, w + 1))
            return S.w_used, w + 1 - (W_GLU - W_KN if w >= W_GLU else 0)

        def load(sp, slot, src, turn, first=False):
            if not first:
                sp.wait_ge(S.lo_done, 4 * turn + (slot - 3))
            sp.dma_start(stage[:, slot, :].rearrange("p (k n) -> p k n", k=src.shape[1]), src
                         ).then_inc(w_in[slot], 16)

        def split_hi(act, slot, turn):
            act.wait_ge(w_in[slot], 16 * turn + 16)
            act.wait_ge(S.w_used, 4 * turn + (slot - 3))
            round_unit(act, slot)

        def split_hi_at(act, w):
            act.wait_ge(w_in[w % RING], loaded(w))
            if w >= RING:
                act.wait_ge(*used(w - RING))
            round_unit(act, w % RING)

        def round_unit(act, slot):
            act.activation(w_hi[:, slot, :], stage[:, slot, :], ACT.Copy).then_inc(S.hi_done, 1)

        def split_lo(pool, slot, turn):
            pool.wait_ge(S.hi_done, 4 * turn + (slot + 1))
            pool.tensor_tensor(w_lo[:, slot, :], stage[:, slot, :], w_hi[:, slot, :].bitcast(F32),
                               ALU.subtract).then_inc(S.lo_done, 1)

        def split_lo_at(pool, w):
            split_lo(pool, w % RING, w // RING)

        def three(pe, o, s_hi, s_lo, m_hi, m_lo, start, stop):
            pe.matmul(o, s_hi, m_hi, start=start, stop=False)
            pe.matmul(o, s_hi, m_lo, start=False, stop=False)
            return pe.matmul(o, s_lo, m_hi, start=False, stop=stop)

        def x_rows(ap, t):
            return ap.rearrange("(q t j) d -> t j q d", t=TT, j=2)[t]

        def natural(ap):
            return ap.rearrange("p (q j) -> p j q", j=L)

        def steps(ap):
            return ap.rearrange("p (j q) -> p j q", j=L)

        nonc = nc.allow_non_contiguous_dma(reason="rows of one SSM group")
        ctx.enter_context(nonc)

        @block.sync
        def _(sp):
            def load_x(t):
                sp.dma_start(xt[:, t, :], x_rows(a["x"], t)).then_inc(x_in[t], 16)

            def load_w(w, col):
                load(sp, w % 4, unit_in(w, col), w // 4, first=w < 4)

            sp.dma_start(g_row[:, :], a["norm_pre"]).then_inc(S.g_row_in, 16)
            load_x(0)
            sp.dma_start(consts[:, :], a["consts"]).then_inc(S.consts_in, 16)
            load_x(1)
            load_x(2)
            load_w(0, COL_U)
            load_x(3)
            for w in range(1, 4):
                load_w(w, COL_U)
            sp.dma_start(araw[:, 0, :], a["ssm_a_re"].rearrange("(g h) n -> g (h n)", h=2)).then_inc(S.prm_in, 16)
            sp.dma_start(araw[:, 1, :], a["ssm_a_im"].rearrange("(g h) n -> g (h n)", h=2)).then_inc(S.prm_in, 16)
            sp.dma_start(lsraw[:, :], a["ssm_log_step"].rearrange("a (g h) -> (a g) h", h=2)).then_inc(S.prm_in, 16)
            sp.dma_start(draw[:, :], a["ssm_d"].rearrange("a (g c) -> (a g) c", c=P)).then_inc(S.prm_in, 16)
            for i, (g, n) in enumerate((("q_norm", 4), ("kv_norm", 2))):
                sp.dma_start(g_lat[:, 4 * i:4 * i + n], a[g].rearrange("a (k p) -> p (a k)", p=P)).then_inc(S.prm_in, 16)
            sp.wait_ge(S.xT_done, 16)
            for i, n in enumerate(("ssm_b_re", "ssm_b_im")):
                sp.dma_start(braw[:, i], a[n].rearrange("(g h) n c -> (h n) g c", h=2)).then_inc(S.bc_in, 16)
            for i, n in enumerate(("ssm_c_re", "ssm_c_im")):
                sp.dma_start(craw[:, i], a[n].rearrange("(b g) c n -> (g c) b n", b=BATCH)).then_inc(S.bc_in, 16)
            sp.dma_start(pos[:, :], a["positions"].to_broadcast([P, SEQ])).then_inc(S.pos_in, 16)
            for w in range(4, 8):
                load_w(w, COL_U + GRP)

            def load_u2(b):
                for r in range(L):
                    src = u_dram[bass.ds(b * (2 * BATCH * GC), 2 * BATCH * GC), (L - 1 - r) * NQ:(L - r) * NQ]
                    sp.dma_start(u2[GC * r:GC * r + GC], src.rearrange("(g c) q -> c g q", c=GC)).then_inc(S.u2_in, 16)

            with sp.Fori(0, 2) as i:
                for par in range(2):
                    for u in range(4):
                        col = (COL_GM - COL_U - 2 * GRP) * i + (COL_U + 2 * GRP + par * GRP)
                        load(sp, u, unit_in(u, col), 2 * i + (2 + par))
            sp.wait_ge(S.ev_stored, 16 * 4)
            with sp.Fori(0, 2) as i:
                for par in range(2):
                    sp.wait_ge(S.vin_evac, 4 * i + (2 * par + 1))
                    load_u2(2 * i + par)
                    for u in range(4):
                        col = (COL_GS - COL_GM - 2 * GRP) * i + (COL_GM + 2 * GRP + par * GRP)
                        load(sp, u, unit_in(u, col), 2 * i + (6 + par))
            sp.wait_ge(S.vin_done, NB)
            load_u2(0)
            sp.dma_start(taps_dram[:, :, 0:PADK - P].rearrange("b (s p) n -> p (b s) n", p=P),
                         zeros[:, :].unsqueeze(1).to_broadcast([P, CH // P, PADK - P])).then_inc(S.zero_stored, 16)
            with sp.Fori(0, 2) as i:
                for par in range(2):
                    for u in range(4):
                        first, then = COL_GS + 2 * GRP + par * GRP, (1 - par) * COL_CKV
                        col = (then - first) * i + first
                        load(sp, u, unit_in(u, col), 2 * i + (10 + par))

            def load_toeplitz(b, meanwhile=None):
                sp.wait_ge(S.taps_ready, 2 * b + 2)
                sp.dma_start(taps_dram[b, :, PADK - P:PADK].rearrange("(s p) n -> p s n", p=P), taps
                             ).then_inc(S.taps_stored, 16)
                if b == 0:
                    sp.wait_ge(S.zero_stored, 16)
                    sp.wait_ge(S.vin_done, NB)
                else:
                    sp.wait_ge(S.y_done, b)
                    meanwhile()
                sp.wait_ge(S.taps_stored, 16 * b + 16)
                for r in range(L):
                    src = taps_dram[b, :, GC * r:GC * r + P].rearrange("(g c) n -> c g n", c=GC)
                    sp.dma_start(mats[GC * r:GC * r + GC], src).then_inc(S.toep_in, 16)

            def store_y(b):
                sp.wait_ge(S.y_ready, 2 * b + 2)
                dst = y_dram[2 * BATCH * GC * b:2 * BATCH * GC * (b + 1)].rearrange("(g c) (j q) -> j c g q", c=GC, j=L)
                for j in range(L):
                    sp.dma_start(dst[j], yb[GC * j:GC * j + GC]).then_inc(S.y_stored, 16)

            def unit_pieces(w):
                slot = stage[:, w % RING, :]
                if w < W_KN:
                    src = unit_in(w, GRP) if w < W_KR else a["w_in"][:, COL_KR:COL_GM].rearrange(
                        "(k p) n -> p k n", p=P)
                    return [(slot.rearrange("p (k n) -> p k n", k=src.shape[1]), src)]
                if w < W_Q:
                    v, i = divmod(w - W_KN, 2)
                    src = a["w_ukv"].rearrange("(k p) (h e n) -> k e p h n", p=P, e=2, n=NOPE)
                    dst = slot.rearrange("p (k h n) -> p k h n", k=2, n=NOPE)
                    return [(dst[:, k], src[k, v][:, 4 * i:4 * i + 4]) for k in range(2)]
                if w < W_GLU:
                    src = a["w_uq"].rearrange("(k p) (h n) -> p k h n", p=P, h=HEADS)
                    if w < W_ROPE:
                        i = w - W_Q
                        dst = slot.rearrange("p (k h n) -> p k h n", k=4, n=NOPE)
                        return [(dst[:, :, h], src[:, :, 2 * i + h, 0:NOPE]) for h in range(2)]
                    dst = slot.rearrange("p (k h n) -> p k h n", k=4, n=32)
                    c = NOPE + 32 * (w - W_ROPE)
                    return [(dst[:, k], src[:, k, :, c:c + 32]) for k in range(4)]
                if w < W_OUT:
                    m, u = divmod(w - W_GLU, 2)
                    src = a["w_glu"].rearrange("(k p) n -> p k n", p=P)[:, 4 * (1 - u):4 * (1 - u) + 4]
                    dst = slot.rearrange("p (k e n) -> p k e n", k=4, e=2)
                    return [(dst[:, :, e], src[:, :, CH * e + P * m:CH * e + P * m + P]) for e in range(2)]
                c, u = divmod(w - W_OUT, 8)
                u = (u + 4) % 8 if c == 0 else u
                return [(slot.rearrange("p (k n) -> p k n", k=2),
                         a["w_out"].rearrange("(k p) n -> p k n", p=P)[:, 2 * u:2 * u + 2, 512 * c:512 * c + 512])]

            def load_gs(m):
                sp.wait_ge(S.glu_prod, m - 1) if m >= 2 else None
                sp.dma_start(lat[:, 4 + m % 2], gs_dram[P * m:P * m + P]).then_inc(gs_in[m % 2], 16)

            def load_gm(h):
                if h < 2:
                    sp.wait_ge(S.glu_prod, 7 + h)
                else:
                    sp.wait_ge(S.o_gated, h - 1)
                sp.dma_start(lat[:, 4 + h % 2], gm_dram[P * h:P * h + P]).then_inc(gm_in[h % 2], 16)

            beside = {
                56: lambda: load_toeplitz(0),
                59: lambda: (load_toeplitz(1, lambda: load_u2(1)), store_y(0)),
                63: lambda: (load_toeplitz(2, lambda: load_u2(2)), store_y(1)),
                67: lambda: (load_toeplitz(3, lambda: load_u2(3)), store_y(2)),
                71: lambda: store_y(3),
                73: lambda: (sp.wait_ge(S.y_stored, 16 * L * NB),
                             sp.dma_start(yraw[:, 4:8], y_dram[4 * P:8 * P].rearrange("(k p) n -> p k n", p=P)
                                          ).then_inc(yraw_in[0], 16),
                             sp.dma_start(yraw[:, 0:4], y_dram[0:4 * P].rearrange("(k p) n -> p k n", p=P)
                                          ).then_inc(yraw_in[1], 16)),
                75: lambda: (sp.wait_ge(S.lat_lo_done, 6), sp.wait_ge(S.ev_stored, 16 * 12), load_gs(0), load_gs(1)),
                98: lambda: (sp.wait_ge(S.o_gated, HEADS), sp.wait_ge(S.o_done, HEADS),
                             sp.dma_start(g_post[:, :], a["norm_post"].to_broadcast([P, D])).then_inc(S.g_post_in, 16),
                             [sp.dma_start(xr[:, t, :], x_rows(a["x"], t)).then_inc(S.xr_in, 16) for t in range(TT)]),
            }
            for m in range(2, 8):
                beside[W_GLU + 2 * m + 3] = lambda m=m: load_gs(m)
            beside[W_OUT + RING] = lambda: [load_gm(h) for h in range(HEADS)]
            for w in range(4 * 14, W_END):
                if w in beside:
                    beside[w]()
                sp.wait_ge(S.lo_done, w - 3)
                for dst, src in unit_pieces(w):
                    sp.dma_start(dst, src).then_inc(w_in[w % RING], 16)
            for n, (t, c0, c1) in enumerate(FIN_PARTS):
                sp.wait_ge(S.fin_done, n + 1)
                sp.dma_start(x_rows(out, t)[:, :, c0:c1], og[:, t, c0:c1]
                             ).then_inc(S.out_stored, 16)
            sp.wait_ge(S.out_stored, 16 * len(FIN_PARTS))

        @block.scalar
        def _(act):
            def x_tile(t):
                for k in range(4):
                    act.wait_ge(S.xT_done, 4 * t + k + 1)
                    act.activation(h_hi[:, 4 * k:4 * k + 4, P * t:P * t + P],
                                   ps[:, XB[t] + k].rearrange("p (k n) -> p k n", k=4),
                                   ACT.Copy).then_inc(S.xhi_done, 1)

            act.wait_ge(S.const_done, 2)
            act.activation(fin[:, 0, 6:7], eps[:, :], ACT.Sqrt)
            def root_mean_square(t):
                act.wait_ge(x_in[t], 16)
                if t:
                    act.wait_ge(S.x_sq, t)
                act.activation(junk, xt[:, t, :], ACT.Square, accum_out=small[:, 0, t:t + 1]).then_inc(S.x_sq, 1)
                act.wait_ge(S.x_sq, t + 1)
                act.activation(small[:, 1, t:t + 1], small[:, 0, t:t + 1], ACT.Sqrt, bias=eps[:, :],
                               scale=1.0 / D).then_inc(S.x_rms, 1)

            root_mean_square(0)
            root_mean_square(1)
            x_tile(0)
            split_hi_at(act, 0)
            x_tile(1)
            root_mean_square(2)
            split_hi_at(act, 1)
            root_mean_square(3)
            x_tile(2)
            split_hi_at(act, 2)
            split_hi_at(act, 3)
            x_tile(3)
            act.wait_ge(S.ls_ready, 2)
            act.activation(prm[:, R_STEP], prm[:, R_STEP], ACT.Exp).then_inc(S.step_done, 1)
            act.wait_ge(S.z_ready, 2)
            act.activation(prm[:, R_ER], prm[:, R_ZR], ACT.Exp).then_inc(S.z_acts, 1)
            act.activation(prm[:, R_TH], prm[:, R_ZR], ACT.Tanh, scale=0.5).then_inc(S.z_acts, 1)
            act.wait_ge(S.angle_ready, 1)
            act.activation(prm[:, R_S], prm[:, R_R], ACT.Sin).then_inc(S.trig_done, 1)
            act.activation(prm[:, R_C], prm[:, R_M], ACT.Sin).then_inc(S.trig_done, 1)

            def evacuate(n, par, func, dram, row):
                act.wait_ge(S.w_used, 4 * n + 4)
                for m in range(2):
                    act.activation(ev[:, m], ps[:, 2 * par + m], func).then_inc(S.proj_evac, 1)
                act.wait_ge(S.proj_evac, 2 * n + 2)
                act.dma_start(dram[bass.ds(row, GRP)].rearrange("(m p) n -> p m n", p=P), ev[:, :, :]
                              ).then_inc(S.ev_stored, 16)
                act.wait_ge(S.ev_stored, 16 * n + 16)

            for n in range(4):
                for u in range(4):
                    split_hi(act, u, n + 1)
                if n == 0:
                    act.wait_ge(S.rope_angle, 1)
                    act.activation(sin[:, :], ang[:, 2], ACT.Sin).then_inc(S.rope_trig, 1)
                    act.activation(cos[:, :], ang[:, 3], ACT.Sin).then_inc(S.rope_trig, 1)
                evacuate(n, n % 2, ACT.Copy, u_dram, GRP * n)
            for n0, func, dram in ((N_GM, ACT.Silu, gm_dram), (N_GS, ACT.Silu, gs_dram)):
                with act.Fori(0, 2) as i:
                    for par in range(2):
                        for u in range(4):
                            split_hi(act, u, 2 * i + (n0 + par + 1))
                        evacuate(2 * i + (n0 + par), par, func, dram, (2 * GRP) * i + par * GRP)

            def gelu(b):
                act.wait_ge(S.y_done, b + 1)
                if b:
                    act.wait_ge(S.y_stored, 16 * L * b)
                for m in range(2):
                    act.activation(yb[:, :, :].rearrange("p (g h) q -> p h g q", h=2)[:, m],
                                   ps[:, 6 + m].rearrange("p (g q) -> p g q", q=NQ),
                                   ACT.Gelu_apprx_tanh).then_inc(S.y_ready, 1)

            def latent(n, first, consumed):
                act.wait_ge(S.w_used, 4 * n + 4)
                act.wait_ge(*consumed)
                for m in range(2):
                    bank = ps[:, 2 * (n % 2) + m]
                    act.activation(natural(ev[:, m]), steps(bank), ACT.Square).then_inc(S.lat_sq, 1)
                    act.activation(natural(lat[:, first + m]), steps(bank), ACT.Copy).then_inc(S.proj_evac, 1)

            def root_of(i, n):
                act.wait_ge(S.lat_ssq, i + 1)
                act.activation(k_rot[:, :], ps[:, 4 + i], ACT.Sqrt, bias=eps[:, :], scale=1.0 / n
                               ).then_inc(S.lat_rms, 1)

            for n, first, consumed in ((12, 4, (S.ev_stored, 16 * 12)), (13, 0, (S.lat_sum, 1)),
                                       (14, 2, (S.lat_sum, 2))):
                for w in (4 * n + 4, 4 * n + 5):
                    split_hi_at(act, w)
                if n == 13:
                    root_of(0, KVR)
                gelu(n - 12)
                for w in (4 * n + 6, 4 * n + 7):
                    split_hi_at(act, w)
                latent(n, first, consumed)

            def lat_tile(k):
                act.activation(mixed_hi[:, LAT[k]], lat[:, k], ACT.Copy).then_inc(S.lat_hi_done, 1)

            act.wait_ge(S.kr_first, 1)
            act.wait_ge(S.lat_normed, 2)
            for k in (4, 5):
                lat_tile(k)
            split_hi_at(act, 64)
            root_of(1, QR)

            def head_tile(j):
                act.wait_ge(S.head_done, j + 1)
                i = j % 8
                src = ps[:, j % 4]
                if j < 8:
                    act.activation(kn[:, i], src, ACT.Copy).then_inc(S.head_evac, 1)
                elif j < 16:
                    act.activation(vv[:, i % 4, 512 * (i // 4):512 * (i // 4) + 512], src, ACT.Copy
                                   ).then_inc(S.head_evac, 1)
                else:
                    act.activation(qn[:, i], src, ACT.Copy, scale=SCALE).then_inc(S.head_evac, 1)

            def y_tile(k):
                act.wait_ge(yraw_in[0 if k > 3 else 1], 16)
                act.activation(y_hi[:, k], yraw[:, k], ACT.Copy).then_inc(S.yhi_done, 1)

            tiles = iter(range(24))
            act.wait_ge(S.taps_ready, 8)
            y_tiles = {W_Q + 2: (6, 7), W_Q + 3: (4, 5), W_ROPE: (0, 1), W_ROPE + 1: (2, 3)}
            for w in range(W_KN, W_GLU):
                if w == W_V:
                    gelu(3)
                if w < W_ROPE:
                    for _ in range(4 if w < W_Q else 2):
                        head_tile(next(tiles))
                split_hi_at(act, w + 4)
                if w == W_KN:
                    act.wait_ge(S.lat_normed, 6)
                    for k in range(4):
                        lat_tile(k)
                for k in y_tiles.get(w, ()):
                    y_tile(k)
            act.wait_ge(S.kr_done, 1)

            def glu(m):
                split_hi_at(act, W_GLU + 4 + 2 * m)
                act.wait_ge(*used(W_GLU + 2 * m + 1))
                if m:
                    act.wait_ge(S.glu_val, m)
                act.activation(glu_t[:, 0], ps[:, 4 + 2 * (m % 2) + 1], ACT.Sigmoid).then_inc(S.sig_done, 1)
                if m == 7:
                    act.activation(fin[:, 0, 6:7], eps[:, :], ACT.Exp)
                split_hi_at(act, W_GLU + 5 + 2 * m)
                act.wait_ge(S.glu_prod, m + 1)
                act.activation(mixed_hi[:, 8 + m], glu_t[:, 1], ACT.Copy).then_inc(S.ghi_done, 1)

            for m in range(7):
                glu(m)

            def softmax_exp(h, i):
                n = P * (i + 1)
                act.wait_ge(S.s_max, 4 * h + i + 1)
                if h:
                    act.wait_ge(S.pT_done, 4 * (h - 1) + i + 1)
                act.activation(lat[:, i, 0:n], ps[:, i, 0:n], ACT.Exp, bias=soft[:, 0, i:i + 1],
                               accum_out=soft[:, 1, i:i + 1]).then_inc(S.exp_done, 1)

            def transposed(h, i):
                act.wait_ge(S.pT_done, 4 * h + max(i + 1, 2))
                if h >= 2:
                    act.wait_ge(S.o_done, h - 1)
                bank, col = PT[i]
                act.activation(pt[:, h % 2, 0:i + 1, P * i:P * i + P],
                               ps[:, bank, col:col + P * (i + 1)].rearrange("p (k n) -> p k n", n=P),
                               ACT.Copy).then_inc(S.pT_evac, 1)

            def gated(h):
                act.wait_ge(S.o_gated, h + 1)
                act.activation(mixed_hi[:, h], glu_t[:, h % 2], ACT.Copy).then_inc(S.ohi_done, 1)

            for i in range(TT):
                softmax_exp(0, i)
            glu(7)
            for h in range(1, HEADS + 1):
                for tiles_now in ((0, 1), (2,), (3,)):
                    if h < HEADS:
                        for i in tiles_now:
                            softmax_exp(h, i)
                    for i in tiles_now:
                        transposed(h - 1, i)
                if h >= 2:
                    gated(h - 2)
            split_hi_at(act, W_OUT + 4)
            gated(HEADS - 1)

            def out_squares(c):
                if c < 3:
                    act.wait_ge(*used(W_OUT + 8 * c + 7))
                for t in range(TT):
                    if c == 3:
                        act.wait_ge(S.tile_done, t + 1)
                    if 4 * c + t:
                        act.wait_ge(S.out_sq, 4 * c + t)
                    act.activation(lat[:, 0], ps[:, 4 * (c % 2) + t], ACT.Square, accum_out=fin[:, t, c:c + 1]
                                   ).then_inc(S.out_sq, 1)
                    if c == 3:
                        act.wait_ge(S.fin_sum, 2)
                        act.wait_ge(S.out_sq, 4 * c + t + 1)
                        act.activation(fin[:, t, 5:6], fin[:, t, 3:4], ACT.Sqrt, bias=fin[:, t, 4:5], scale=1.0 / D
                                       ).then_inc(S.fin_root, 1)

            for c in range(4):
                for w in range(W_OUT + 8 * c + (4 if c else 5), min(W_OUT + 8 * c + 12, W_END)):
                    split_hi_at(act, w)
                out_squares(c)
        def weights_view(x, b, ri, n):
            v = x[:, 0:n, ri, bass.ds(b * BATCH, BATCH)].rearrange("p k g -> p g k")
            return v.unsqueeze(3).to_broadcast([P, BATCH, n, GC])

        def table_view(x, b, ri, n):
            return x[:, ri, bass.ds(b * BATCH, BATCH)].unsqueeze(2).to_broadcast([P, BATCH, n, GC])

        def weights_real(v, table, b, n, count, sign, free=None):
            v.tensor_tensor(tmp[:, 0, :, 0:n], weights_view(powers, b, 1, n), table_view(table, b, 1, n),
                            ALU.mult).then_inc(S.cwr_step, 1)
            if free:
                free()
            v.tensor_tensor(cw[:, :, 1, 0:n], weights_view(powers, b, 1 if sign > 0 else 2, n),
                            table_view(table, b, 0, n), ALU.mult).then_inc(S.cwi_part, 1)
            v.tensor_tensor(cw[:, :, 0, 0:n], weights_view(powers, b, 0, n), table_view(table, b, 0, n),
                            ALU.mult).then_inc(S.cwr_step, 1)
            v.wait_ge(S.cwr_step, count + 2)
            v.tensor_tensor(cw[:, :, 0, 0:n], cw[:, :, 0, 0:n], tmp[:, 0, :, 0:n], ALU.subtract
                            ).then_inc(S.cwr_step, 1)

        def weights_imag(pool, table, b, n, turn, sign):
            pool.tensor_tensor(tmp[:, 1, :, 0:n], weights_view(powers, b, 0, n), table_view(table, b, 1, n),
                               ALU.mult).then_inc(S.cwi_step, 1)
            pool.wait_ge(S.cwi_step, 2 * turn + 1)
            pool.wait_ge(S.cwi_part, turn + 1)
            pool.tensor_tensor(cw[:, :, 1, 0:n], cw[:, :, 1, 0:n], tmp[:, 1, :, 0:n],
                               ALU.add if sign > 0 else ALU.subtract).then_inc(S.cwi_step, 1)

        @block.gpsimd
        def _(pool):
            pool.wait_ge(S.g_pre_done, 4)
            for t in range(2):
                tail = xt[:, t, X_SPLIT:D]
                pool.wait_ge(x_in[t], 16)
                pool.wait_ge(S.x_sq, t + 1)
                pool.tensor_tensor(tail, tail, g_pre[:, X_SPLIT:D], ALU.mult).then_inc(S.x_scaled, 1)
                pool.wait_ge(S.x_scaled, t + 1)
                pool.wait_ge(S.x_rinv, t + 1)
                pool.tensor_tensor(tail, tail, small[:, 2, t:t + 1].to_broadcast([P, D - X_SPLIT]), ALU.mult
                                   ).then_inc(S.x_tail, 1)
            for w in range(RING):
                split_lo(pool, w, 0)
            with pool.Fori(0, 2) as i:
                for par in range(2):
                    for u in range(4):
                        split_lo(pool, u, 2 * i + (par + 1))
            pool.wait_ge(S.b_done, 1)
            with pool.Fori(0, 2) as i:
                for par in range(2):
                    weights_imag(pool, bbar, 2 * i + par, L, 2 * i + par, 1)
                    for u in range(4):
                        split_lo(pool, u, 2 * i + (N_GM + par + 1))
                    pool.wait_ge(S.bxT_done, 8 * i + (4 * par + 4))

            weights_imag(pool, ct, 0, L + 1, NB, -1)
            with pool.Fori(0, 2) as i:
                for par in range(2):
                    for u in range(4):
                        split_lo(pool, u, 2 * i + (N_GS + par + 1))

            def add(o, x, y):
                pool.tensor_tensor(o, x, y, ALU.add).then_inc(S.lat_sum, 1)

            for n in (12, 13, 14):
                b = n - 11
                for w in (4 * n + 4, 4 * n + 5):
                    split_lo_at(pool, w)
                pool.wait_ge(S.swap_step, 6 * b)
                weights_imag(pool, ct, b, L + 1, NB + b, -1)
                for w in (4 * n + 6, 4 * n + 7):
                    split_lo_at(pool, w)
                pool.wait_ge(S.lat_sq, 2 * (n - 11))
                if n == 12:
                    add(k_rot[:, :], ev[:, 0], ev[:, 1])
                elif n == 13:
                    pool.wait_ge(S.lat_normed, 2)
                    add(k_rot[:, :], ev[:, 0], ev[:, 1])
                else:
                    add(k_rot[:, :], k_rot[:, :], ev[:, 0])
                    pool.wait_ge(S.lat_sum, 3)
                    add(k_rot[:, :], k_rot[:, :], ev[:, 1])
            split_lo_at(pool, 64)
            for w in range(W_KN, W_GLU):
                split_lo_at(pool, w + 4)
            for m in range(8):
                for w in (W_GLU + 4 + 2 * m, W_GLU + 5 + 2 * m):
                    split_lo_at(pool, w)
                pool.wait_ge(S.ghi_done, m + 1)
                pool.tensor_tensor(mixed_lo[:, 8 + m], glu_t[:, 1], mixed_hi[:, 8 + m].bitcast(F32), ALU.subtract
                                   ).then_inc(S.glo_done, 1)
            for h in range(HEADS):
                if h == HEADS - 1:
                    split_lo_at(pool, W_OUT + 4)
                pool.wait_ge(S.ohi_done, h + 1)
                pool.tensor_tensor(mixed_lo[:, h], glu_t[:, h % 2], mixed_hi[:, h].bitcast(F32), ALU.subtract
                                   ).then_inc(S.olo_done, 1)
            for w in range(W_OUT + 5, W_END):
                split_lo_at(pool, w)

        @block.vector
        def _(v):
            v.memset(ones[:, :], 1.0).then_inc(S.const_done, 1)
            v.memset(eps[:, :], EPS).then_inc(S.const_done, 1)

            def x_remainder(t):
                for k in range(4):
                    v.wait_ge(S.xhi_done, 4 * t + k + 1)
                    o = (slice(None), slice(4 * k, 4 * k + 4), slice(P * t, P * t + P))
                    v.tensor_tensor(h_lo[o], ps[:, XB[t] + k].rearrange("p (k n) -> p k n", k=4),
                                    h_hi[o].bitcast(F32), ALU.subtract).then_inc(S.xlo_done, 1)

            def g_copy(c):
                v.wait_ge(S.g_bank, c + 1)
                v.tensor_copy(g_pre[:, 512 * c:512 * c + 512], ps[:, c]).then_inc(S.g_pre_done, 1)

            for c in range(3):
                g_copy(c)
            v.wait_ge(S.g_pre_done, 3)
            def normalise_x(t):
                v.wait_ge(S.x_rms, t + 1)
                v.reciprocal(small[:, 2, t:t + 1], small[:, 1, t:t + 1]).then_inc(S.x_rinv, 1)
                v.wait_ge(S.x_rinv, t + 1)
                for c0, c1 in ((0, D // 2), (D // 2, X_SPLIT if t < 2 else D)):
                    v.scalar_tensor_tensor(xt[:, t, c0:c1], xt[:, t, c0:c1], small[:, 2, t:t + 1], g_pre[:, c0:c1],
                                           ALU.mult, ALU.mult).then_inc(S.x_normed, 1)
                    if t == 0 and c0 == 0:
                        g_copy(3)

            for pair in (0, 2):
                normalise_x(pair)
                normalise_x(pair + 1)
                x_remainder(pair)
                if pair == 0:
                    x_remainder(1)
            v.wait_ge(S.prm_in, 16 * 6)
            v.tensor_copy(araw[:, 2].rearrange("g (h n) -> g h n", h=2),
                          lsraw[:, :].unsqueeze(2).to_broadcast([PAIRS, 2, STATES])).then_inc(S.ls_ready, 1)
            x_remainder(TT - 1)

            links = [0]

            def link(ins):
                links[0] += 1
                ins.then_inc(S.prm_links, 1)
                v.wait_ge(S.prm_links, links[0])

            def angle(x, n, r, m, last):
                link(v.tensor_scalar(n, x, 1.0 / TWO_PI, ROUND, ALU.mult, ALU.add))
                link(v.tensor_scalar(n, n, ROUND, None, ALU.subtract))
                link(v.scalar_tensor_tensor(r, n, -PI_A, x, ALU.mult, ALU.add))
                link(v.scalar_tensor_tensor(r, n, -PI_B, r, ALU.mult, ALU.add))
                link(v.scalar_tensor_tensor(r, n, -PI_C, r, ALU.mult, ALU.add))
                link(v.tensor_scalar(r, r, PI_SAFE, -PI_SAFE, ALU.min, ALU.max))
                link(v.scalar_tensor_tensor(m, r, -1.0, r, ALU.mult, ALU.max))
                v.tensor_scalar(m, m, -1.0, HALF_PI, ALU.mult, ALU.add).then_inc(last, 1)

            def R(i):
                return prm[:, i]

            def tt(o, x, y, op):
                link(v.tensor_tensor(o, x, y, op))

            v.wait_ge(S.prmT_done, 1)
            v.tensor_copy(prm[:, R_ARE:R_STEP + 1].rearrange("p r g -> p (r g)"), ps[:, 2, 0:3 * PAIRS]
                          ).then_inc(S.ls_ready, 1)
            link(v.tensor_copy(dsk[:, :], ps[:, 2, 3 * PAIRS:3 * PAIRS + CH // P]))
            v.wait_ge(S.step_done, 1)
            v.tensor_tensor(R(R_ZR), R(R_ARE), R(R_STEP), ALU.mult).then_inc(S.z_ready, 1)
            v.tensor_tensor(R(R_ZI), R(R_AIM), R(R_STEP), ALU.mult).then_inc(S.z_ready, 1)
            v.wait_ge(S.z_ready, 2)
            link(v.tensor_scalar(R(R_V), R(R_ZI), 0.5, None, ALU.mult))
            angle(R(R_V), R(R_N), R(R_R), R(R_M), S.angle_ready)
            v.wait_ge(S.z_acts, 2)
            link(v.tensor_scalar(R(R_X), R(R_ER), 1.0, None, ALU.add))
            tt(R(R_NR), R(R_X), R(R_TH), ALU.mult)
            v.wait_ge(S.trig_done, 2)
            link(v.scalar_tensor_tensor(R(R_S2), R(R_S), 2.0, R(R_S), ALU.mult, ALU.mult))
            tt(R(R_X), R(R_ER), R(R_S2), ALU.mult)
            tt(R(R_NR), R(R_NR), R(R_X), ALU.subtract)
            link(v.scalar_tensor_tensor(R(R_Y), R(R_S), 2.0, R(R_C), ALU.mult, ALU.mult))
            tt(R(R_NI), R(R_ER), R(R_Y), ALU.mult)
            for ri in range(3):
                link(v.memset(powers[:, 0, ri], 0.0 if ri else 1.0))
            tt(powers[:, 1, 0], R(R_ER), R(R_X), ALU.subtract)
            link(v.tensor_copy(powers[:, 1, 1], R(R_NI)))
            tt(R(R_DEN), R(R_ARE), R(R_ARE), ALU.mult)
            tt(R(R_X), R(R_AIM), R(R_AIM), ALU.mult)
            tt(R(R_DEN), R(R_DEN), R(R_X), ALU.add)
            link(v.reciprocal(R(R_DEN), R(R_DEN)))
            tt(R(R_X), R(R_NR), R(R_ARE), ALU.mult)
            tt(R(R_Y), R(R_NI), R(R_AIM), ALU.mult)
            tt(R(R_X), R(R_X), R(R_Y), ALU.add)
            tt(R(R_FR), R(R_X), R(R_DEN), ALU.mult)
            tt(R(R_X), R(R_NI), R(R_ARE), ALU.mult)
            tt(R(R_Y), R(R_NR), R(R_AIM), ALU.mult)
            tt(R(R_X), R(R_X), R(R_Y), ALU.subtract)
            tt(R(R_FI), R(R_X), R(R_DEN), ALU.mult)
            v.wait_ge(S.pos_in, 16)
            link(v.tensor_copy(ang[:, 0], pos[:, :]))
            link(v.tensor_scalar(ang[:, 0], ang[:, 0], inv_freq, None, ALU.mult))
            angle(ang[:, 0], ang[:, 1], ang[:, 2], ang[:, 3], S.rope_angle)
            scratch = prm[:, R_ZR:R_ZR + 4]
            for k in (1, 2, 4):
                src = [powers[:, 1:k + 1, ri] for ri in range(2)]
                by = [powers[:, k, ri].unsqueeze(1).to_broadcast([P, k, PAIRS]) for ri in range(2)]
                new = [powers[:, k + 1:2 * k + 1, ri] for ri in range(2)]
                s4 = scratch[:, 0:k]
                tt(new[0], src[0], by[0], ALU.mult)
                tt(s4, src[1], by[1], ALU.mult)
                tt(new[0], new[0], s4, ALU.subtract)
                tt(new[1], src[0], by[1], ALU.mult)
                tt(s4, src[1], by[0], ALU.mult)
                tt(new[1], new[1], s4, ALU.add)
            link(v.tensor_scalar(powers[:, 1:L + 1, 2], powers[:, 1:L + 1, 1], -1.0, None, ALU.mult))
            link(v.tensor_copy(chunk_a[:, 0, 0], powers[:, L, 0]))
            link(v.tensor_copy(chunk_a[:, 1, 1], powers[:, L, 0]))
            link(v.tensor_copy(chunk_a[:, 0, 1], powers[:, L, 2]))
            link(v.tensor_copy(chunk_a[:, 1, 0], powers[:, L, 1]))
            v.wait_ge(S.bc_in, 64)
            fr = R(R_FR).unsqueeze(2).to_broadcast([P, PAIRS, GC])
            fi = R(R_FI).unsqueeze(2).to_broadcast([P, PAIRS, GC])
            t0 = tmp[:, 0].rearrange("p g k c -> p (g k c)")[:, 0:PAIRS * GC].rearrange("p (g c) -> p g c", c=GC)
            tt(bbar[:, 0], braw[:, 0], fr, ALU.mult)
            tt(t0, braw[:, 1], fi, ALU.mult)
            tt(bbar[:, 0], bbar[:, 0], t0, ALU.subtract)
            tt(bbar[:, 1], braw[:, 1], fr, ALU.mult)
            tt(t0, braw[:, 0], fi, ALU.mult)
            v.tensor_tensor(bbar[:, 1], bbar[:, 1], t0, ALU.add).then_inc(S.b_done, 1)
            v.wait_ge(S.b_done, 1)
            v.wait_ge(S.ctT_done, 1)
            for ri in range(2):
                v.tensor_copy(ct[:, ri].rearrange("p g c -> p (g c)"), ps[:, 5 + ri]).then_inc(S.b_done, 1)
            v.wait_ge(S.b_done, 3)
            link(v.tensor_reduce(same_ch[:, :], ident.rearrange("p (k c) -> p c k", c=GC), AX.X, ALU.add))
            link(v.memset(zeros[:, :], 0.0))
            v.wait_ge(S.rope_trig, 2)
            v.memset(states[:, 0], 0.0).then_inc(S.vin_evac, 1)

            with v.Fori(0, 2) as i:
                for par in range(2):
                    b = 2 * i + par
                    weights_real(v, bbar, b, L, 6 * i + 3 * par, 1)
                    for k in range(4):
                        v.wait_ge(S.bxT_done, 8 * i + (4 * par + k + 1))
                        v.tensor_copy(mats[:, 4 * k:4 * k + 4].rearrange("p g n -> p (g n)"), ps[:, 4 + k]
                                      ).then_inc(S.bx_ready, 1)
                    v.wait_ge(S.vin_done, 2 * i + (par + 1))
                    for m in range(2):
                        v.tensor_copy(
                            states[:, 1:NQ + 1, :, bass.ds(b * BATCH + 4 * m, 4)].rearrange("p q r g -> p g r q"),
                            ps[:, 4 + m].rearrange("p (g r q) -> p g r q", g=4, r=2)).then_inc(S.vin_evac, 1)
            def block_diagonal(b):
                if b:
                    v.wait_ge(S.taps_done, b)
                for h in range(2):
                    v.tensor_copy(bd[64 * h:64 * h + 64, :, :, GC * h:GC * h + GC],
                                     bbar[64 * h:64 * h + 64, :, b * BATCH:(b + 1) * BATCH].rearrange(
                                         "p r g c -> p g r c")).then_inc(S.bd_done, 1)

            v.memset(bd[:, :, :, :], 0.0).then_inc(S.bd_done, 1)
            v.wait_ge(S.bd_done, 1)
            block_diagonal(0)
            v.wait_ge(S.bxT_done, 4 * NB)
            weights_real(v, ct, 0, L + 1, 3 * NB, -1)
            def taps_of(b):
                v.tensor_tensor(dm[:, :, :], same_ch[:, :].unsqueeze(1).to_broadcast([P, 2, GC]),
                                dsk[:, 2 * b:2 * b + 2].unsqueeze(2).to_broadcast([P, 2, GC]),
                                ALU.mult).then_inc(S.taps_step, 1)
                v.wait_ge(S.taps_step, b + 1)
                v.wait_ge(S.taps_done, b + 1)
                v.tensor_copy(taps[:, :, GC:P], ps[:, 4:6, GC:P]).then_inc(S.taps_ready, 1)
                v.tensor_tensor(taps[:, :, 0:GC], ps[:, 4:6, 0:GC], dm[:, :, :], ALU.add).then_inc(S.taps_ready, 1)

            swaps = [0]

            def swap_halves(x, spare):
                for to, of in ((spare, x(1, 0)), (x(1, 0), x(0, 1)), (x(0, 1), spare)):
                    v.tensor_copy(to, of).then_inc(S.swap_step, 1)
                    swaps[0] += 1
                    v.wait_ge(S.swap_step, swaps[0])

            def swap_weights():
                swap_halves(lambda half, slot: cw[64 * half:64 * half + 64, :, slot], tmp[0:64, 1])

            def swap_states(b):
                spare = tmp[0:64, 1].rearrange("p g k c -> p (g k c)")[:, 0:NQ * BATCH].rearrange("p (q g) -> p q g", q=NQ)
                swap_halves(lambda half, slot: states[64 * half:64 * half + 64, 0:NQ, slot, b * BATCH:(b + 1) * BATCH],
                            spare)

            taps_of(0)
            swap_weights()
            v.wait_ge(S.vin_evac, 2 * NB + 1)
            with v.Fori(0, (NQ - 2) // 2) as i:
                for s in range(2):
                    v.tensor_tensor(sw[:, :, :, :], chunk_a[:, :, :, :],
                                    states[:, bass.ds(2 * i + (s + 1), 1)].to_broadcast([P, 2, 2, PAIRS]), ALU.mult
                                    ).then_inc(S.scan_step, 1)
                    v.wait_ge(S.scan_step, 6 * i + (3 * s + 1))
                    v.tensor_tensor(st[:, :, :], sw[:, :, 0], sw[:, :, 1], ALU.add).then_inc(S.scan_step, 1)
                    v.wait_ge(S.scan_step, 6 * i + (3 * s + 2))
                    nxt = states[:, bass.ds(2 * i + (s + 2), 1)].rearrange("p a r g -> p (a r) g")
                    v.tensor_tensor(nxt, nxt, st[:, :, :], ALU.add).then_inc(S.scan_step, 1)
                    v.wait_ge(S.scan_step, 6 * i + (3 * s + 3))

            def output_weights(b):
                v.wait_ge(S.taps_stored, 16 * b)
                block_diagonal(b)
                weights_real(v, ct, b, L + 1, 3 * (NB + b), -1, lambda: v.wait_ge(S.y_done, b))

            def normalise(tiles, root):
                v.wait_ge(S.lat_rms, root)
                v.reciprocal(k_rot[:, :], k_rot[:, :]).then_inc(S.lat_link, 1)
                v.wait_ge(S.lat_link, root)
                for k in tiles:
                    v.scalar_tensor_tensor(lat[:, k], lat[:, k], g_lat[:, k:k + 1], k_rot[:, :], ALU.mult, ALU.mult
                                           ).then_inc(S.lat_normed, 1)

            def lat_remainder(k, n):
                v.wait_ge(S.lat_hi_done, n)
                v.tensor_tensor(mixed_lo[:, LAT[k]], lat[:, k], mixed_hi[:, LAT[k]].bitcast(F32), ALU.subtract
                                ).then_inc(S.lat_lo_done, 1)

            swap_states(0)
            output_weights(1)
            taps_of(1)
            swap_weights()
            swap_states(1)
            normalise((4, 5), 1)
            output_weights(2)
            taps_of(2)
            swap_weights()
            swap_states(2)
            output_weights(3)
            taps_of(3)
            swap_weights()
            swap_states(3)
            lat_remainder(4, 1)
            lat_remainder(5, 2)
            v.wait_ge(S.w_used, W_KR + 1)
            v.wait_ge(S.lat_sum, 4)
            for to, of, n, m in ((0, 0, 64, 0), (64, 0, 64, 0), (0, 32, 32, 1), (32, 0, 32, 1),
                                 (64, 32, 32, 1), (96, 0, 32, 1)):
                v.tensor_copy(natural(ev[to:to + n, m]), steps(ps[of:of + n, 3])).then_inc(S.kr_evac, 1)
            normalise(range(4), 2)
            for k in range(4):
                lat_remainder(k, 3 + k)
            v.wait_ge(S.kr_evac, 6)
            v.tensor_tensor(ev[:, 0], ev[:, 0], cos[:, :], ALU.mult).then_inc(S.kr_link, 1)
            v.scalar_tensor_tensor(ev[:, 1], ev[:, 1], rope_sign, sin[:, :], ALU.mult, ALU.mult
                                   ).then_inc(S.kr_link, 1)
            v.wait_ge(S.kr_link, 2)
            v.tensor_tensor(k_rot[:, :], ev[:, 0], ev[:, 1], ALU.add).then_inc(S.kr_done, 1)
            for i, k in enumerate((6, 7, 4, 5, 0, 1, 2, 3)):
                v.wait_ge(S.yhi_done, i + 1)
                v.tensor_tensor(y_lo[:, k], yraw[:, k], y_hi[:, k].bitcast(F32), ALU.subtract
                                ).then_inc(S.ylo_done, 1)

            for quad in range(2):
                v.wait_ge(S.head_done, 27 + quad)
                if quad:
                    v.wait_ge(S.rope_done, 8)
                for k, (bank, table) in enumerate(((0, cos), (2, sin), (2, cos), (0, sin))):
                    v.scalar_tensor_tensor(lat[:, k], ps[:, bank + quad], SCALE, table[:, :], ALU.mult, ALU.mult
                                           ).then_inc(S.rope_mul, 1)
                v.wait_ge(S.rope_mul, 4 * quad + 4)
                for hq in range(4):
                    h = 4 * quad + hq
                    rows = slice(32 * hq, 32 * hq + 32)
                    to = 64 * (h % 2)
                    v.tensor_tensor(qr[to:to + 32, h // 2], lat[rows, 0], lat[rows, 1], ALU.subtract
                                    ).then_inc(S.rope_done, 1)
                    v.tensor_tensor(qr[to + 32:to + 64, h // 2], lat[rows, 2], lat[rows, 3], ALU.add
                                    ).then_inc(S.rope_done, 1)

            def glu(m, par, turn):
                v.wait_ge(S.sig_done, m + 1)
                v.tensor_tensor(glu_t[:, 1], ps[:, 4 + 2 * par], glu_t[:, 0], ALU.mult).then_inc(S.glu_val, 1)
                v.wait_ge(S.glu_val, m + 1)
                v.wait_ge(gs_in[par], 16 * turn + 16)
                v.tensor_tensor(glu_t[:, 1], glu_t[:, 1], lat[:, 4 + par], ALU.mult).then_inc(S.glu_prod, 1)

            def product_taken(m):
                v.wait_ge(S.ghi_done, m + 1)
                v.wait_ge(S.glo_done, m + 1)

            with v.Fori(0, 3) as i:
                for par in range(2):
                    glu(2 * i + par, par, i)
                    product_taken(2 * i + par)
            glu(6, 0, 3)
            product_taken(6)

            def row_max(h, i):
                n = P * (i + 1)
                diag = ps[:, i, P * i:n]
                v.wait_ge(S.s_done, 4 * h + i + 1)
                v.tensor_tensor(diag, diag, mask, ALU.add).then_inc(S.s_link, 1)
                v.wait_ge(S.s_link, 4 * h + i + 1)
                if h:
                    v.wait_ge(S.exp_done, 4 * (h - 1) + i + 1)
                v.tensor_reduce(soft[:, 0, i:i + 1], ps[:, i, 0:n], AX.X, ALU.max, negate=True).then_inc(S.s_max, 1)

            def normalised(h, i):
                v.wait_ge(S.exp_done, 4 * h + i + 1)
                v.reciprocal(soft[:, 2, i:i + 1], soft[:, 1, i:i + 1]).then_inc(S.den_done, 1)
                v.wait_ge(S.den_done, 4 * h + i + 1)
                v.tensor_scalar(lat[:, i, 0:P * (i + 1)], lat[:, i, 0:P * (i + 1)], soft[:, 2, i:i + 1], None,
                                ALU.mult).then_inc(S.p_done, 1)

            def gate(h):
                v.wait_ge(S.o_done, h + 1)
                v.wait_ge(gm_in[h % 2], 16 * (h // 2) + 16)
                if h >= 2:
                    v.wait_ge(S.ohi_done, h - 1)
                    v.wait_ge(S.olo_done, h - 1)
                v.tensor_tensor(steps(glu_t[:, h % 2]), natural(ps[:, 6]), steps(lat[:, 4 + h % 2]), ALU.mult
                                ).then_inc(S.o_gated, 1)

            for h in range(HEADS + 2):
                if h < HEADS:
                    for i in range(TT):
                        row_max(h, i)
                if h == 2:
                    product_taken(7)
                if h >= 2:
                    gate(h - 2)
                if h < HEADS:
                    for i in range(TT):
                        normalised(h, i)
                if h == 0:
                    glu(7, 1, 3)

            v.wait_ge(S.g_post_in, 16)
            for c in range(4):
                for t in range(TT):
                    v.wait_ge(S.out_sq, 4 * c + t + 1)
                    v.tensor_tensor(og[:, t, 512 * c:512 * c + 512], ps[:, 4 * (c % 2) + t],
                                    g_post[:, 512 * c:512 * c + 512], ALU.mult).then_inc(S.og_done, 1)
                    if c == 3:
                        if t == 0:
                            v.wait_ge(S.xr_in, 16 * TT)
                        v.wait_ge(S.fin_root, t + 1)
                        v.reciprocal(fin[:, t, 6:7], fin[:, t, 5:6]).then_inc(S.fin_inv, 1)
                        v.wait_ge(S.fin_inv, t + 1)
                        v.wait_ge(S.og_done, 4 * c + t + 1)
                        for _, c0, c1 in (p for p in FIN_PARTS if p[0] == t):
                            cols = slice(c0, c1)
                            v.scalar_tensor_tensor(og[:, t, cols], og[:, t, cols], fin[:, t, 6:7], xr[:, t, cols],
                                                   ALU.mult, ALU.add).then_inc(S.fin_done, 1)
                if c == 2:
                    v.tensor_reduce(fin[:, :, 4], fin[:, :, 0:3], AX.X, ALU.add).then_inc(S.fin_sum, 1)
                    v.wait_ge(S.fin_sum, 1)
                    v.tensor_scalar(fin[:, :, 4], fin[:, :, 4], 1.0 / D, EPS, ALU.mult, ALU.add
                                    ).then_inc(S.fin_sum, 1)

        @block.tensor
        def _(pe):
            pe.wait_ge(S.const_done, 2)
            pe.wait_ge(S.g_row_in, 16)
            for c in range(4):
                pe.matmul(ps[:, c], ones[0:1, :], g_row[0:1, 512 * c:512 * c + 512], start=True, stop=True
                          ).then_inc(S.g_bank, 1)
            pe.wait_ge(S.consts_in, 16)
            def transpose_x(t):
                for k in range(KT):
                    if k in (0, KT // 2):
                        pe.wait_ge(S.x_normed, 2 * t + (2 if k else 1))
                    if P * k == X_SPLIT and t < 2:
                        pe.wait_ge(S.x_tail, t + 1)
                    if t == 1 and k == 0:
                        pe.wait_ge(S.g_pre_done, 4)
                    if t >= 2 and k % 4 == 0:
                        pe.wait_ge(S.xlo_done, 4 * (0 if t == 2 else 2) + k // 4 + 1)
                    m = pe.transpose(ps[:, XB[t] + k // 4, P * (k % 4):P * (k % 4) + P],
                                     xt[:, t, P * k:P * k + P], ident)
                    if k % 4 == 3:
                        m.then_inc(S.xT_done, 1)

            def half_unit(u, half):
                tok = slice(SEQ // 2 * half, SEQ // 2 * (half + 1))
                pe.wait_ge(S.lo_done, u + 1)
                for k in range(4):
                    for m in range(2):
                        cols = slice(GRP * k + P * m, GRP * k + P * m + P)
                        mm = three(pe, ps[:, m, tok], w_hi[:, u, cols], w_lo[:, u, cols], h_hi[:, 4 * u + k, tok],
                                   h_lo[:, 4 * u + k, tok], u == 0 and k == 0, u == 3 and k == 3)
                return mm

            transpose_x(0)
            transpose_x(1)
            pe.wait_ge(S.xlo_done, 8)
            half_unit(0, 0)
            transpose_x(2)
            half_unit(1, 0)
            transpose_x(3)
            pe.wait_ge(S.ls_ready, 1)
            for i in range(3):
                pe.transpose(ps[:, 2, PAIRS * i:PAIRS * (i + 1)], araw[:, i], ident[0:PAIRS, 0:PAIRS])
            pe.transpose(ps[:, 2, 3 * PAIRS:3 * PAIRS + CH // P], draw[:, :], ident[0:CH // P, 0:CH // P]
                         ).then_inc(S.prmT_done, 1)
            for u in range(2, 4):
                half_unit(u, 0)
            pe.wait_ge(S.xlo_done, 16)
            for u in range(4):
                half_unit(u, 1).then_inc(S.w_used, 1)

            def group(n, par, between=None, first=False, at=(1, 3)):
                if not first:
                    pe.wait_ge(S.proj_evac, 2 * n - 2)
                for u in range(4):
                    pe.wait_ge(S.lo_done, 4 * n + u + 1)
                    for k in range(4):
                        for m in range(2):
                            cols = slice(GRP * k + P * m, GRP * k + P * m + P)
                            mm = three(pe, ps[:, 2 * par + m], w_hi[:, u, cols], w_lo[:, u, cols],
                                       h_hi[:, 4 * u + k], h_lo[:, 4 * u + k], u == 0 and k == 0, u == 3 and k == 3)
                        if (u, k) == at and between and k < 3:
                            between()
                    mm.then_inc(S.w_used, 1)
                    if (u, 3) == at and between:
                        between()

            for n in range(4):
                if n == 1:
                    pe.wait_ge(S.ls_ready, 2)
                    pe.wait_ge(S.prm_links, 1)
                if n:
                    group(n, n % 2, first=n < 2)
                if n == 0:
                    pe.wait_ge(S.bc_in, 64)
                    pe.wait_ge(S.ls_ready, 2)
                    for ri in range(2):
                        for blk in range(BATCH):
                            for h in range(2):
                                m = pe.matmul(ps[64 * h:64 * h + 64, 5 + ri, 64 * blk:64 * blk + 64],
                                              craw[:, ri, blk],
                                              ident.rearrange("p (g h c) -> p h g c", h=2, c=GC)[:, h],
                                              start=True, stop=True)
                    m.then_inc(S.ctT_done, 1)

            def transpose_inputs(b):
                pe.wait_ge(S.cwr_step, 3 * b + 3)
                pe.wait_ge(S.cwi_step, 2 * b + 2)
                pe.wait_ge(S.vin_evac, 2 * b + 1)
                pe.wait_ge(S.b_done, 3)
                for k in range(16):
                    m = pe.transpose(ps[:, 4 + k // 4, P * (k % 4):P * (k % 4) + P],
                                     cw[:, k // 2, k % 2, 0:L].rearrange("p k c -> p (k c)"), ident)
                    if k % 4 == 3:
                        m.then_inc(S.bxT_done, 1)

            def chunk_inputs(b):
                pe.wait_ge(S.bx_ready, 4 * b + 4)
                pe.wait_ge(S.u2_in, 16 * L * b + 16 * L)
                for k in range(16):
                    for h in range(2):
                        m = pe.matmul(ps[64 * h:64 * h + 64, 4 + k // 8, NQ * (k % 8):NQ * (k % 8) + NQ],
                                      mats[:, k, 64 * h:64 * h + 64], u2[:, 2 * (k // 2) + h], start=True, stop=True)
                m.then_inc(S.vin_done, 1)

            with pe.Fori(0, 2) as i:
                for par in range(2):
                    b = 2 * i + par
                    group(2 * i + (N_GM + par), par, lambda: transpose_inputs(b))
                    chunk_inputs(b)
            def taps_mm(b):
                pe.wait_ge(S.cwr_step, 3 * (NB + b) + 3)
                pe.wait_ge(S.cwi_step, 2 * (NB + b) + 2)
                pe.wait_ge(S.bd_done, 2 * b + 3)
                if b == 0:
                    pe.wait_ge(S.vin_evac, 2 * NB + 1)
                else:
                    pe.wait_ge(S.taps_ready, 2 * b)
                if b == 2:
                    pe.wait_ge(S.lat_rms, 1)
                for s in range(2):
                    for ri in range(2):
                        for j in range(4):
                            g = 4 * s + j
                            m = pe.matmul(ps[2 * GC * j:2 * GC * (j + 1), 4 + s, 0:P], bd[:, g, ri],
                                          cw[:, g, ri, 0:L].rearrange("p k c -> p (k c)"), start=ri == 0, stop=ri == 1)
                m.then_inc(S.taps_done, 1)

            def outputs(b):
                pe.wait_ge(S.toep_in, 128 * b + 128)
                pe.wait_ge(S.u2_in, 16 * L * (NB + b + 1))
                pe.wait_ge(S.swap_step, 6 * b + 6)
                if b:
                    pe.wait_ge(S.y_ready, 2 * b)
                for h in range(2):
                    for pair in range(BATCH):
                        for mh in range(2):
                            pe.matmul(ps[64 * mh:64 * mh + 64, 6 + h, NQ * pair:NQ * pair + NQ],
                                      mats[:, 2 * pair + h, 64 * mh:64 * mh + 64], u2[:, 2 * pair + h],
                                      start=pair == 0, stop=False, skip_group_check=True)
                for h in range(2):
                    for pair in range(BATCH):
                        for mh in range(2):
                            m = pe.matmul(ps[64 * mh:64 * mh + 64, 6 + h, NQ * pair:NQ * pair + NQ],
                                          cw[:, pair, h, 1 + 4 * mh:5 + 4 * mh].rearrange("p k c -> p (k c)"),
                                          states[:, 0:NQ, h, b * BATCH + pair], start=False, stop=True,
                                          skip_group_check=True)
                m.then_inc(S.y_done, 1)

            def latent_squares(i):
                pe.wait_ge(S.lat_sum, 4 if i else 1)
                pe.wait_ge(S.taps_ready, 8 if i else 4)
                pe.matmul(ps[:, 4 + i], ones[:, :], k_rot[:, :], start=True, stop=True).then_inc(S.lat_ssq, 1)

            for n in range(N_GS, N_CKV):
                group(n, n % 2, (lambda: taps_mm(0)) if n == N_GS else None)
            group(N_CKV, 0, lambda: outputs(0), at=(2, 2))
            taps_mm(1)
            group(N_CQ, 1, lambda: (latent_squares(0), outputs(1)), at=(2, 2))
            taps_mm(2)
            group(N_CQ + 1, 0, lambda: outputs(2), at=(2, 2))
            taps_mm(3)
            pe.wait_ge(S.lo_done, W_KR + 1)
            pe.wait_ge(S.proj_evac, 28)
            for i, k in enumerate((8, 9, *range(8), *range(10, KT))):
                cols = slice(ROPE * k, ROPE * k + ROPE)
                mm = three(pe, ps[0:ROPE, 3], w_hi[:, 0, cols], w_lo[:, 0, cols], h_hi[:, k], h_lo[:, k], i == 0,
                           i == KT - 1)
                if i == 1:
                    mm.then_inc(S.kr_first, 1)
            mm.then_inc(S.w_used, 1)
            latent_squares(1)

            def head_bank(j):
                if j == 0:
                    pe.wait_ge(S.proj_evac, 30)
                elif j == 3:
                    pe.wait_ge(S.kr_evac, 6)
                elif j >= 4:
                    pe.wait_ge(S.head_evac, j - 3)
                return ps[:, j % 4]

            def head_tile(j, slot, width, m0, kts, vals=False):
                o = head_bank(j)
                for i, k in enumerate(kts):
                    if vals:
                        tok = slice(P * m0, P * m0 + P)
                        cols = slice(512 * i, 512 * i + 512)
                        pe.matmul(o, mixed_hi[:, LAT[k], tok], w_hi[:, slot, cols], start=i == 0, stop=False)
                        pe.matmul(o, mixed_hi[:, LAT[k], tok], w_lo[:, slot, cols], start=False, stop=False)
                        mm = pe.matmul(o, mixed_lo[:, LAT[k], tok], w_hi[:, slot, cols], start=False, stop=i == len(kts) - 1)
                    else:
                        cols = slice(width * i + P * m0, width * i + P * m0 + P)
                        mm = three(pe, o, w_hi[:, slot, cols], w_lo[:, slot, cols], mixed_hi[:, LAT[k]],
                                   mixed_lo[:, LAT[k]], i == 0,
                                   i == len(kts) - 1)
                return mm

            j = 0
            for w in range(W_KN, W_GLU):
                pe.wait_ge(S.lo_done, w + 1)
                slot = w % 4
                if w == W_KN:
                    pe.wait_ge(S.lat_hi_done, 2)
                    pe.wait_ge(S.lat_lo_done, 2)
                if w == W_Q:
                    pe.wait_ge(S.lat_hi_done, 6)
                    pe.wait_ge(S.lat_lo_done, 6)
                for m in range(4 if w < W_Q else 2):
                    if w < W_V:
                        mm = head_tile(j, slot, 512, m, (4, 5))
                    elif w < W_Q:
                        mm = head_tile(j, slot, 512, m, (4, 5), True)
                    else:
                        mm = head_tile(j, slot, 256, m, (0, 1, 2, 3))
                    mm.then_inc(S.head_done, 1)
                    j += 1
                if w == W_KN + 1:
                    outputs(3)

            def glu(m):
                if m < 2:
                    pe.wait_ge(S.lat_rms, 2)
                    pe.wait_ge(S.y_ready, 8)
                else:
                    pe.wait_ge(S.sig_done, m - 1)
                    pe.wait_ge(S.glu_val, m - 1)
                for i, k in enumerate((6, 7, 4, 5, 0, 1, 2, 3)):
                    u = i // 4
                    slot = (W_GLU + 2 * m + u) % RING
                    if i % 4 == 0:
                        pe.wait_ge(S.lo_done, W_GLU + 2 * m + u + 1)
                    if m == 0:
                        pe.wait_ge(S.yhi_done, i + 1)
                        pe.wait_ge(S.ylo_done, i + 1)
                    for e in range(2):
                        cols = slice(2 * P * (k % 4) + P * e, 2 * P * (k % 4) + P * e + P)
                        mm = three(pe, ps[:, 4 + 2 * (m % 2) + e], w_hi[:, slot, cols], w_lo[:, slot, cols], y_hi[:, k],
                                   y_lo[:, k], i == 0, i == 7)
                    if i % 4 == 3:
                        mm.then_inc(S.w_used, 1)

            def scores(h):
                half = slice(64 * (h % 2), 64 * (h % 2) + 64)
                for i in range(TT):
                    n = P * (i + 1)
                    q = slice(P * i, n)
                    if h:
                        pe.wait_ge(S.exp_done, 4 * (h - 1) + i + 1)
                    pe.matmul(ps[:, i, 0:n], qn[:, h, q], kn[:, h, 0:n], start=True, stop=False)
                    pe.matmul(ps[:, i, 0:n], qr[half, h // 2, q], k_rot[half, 0:n], start=False, stop=True
                              ).then_inc(S.s_done, 1)

            def transposes(h):
                for i in range(TT):
                    bank, col = PT[i]
                    pe.wait_ge(S.p_done, 4 * h + i + 1)
                    if h:
                        pe.wait_ge(S.pT_evac, 4 * (h - 1) + max(i + 1, 2))
                    else:
                        pe.wait_ge(S.sig_done, 8)
                        pe.wait_ge(S.glu_val, 8)
                    for k in range(i + 1):
                        m = pe.transpose(ps[:, bank, col + P * k:col + P * k + P], lat[:, i, P * k:P * k + P], ident)
                    m.then_inc(S.pT_done, 1)

            def values(h):
                pe.wait_ge(S.pT_evac, 4 * h + 4)
                if h:
                    pe.wait_ge(S.o_gated, h)
                for k in range(TT):
                    m = pe.matmul(ps[:, 6, P * k:SEQ], vv[:, k, P * h:P * h + P], pt[:, h % 2, k, P * k:SEQ],
                                  start=k == 0, stop=k == TT - 1)
                m.then_inc(S.o_done, 1)

            for m in range(7):
                glu(m)
            pe.wait_ge(S.kr_done, 1)
            pe.wait_ge(S.rope_done, 16)
            scores(0)
            glu(7)
            for h in range(1, HEADS):
                scores(h)
                if h >= 2:
                    values(h - 2)
                transposes(h - 1)

            def products(c, u, t, first, last):
                w = W_OUT + 8 * c + u
                for i in range(2):
                    k = 2 * ((u + 4) % 8 if c == 0 else u) + i
                    cols = slice(512 * i, 512 * i + 512)
                    o = ps[:, 4 * (c % 2) + t]
                    tok = slice(P * t, P * t + P)
                    pe.matmul(o, mixed_hi[:, k, tok], w_hi[:, w % 4, cols], start=first and i == 0, stop=False)
                    pe.matmul(o, mixed_hi[:, k, tok], w_lo[:, w % 4, cols], start=False, stop=False)
                    mm = pe.matmul(o, mixed_lo[:, k, tok], w_hi[:, w % 4, cols], start=False, stop=last and i == 1)
                return mm

            for c in range(4):
                if c == 1:
                    pe.wait_ge(S.pT_evac, 4 * HEADS)
                    pe.wait_ge(S.o_gated, HEADS)
                elif c >= 2:
                    pe.wait_ge(S.og_done, 4 * (c - 1))
                for u in range(8 if c < 3 else 4):
                    pe.wait_ge(S.lo_done, W_OUT + 8 * c + u + 1)
                    if c == 0:
                        hi, lo, n = (S.ghi_done, S.glo_done, 2 * u + 2) if u < 4 else (S.ohi_done, S.olo_done, 2 * u - 6)
                        pe.wait_ge(hi, n)
                        pe.wait_ge(lo, n)
                    for t in range(TT):
                        if c == 0 and u == 0:
                            pe.wait_ge(S.exp_done, 4 * (HEADS - 1) + t + 1)
                        mm = products(c, u, t, u == 0, u == 7)
                    mm.then_inc(S.w_used, 1)
                    if c == 0 and u == 0:
                        transposes(HEADS - 1)
                        values(HEADS - 2)
                    if c == 0 and u == 1:
                        values(HEADS - 1)
            for t in range(TT):
                for u in range(4, 8):
                    if t == 0:
                        pe.wait_ge(S.lo_done, W_OUT + 8 * 3 + u + 1)
                    mm = products(3, u, t, False, u == 7)
                mm.then_inc(S.tile_done, 1)


_INS = ['x', 'positions', 'norm_pre', 'norm_post', 'w_in', 'q_norm', 'w_uq', 'kv_norm', 'w_ukv', 'ssm_a_re',
        'ssm_a_im', 'ssm_b_re', 'ssm_b_im', 'ssm_c_re', 'ssm_c_im', 'ssm_d', 'ssm_log_step', 'w_glu', 'w_out']
_MATRICES = ('x', 'w_in', 'w_uq', 'w_ukv', 'ssm_a_re', 'ssm_a_im', 'ssm_b_re', 'ssm_b_im', 'ssm_c_re', 'ssm_c_im',
             'w_glu', 'w_out')


def _constants():
    import numpy as np

    c = np.zeros((P, C_COLS), np.float32)
    c[:, C_ID:C_ID + P] = np.eye(P)
    c[:, C_MASK:C_MASK + P] = np.where(np.tri(P, dtype=bool), 0.0, -3e38)
    r = np.arange(P)
    c[:, C_FREQ] = (np.float32(10000.0) ** (-np.arange(0, ROPE, 2, dtype=np.float32) / np.float32(ROPE)))[r % 32]
    c[:, C_SIGN] = np.where(r // 32 % 2, 1.0, -1.0)
    return c


def kernel(**inputs):
    import numpy as _np
    import concourse.bacc as _bacc
    from concourse import mybir as _mybir
    from concourse.bass_utils import run_bass_kernel_spmd as _run

    nc = _bacc.Bacc("TRN2", target_bir_lowering=False, num_devices=1)
    arrays, aps = {}, {}
    for name in _INS:
        v = _np.ascontiguousarray(inputs[name])
        if name in _MATRICES:
            v = v.reshape(v.shape[1:])
        arrays[f"in_{name}_dram"] = v
    arrays["in_consts_dram"] = _constants()
    for key, v in arrays.items():
        aps[key[3:-5]] = nc.dram_tensor(key, v.shape, _mybir.dt.from_np(v.dtype), kind="ExternalInput").ap()
    out = nc.dram_tensor("out_0_dram", (SEQ, D), F32, kind="ExternalOutput").ap()
    hybrid_layer(nc, aps, out)
    r = _run(nc, [arrays], core_ids=[0])
    return r.results[0]["out_0_dram"].reshape(1, SEQ, D)
```
